# Optimizing a Trainium2 kernel written in Bass

```python
import jax, jax.numpy as jnp
from jax import lax
import numpy as np
import math

D_MODEL = 1024
BATCH = 1
SEQ = 512
DEPTH = 1

N_ATTN_HEADS = 8
HEAD_DIM = 64
ATTN_WIDTH = N_ATTN_HEADS * HEAD_DIM
POOL_WIDTH = D_MODEL - ATTN_WIDTH
POOL_WINDOWS = (2, 4, 8, 16)
N_POOL_GROUPS = len(POOL_WINDOWS)
POOL_GROUP = POOL_WIDTH // N_POOL_GROUPS
IN_WIDTH = 3 * ATTN_WIDTH + POOL_WIDTH
MOBA_BLOCK = 256
MOBA_TOPK = 3
QUERY_CHUNK = 32
D_FF = 4 * D_MODEL
EPS = 1e-6


def _alibi_slopes(n_heads):
    return jnp.asarray(2.0 ** (-8.0 * np.arange(1, n_heads + 1) / n_heads), dtype=jnp.float32)

def rms_norm(x, g):
    xf = x.astype(jnp.float32)
    y = xf * lax.rsqrt(jnp.mean(xf * xf, axis=-1, keepdims=True) + EPS)
    return (y * g.astype(jnp.float32)).astype(x.dtype)

def moba_attention(q, k, v):
    B, H, S, Dh = q.shape
    nb = -(-S // MOBA_BLOCK)
    pad = nb * MOBA_BLOCK - S
    kp = jnp.pad(k, ((0, 0), (0, 0), (0, pad), (0, 0)))
    vp = jnp.pad(v, ((0, 0), (0, 0), (0, pad), (0, 0)))
    kb = kp.reshape(B, H, nb, MOBA_BLOCK, Dh)
    vb = vp.reshape(B, H, nb, MOBA_BLOCK, Dh)
    slopes = _alibi_slopes(H)
    scale = HEAD_DIM ** -0.5

    counts = jnp.asarray(np.clip(S - np.arange(nb) * MOBA_BLOCK, 1, MOBA_BLOCK), dtype=jnp.float32)
    kmean = kb.astype(jnp.float32).sum(axis=3) / counts[:, None]
    pos = jnp.arange(S)
    qblk = pos // MOBA_BLOCK
    gate = jnp.einsum('bhtd,bhnd->bhtn', q.astype(jnp.float32), kmean)
    past = jnp.arange(nb)[None, :] < qblk[:, None]
    gate = jnp.where(past[None, None], gate, -jnp.inf)
    n_sel = max(1, min(MOBA_TOPK, nb - 1))
    _, sel = lax.top_k(gate, n_sel)
    sel_valid = jnp.arange(n_sel)[None, :] < qblk[:, None]

    nc = S // QUERY_CHUNK
    qc = q.reshape(B, H, nc, QUERY_CHUNK, Dh).transpose(2, 0, 1, 3, 4)
    selc = sel.reshape(B, H, nc, QUERY_CHUNK, n_sel).transpose(2, 0, 1, 3, 4)
    validc = sel_valid.reshape(nc, QUERY_CHUNK, n_sel)
    bi = jnp.arange(B)[:, None, None, None]
    hi = jnp.arange(H)[None, :, None, None]
    blk_off = jnp.arange(MOBA_BLOCK)

    def chunk(args):
        c, q_c, sel_c, valid_c = args
        t = c * QUERY_CHUNK + jnp.arange(QUERY_CHUNK)
        own = t[0] // MOBA_BLOCK
        k_own = lax.dynamic_index_in_dim(kb, own, axis=2, keepdims=False)
        v_own = lax.dynamic_index_in_dim(vb, own, axis=2, keepdims=False)
        s_own = own * MOBA_BLOCK + blk_off
        sc_own = jnp.einsum('bhtd,bhsd->bhts', q_c, k_own).astype(jnp.float32) * scale
        dist_own = (t[:, None] - s_own[None, :]).astype(jnp.float32)
        sc_own = sc_own - slopes[:, None, None] * dist_own[None]
        sc_own = jnp.where((s_own[None, :] <= t[:, None])[None, None], sc_own, -jnp.inf)

        k_sel = kb[bi, hi, sel_c]
        v_sel = vb[bi, hi, sel_c]
        s_sel = sel_c[..., None] * MOBA_BLOCK + blk_off
        sc_sel = jnp.einsum('bhtd,bhtrsd->bhtrs', q_c, k_sel).astype(jnp.float32) * scale
        dist_sel = (t[None, None, :, None, None] - s_sel).astype(jnp.float32)
        sc_sel = sc_sel - slopes[None, :, None, None, None] * dist_sel
        sc_sel = jnp.where(valid_c[None, None, :, :, None], sc_sel, -jnp.inf)

        scores = jnp.concatenate(
            [sc_own, sc_sel.reshape(B, H, QUERY_CHUNK, n_sel * MOBA_BLOCK)], axis=-1)
        p = jax.nn.softmax(scores, axis=-1)
        p_own = p[..., :MOBA_BLOCK].astype(v.dtype)
        p_sel = p[..., MOBA_BLOCK:].reshape(B, H, QUERY_CHUNK, n_sel, MOBA_BLOCK).astype(v.dtype)
        out = (jnp.einsum('bhts,bhsd->bhtd', p_own, v_own)
               + jnp.einsum('bhtrs,bhtrsd->bhtd', p_sel, v_sel))
        return out.astype(q.dtype)

    out = lax.map(chunk, (jnp.arange(nc), qc, selc, validc))
    return out.transpose(1, 2, 0, 3, 4).reshape(B, H, S, Dh)

def multiscale_pool(u, w_pool, pool_scale):
    B, S, _ = u.shape
    ug = u.astype(jnp.float32).reshape(B, S, N_POOL_GROUPS, POOL_GROUP)
    cs = jnp.cumsum(ug, axis=1)
    pos = jnp.arange(S)
    outs = []
    for g, w in enumerate(POOL_WINDOWS):
        c = cs[:, :, g]
        prev = jnp.pad(c, ((0, 0), (w, 0), (0, 0)))[:, :S]
        cnt = jnp.minimum(pos + 1, w).astype(jnp.float32)[None, :, None]
        outs.append((c - prev) / cnt - ug[:, :, g])
    mixed = jnp.stack(outs, axis=2)
    y = jnp.einsum('bsgc,gcd->bsgd', mixed, w_pool.astype(jnp.float32))
    y = y.reshape(B, S, POOL_WIDTH) * pool_scale.astype(jnp.float32)
    return y.astype(u.dtype)

def first_inputs(seed: int = 0) -> dict:
    key = jax.random.key(seed)
    ks = jax.random.split(key, 12)
    f32 = jnp.float32
    x = jax.random.normal(ks[0], (BATCH, SEQ, D_MODEL), f32)
    norm_mix = 1.0 + 0.02 * jax.random.normal(ks[1], (DEPTH, D_MODEL), f32)
    w_in = jax.random.normal(ks[2], (DEPTH, D_MODEL, IN_WIDTH), f32) * D_MODEL ** -0.5
    w_pool = jax.random.normal(ks[3], (DEPTH, N_POOL_GROUPS, POOL_GROUP, POOL_GROUP), f32) * POOL_GROUP ** -0.5
    pool_scale = 1.0 + 0.02 * jax.random.normal(ks[4], (DEPTH, POOL_WIDTH), f32)
    w_out = jax.random.normal(ks[5], (DEPTH, D_MODEL, D_MODEL), f32) * D_MODEL ** -0.5
    norm_mlp = 1.0 + 0.02 * jax.random.normal(ks[6], (DEPTH, D_MODEL), f32)
    w_up = jax.random.normal(ks[7], (DEPTH, D_MODEL, D_FF), f32) * D_MODEL ** -0.5
    w_down = jax.random.normal(ks[8], (DEPTH, D_FF, D_MODEL), f32) * D_FF ** -0.5
    norm_final = 1.0 + 0.02 * jax.random.normal(ks[9], (D_MODEL,), f32)
    return {"x": x, "norm_mix": norm_mix, "w_in": w_in, "w_pool": w_pool,
            "pool_scale": pool_scale, "w_out": w_out, "norm_mlp": norm_mlp,
            "w_up": w_up, "w_down": w_down, "norm_final": norm_final}

def first_block(x, norm_mix, w_in, w_pool, pool_scale, w_out, norm_mlp, w_up, w_down, norm_final):
    B, S, _ = x.shape
    for l in range(DEPTH):
        h = rms_norm(x, norm_mix[l])
        proj = h @ w_in[l]
        q, k, v, u = jnp.split(proj, [ATTN_WIDTH, 2 * ATTN_WIDTH, 3 * ATTN_WIDTH], axis=-1)
        to_heads = lambda t: t.reshape(B, S, N_ATTN_HEADS, HEAD_DIM).transpose(0, 2, 1, 3)
        a = moba_attention(to_heads(q), to_heads(k), to_heads(v))
        a = a.transpose(0, 2, 1, 3).reshape(B, S, ATTN_WIDTH)
        p = multiscale_pool(u, w_pool[l], pool_scale[l])
        x = x + jnp.concatenate([a, p], axis=-1) @ w_out[l]
        h = rms_norm(x, norm_mlp[l])
        x = x + jnp.square(jax.nn.relu(h @ w_up[l])) @ w_down[l]
    return rms_norm(x, norm_final)


N_MEM = 256
R_HEAD = 64
R_HEADS = D_MODEL // R_HEAD
R_WIDTH = R_HEADS * R_HEAD
R_LORA_W = 64
R_LORA_A = 64
R_LORA_G = 160
LNX_EPS = 64e-5
N_HEADS = 16
N_KV = 4
N_HG = N_HEADS // N_KV
CMP_BLOCK = 32
CMP_STRIDE = 16
CMP_HIDDEN = 256
SEL_BLOCK = 64
SEL_TOPK = 16
WINDOW = 512
Q_BLOCK = 32
FORCE_SCORE = 1e4
REL_BUCKETS = 32
REL_MAX_DIST = 128
CA_HEADS = 4
CA_HEAD_DIM = D_MODEL // CA_HEADS
D_FF_2 = 2816
CONV_W = 3
NORM_EPS = 1e-6
QK_EPS = 1e-6
RWKV_COLS = 3 * R_WIDTH + R_LORA_W + R_LORA_A + R_LORA_G
NSA_KV = N_KV * HEAD_DIM
NSA_COLS = N_HEADS * HEAD_DIM + 6 * NSA_KV + 3 * N_HEADS
GATE_COLS = 2 * D_MODEL
IN_COLS = RWKV_COLS + NSA_COLS + GATE_COLS


def rms_norm_2(x, g, eps=NORM_EPS):
    xf = x.astype(jnp.float32)
    y = xf * lax.rsqrt(jnp.mean(xf * xf, axis=-1, keepdims=True) + eps)
    return (y * g.astype(jnp.float32)).astype(x.dtype)

def masked_softmax(logits, mask):
    logits = jnp.where(mask, logits.astype(jnp.float32), -jnp.inf)
    m = jnp.max(logits, axis=-1, keepdims=True)
    m = jnp.where(jnp.isfinite(m), m, 0.0)
    e = jnp.exp(logits - m)
    s = jnp.sum(e, axis=-1, keepdims=True)
    return e / jnp.where(s > 0, s, 1.0)

def t5_bucket(dist):
    n = jnp.maximum(dist, 0)
    exact = REL_BUCKETS // 2
    nf = jnp.maximum(n, 1).astype(jnp.float32)
    large = exact + (jnp.log(nf / exact) / math.log(REL_MAX_DIST / exact) * (REL_BUCKETS - exact)).astype(jnp.int32)
    large = jnp.minimum(large, REL_BUCKETS - 1)
    return jnp.where(n < exact, n, large)

def group_bias(table, bucket):
    tg = table.astype(jnp.float32).reshape(REL_BUCKETS, N_KV, N_HG)
    gi = jnp.arange(N_KV).reshape(1, N_KV, 1, 1)
    return jnp.moveaxis(tg[bucket, gi], -1, -2)

def token_shift(z, mu):
    prev = jnp.pad(z[:, :-1], ((0, 0), (1, 0), (0, 0)))
    return z + (prev - z) * mu

def rwkv7_scan(r, w, k, v, a, b):
    B, S, H, N = r.shape
    xs = tuple(jnp.swapaxes(t.astype(jnp.float32), 0, 1) for t in (r, w, k, v, a, b))

    def step(state, inp):
        r_t, w_t, k_t, v_t, a_t, b_t = inp
        sa = jnp.einsum('bhvk,bhk->bhv', state, a_t)
        state = state * w_t[:, :, None, :] + sa[..., None] * b_t[:, :, None, :] + v_t[..., None] * k_t[:, :, None, :]
        return state, jnp.einsum('bhvk,bhk->bhv', state, r_t)

    s0 = jnp.zeros((B, H, N, N), jnp.float32)
    _, ys = lax.scan(step, s0, xs)
    return jnp.swapaxes(ys, 0, 1)

def rwkv7_mixer(z, mu, w0, w2, a0, a2, g2, k_k, k_a, r_k, lnx_w, lnx_b):
    B, S, _ = z.shape
    z = token_shift(z, mu)
    r, k, v, zw, za, zg = jnp.split(z, np.cumsum([R_WIDTH, R_WIDTH, R_WIDTH, R_LORA_W, R_LORA_A]).tolist(), axis=-1)
    w = -jax.nn.softplus(-(w0 + jnp.tanh(zw) @ w2)) - 0.5
    a = jax.nn.sigmoid(a0 + za @ a2)
    g = jax.nn.sigmoid(zg) @ g2
    hd = lambda t: t.reshape(B, S, R_HEADS, R_HEAD)
    kk = hd(k * k_k).astype(jnp.float32)
    kk = kk / jnp.maximum(jnp.sqrt(jnp.sum(kk * kk, axis=-1, keepdims=True)), 1e-12)
    k = k * (1 + (a - 1) * k_a)
    decay = jnp.exp(-jnp.exp(w.astype(jnp.float32)))
    a_h = hd(a).astype(jnp.float32)
    y = rwkv7_scan(hd(r), hd(decay), hd(k), hd(v), -kk, kk * a_h)
    mean = jnp.mean(y, axis=-1, keepdims=True)
    var = jnp.mean(jnp.square(y - mean), axis=-1, keepdims=True)
    y = ((y - mean) * lax.rsqrt(var + LNX_EPS)).reshape(B, S, R_WIDTH)
    y = y * lnx_w.astype(jnp.float32) + lnx_b.astype(jnp.float32)
    bonus = jnp.sum(hd(r) * hd(k) * r_k, axis=-1, keepdims=True) * hd(v)
    out = (y + bonus.reshape(B, S, R_WIDTH).astype(jnp.float32)) * g.astype(jnp.float32)
    return out.astype(z.dtype)

def nsa_mixer(q, kc, vc, ks, vs, kw, vw, gates, rel_table, q_gain, k_gain, pe_k, pe_v, c1k, c2k, c1v, c2v):
    B, S, _ = q.shape
    q = rms_norm_2(q.reshape(B, S, N_KV, N_HG, HEAD_DIM), q_gain, QK_EPS)
    kvh = lambda t: t.reshape(B, S, N_KV, HEAD_DIM)
    scale = HEAD_DIM ** -0.5
    n_cmp = (S - CMP_BLOCK) // CMP_STRIDE + 1
    cidx = jnp.arange(n_cmp)[:, None] * CMP_STRIDE + jnp.arange(CMP_BLOCK)[None, :]

    def compress(t, pe, w1, w2):
        blk = kvh(t)[:, cidx] + pe[:, None, :]
        hid = jax.nn.gelu(jnp.einsum('bnlgd,ldc->bngc', blk, w1.reshape(CMP_BLOCK, HEAD_DIM, CMP_HIDDEN)))
        return jnp.einsum('bngc,cd->bngd', hid, w2)

    k_cmp = rms_norm_2(compress(kc, pe_k, c1k, c2k), k_gain[0], QK_EPS)
    v_cmp = compress(vc, pe_v, c1v, c2v)
    cmp_end = jnp.arange(n_cmp) * CMP_STRIDE + CMP_BLOCK - 1
    n_blk = S // SEL_BLOCK
    n_top = min(SEL_TOPK, n_blk)
    ci = jnp.arange(n_cmp)[:, None] * CMP_STRIDE
    sj = jnp.arange(n_blk)[None, :] * SEL_BLOCK
    cmp_to_sel = ((ci <= sj + SEL_BLOCK - 1) & (ci + CMP_BLOCK - 1 >= sj)).astype(jnp.float32)
    kb = rms_norm_2(kvh(ks), k_gain[1], QK_EPS).reshape(B, n_blk, SEL_BLOCK, N_KV, HEAD_DIM).transpose(0, 3, 1, 2, 4)
    vb = kvh(vs).reshape(B, n_blk, SEL_BLOCK, N_KV, HEAD_DIM).transpose(0, 3, 1, 2, 4)
    pad = ((0, 0), (WINDOW, 0), (0, 0), (0, 0))
    k_win = jnp.pad(rms_norm_2(kvh(kw), k_gain[2], QK_EPS), pad)
    v_win = jnp.pad(kvh(vw), pad)
    g_all = jax.nn.sigmoid(gates.astype(jnp.float32)).reshape(B, S, N_KV, N_HG, 3)
    nq = S // Q_BLOCK
    q_blocks = jnp.swapaxes(q.reshape(B, nq, Q_BLOCK, N_KV, N_HG, HEAD_DIM), 0, 1)
    g_blocks = jnp.swapaxes(g_all.reshape(B, nq, Q_BLOCK, N_KV, N_HG, 3), 0, 1)
    starts = jnp.arange(nq, dtype=jnp.int32) * Q_BLOCK
    bi = jnp.arange(B)[:, None, None, None]
    gi = jnp.arange(N_KV)[None, :, None, None]
    blk_ids = jnp.arange(n_blk)

    def block(args):
        qb, gb, q0 = args
        t = q0 + jnp.arange(Q_BLOCK)
        s_c = jnp.einsum('bqghd,bngd->bgqhn', qb, k_cmp).astype(jnp.float32) * scale
        s_c = s_c + group_bias(rel_table, t5_bucket(t[:, None] - cmp_end[None, :])[None, None])
        p_c = masked_softmax(s_c, (cmp_end[None, :] <= t[:, None])[None, None, :, None, :])
        o_c = jnp.einsum('bgqhn,bngd->bqghd', p_c.astype(v_cmp.dtype), v_cmp)
        imp = jnp.einsum('bgqhn,nj->bgqj', p_c, cmp_to_sel)
        cur = t // SEL_BLOCK
        forced = (blk_ids[None, :] == 0) | (blk_ids[None, :] == cur[:, None]) | (blk_ids[None, :] == cur[:, None] - 1)
        valid = blk_ids[None, :] * SEL_BLOCK <= t[:, None]
        imp = jnp.where(valid, jnp.where(forced, FORCE_SCORE, imp), -jnp.inf)
        _, idx = lax.top_k(imp, n_top)
        k_g = kb[bi, gi, idx].reshape(B, N_KV, Q_BLOCK, n_top * SEL_BLOCK, HEAD_DIM)
        v_g = vb[bi, gi, idx].reshape(B, N_KV, Q_BLOCK, n_top * SEL_BLOCK, HEAD_DIM)
        kpos = (idx[..., None] * SEL_BLOCK + jnp.arange(SEL_BLOCK)).reshape(B, N_KV, Q_BLOCK, n_top * SEL_BLOCK)
        dist_s = t[None, None, :, None] - kpos
        s_s = jnp.einsum('bqghd,bgqkd->bgqhk', qb, k_g).astype(jnp.float32) * scale + group_bias(rel_table, t5_bucket(dist_s))
        p_s = masked_softmax(s_s, (dist_s >= 0)[:, :, :, None, :])
        o_s = jnp.einsum('bgqhk,bgqkd->bqghd', p_s.astype(v_g.dtype), v_g)
        kw_b = lax.dynamic_slice_in_dim(k_win, q0, WINDOW + Q_BLOCK, axis=1)
        vw_b = lax.dynamic_slice_in_dim(v_win, q0, WINDOW + Q_BLOCK, axis=1)
        wpos = q0 - WINDOW + jnp.arange(WINDOW + Q_BLOCK)
        dist_w = t[:, None] - wpos[None, :]
        m_w = (wpos[None, :] >= 0) & (dist_w >= 0) & (dist_w < WINDOW)
        s_w = jnp.einsum('bqghd,bkgd->bgqhk', qb, kw_b).astype(jnp.float32) * scale
        s_w = s_w + group_bias(rel_table, t5_bucket(dist_w)[None, None])
        p_w = masked_softmax(s_w, m_w[None, None, :, None, :])
        o_w = jnp.einsum('bgqhk,bkgd->bqghd', p_w.astype(vw_b.dtype), vw_b)
        out = gb[..., 0:1] * o_c + gb[..., 1:2] * o_s + gb[..., 2:3] * o_w
        return out.astype(qb.dtype)

    o = lax.map(block, (q_blocks, g_blocks, starts))
    return jnp.swapaxes(o, 0, 1).reshape(B, S, N_HEADS * HEAD_DIM)

def cross_attn(xn, mn, wq, wkv, q_gain, k_gain, wo):
    B, S, _ = xn.shape
    M = mn.shape[1]
    q = rms_norm_2((xn @ wq).reshape(B, S, CA_HEADS, CA_HEAD_DIM), q_gain, QK_EPS)
    kv = (mn @ wkv).reshape(B, M, 2, CA_HEADS, CA_HEAD_DIM)
    k = rms_norm_2(kv[:, :, 0], k_gain, QK_EPS)
    v = kv[:, :, 1]
    s = jnp.einsum('bshd,bmhd->bhsm', q, k).astype(jnp.float32) * (CA_HEAD_DIM ** -0.5)
    p = jax.nn.softmax(s, axis=-1).astype(v.dtype)
    o = jnp.einsum('bhsm,bmhd->bshd', p, v).reshape(B, S, CA_HEADS * CA_HEAD_DIM)
    return o @ wo

def conv_ffn(xn, w_up, conv_w, conv_b, w_down):
    a, b = jnp.split(xn @ w_up, 2, axis=-1)
    a = lax.conv_general_dilated(a, conv_w[:, None, :].astype(a.dtype), (1,), [(CONV_W - 1, 0)],
                                 dimension_numbers=('NWC', 'WIO', 'NWC'), feature_group_count=D_FF_2) + conv_b
    return (jax.nn.silu(a) * b) @ w_down

def second_inputs(seed: int = 0) -> dict:
    key = jax.random.key(seed)
    ks = iter(jax.random.split(key, 64))
    L, D = DEPTH, D_MODEL
    nrm = lambda shape, scale: jax.random.normal(next(ks), shape, jnp.float32) * scale
    lin = lambda fi, fo: nrm((L, fi, fo), fi ** -0.5)
    gain = lambda *s: 1.0 + nrm((L,) + s, 0.02)
    return {
        "x": nrm((BATCH, SEQ, D), 1.0),
        "mem": nrm((BATCH, N_MEM, D), 1.0),
        "rel_bias": nrm((REL_BUCKETS, N_HEADS), 0.1),
        "norm_mix": gain(D),
        "w_in": lin(D, IN_COLS),
        "rwkv_mu": jax.random.uniform(next(ks), (L, RWKV_COLS), jnp.float32),
        "rwkv_w0": jax.random.uniform(next(ks), (L, R_WIDTH), jnp.float32, -6.0, 0.5),
        "rwkv_w2": nrm((L, R_LORA_W, R_WIDTH), 0.5 * R_LORA_W ** -0.5),
        "rwkv_a0": nrm((L, R_WIDTH), 0.1),
        "rwkv_a2": nrm((L, R_LORA_A, R_WIDTH), 0.5 * R_LORA_A ** -0.5),
        "rwkv_g2": lin(R_LORA_G, R_WIDTH),
        "rwkv_kk": 0.85 + nrm((L, R_WIDTH), 0.02),
        "rwkv_ka": 1.0 + nrm((L, R_WIDTH), 0.02),
        "rwkv_rk": nrm((L, R_HEADS, R_HEAD), 0.1),
        "rwkv_lnx_w": gain(R_WIDTH),
        "rwkv_lnx_b": nrm((L, R_WIDTH), 0.02),
        "nsa_q_gain": gain(HEAD_DIM),
        "nsa_k_gain": gain(3, HEAD_DIM),
        "cmp_pe_k": nrm((L, CMP_BLOCK, HEAD_DIM), 0.1),
        "cmp_pe_v": nrm((L, CMP_BLOCK, HEAD_DIM), 0.1),
        "cmp_w1_k": lin(CMP_BLOCK * HEAD_DIM, CMP_HIDDEN),
        "cmp_w2_k": lin(CMP_HIDDEN, HEAD_DIM),
        "cmp_w1_v": lin(CMP_BLOCK * HEAD_DIM, CMP_HIDDEN),
        "cmp_w2_v": lin(CMP_HIDDEN, HEAD_DIM),
        "w_branch_rwkv": lin(R_WIDTH, D),
        "w_branch_nsa": lin(N_HEADS * HEAD_DIM, D),
        "w_mix_out": lin(D, D),
        "norm_cross": gain(D),
        "norm_mem": gain(D),
        "ca_wq": lin(D, CA_HEADS * CA_HEAD_DIM),
        "ca_wkv": lin(D, 2 * CA_HEADS * CA_HEAD_DIM),
        "ca_q_gain": gain(CA_HEAD_DIM),
        "ca_k_gain": gain(CA_HEAD_DIM),
        "ca_wo": lin(CA_HEADS * CA_HEAD_DIM, D),
        "norm_ffn": gain(D),
        "ffn_up": lin(D, 2 * D_FF_2),
        "ffn_conv": nrm((L, CONV_W, D_FF_2), CONV_W ** -0.5),
        "ffn_conv_b": nrm((L, D_FF_2), 0.02),
        "ffn_down": lin(D_FF_2, D),
    }

def second_block(x, mem, rel_bias, norm_mix, w_in, rwkv_mu, rwkv_w0, rwkv_w2, rwkv_a0, rwkv_a2, rwkv_g2,
              rwkv_kk, rwkv_ka, rwkv_rk, rwkv_lnx_w, rwkv_lnx_b, nsa_q_gain, nsa_k_gain, cmp_pe_k, cmp_pe_v,
              cmp_w1_k, cmp_w2_k, cmp_w1_v, cmp_w2_v, w_branch_rwkv, w_branch_nsa, w_mix_out,
              norm_cross, norm_mem, ca_wq, ca_wkv, ca_q_gain, ca_k_gain, ca_wo,
              norm_ffn, ffn_up, ffn_conv, ffn_conv_b, ffn_down):
    B, S, D = x.shape
    split_pts = np.cumsum([RWKV_COLS, N_HEADS * HEAD_DIM] + [NSA_KV] * 6 + [3 * N_HEADS]).tolist()
    h = x
    for l in range(DEPTH):
        xn = rms_norm_2(h, norm_mix[l])
        z = xn @ w_in[l]
        z_r, z_q, z_kc, z_vc, z_ks, z_vs, z_kw, z_vw, z_g, z_m = jnp.split(z, split_pts, axis=-1)
        y_r = rwkv7_mixer(z_r, rwkv_mu[l], rwkv_w0[l], rwkv_w2[l], rwkv_a0[l], rwkv_a2[l], rwkv_g2[l],
                          rwkv_kk[l], rwkv_ka[l], rwkv_rk[l], rwkv_lnx_w[l], rwkv_lnx_b[l])
        y_n = nsa_mixer(z_q, z_kc, z_vc, z_ks, z_vs, z_kw, z_vw, z_g, rel_bias, nsa_q_gain[l], nsa_k_gain[l],
                        cmp_pe_k[l], cmp_pe_v[l], cmp_w1_k[l], cmp_w2_k[l], cmp_w1_v[l], cmp_w2_v[l])
        gm = jax.nn.sigmoid(z_m.astype(jnp.float32)).reshape(B, S, 2, D)
        merged = gm[:, :, 0] * (y_r @ w_branch_rwkv[l]) + gm[:, :, 1] * (y_n @ w_branch_nsa[l])
        h = h + merged.astype(h.dtype) @ w_mix_out[l]
        h = h + cross_attn(rms_norm_2(h, norm_cross[l]), rms_norm_2(mem, norm_mem[l]), ca_wq[l], ca_wkv[l],
                           ca_q_gain[l], ca_k_gain[l], ca_wo[l])
        h = h + conv_ffn(rms_norm_2(h, norm_ffn[l]), ffn_up[l], ffn_conv[l], ffn_conv_b[l], ffn_down[l])
    return h


def setup_inputs(seed=0):
    out = dict(first_inputs(seed))
    for name, value in second_inputs(seed + 1).items():
        if name != "x":
            out[name + "_2"] = value
    return out


def reference(
    x, norm_mix, w_in, w_pool, pool_scale, w_out, norm_mlp, w_up, w_down, norm_final, mem_2,
    rel_bias_2, norm_mix_2, w_in_2, rwkv_mu_2, rwkv_w0_2, rwkv_w2_2, rwkv_a0_2, rwkv_a2_2,
    rwkv_g2_2, rwkv_kk_2, rwkv_ka_2, rwkv_rk_2, rwkv_lnx_w_2, rwkv_lnx_b_2, nsa_q_gain_2,
    nsa_k_gain_2, cmp_pe_k_2, cmp_pe_v_2, cmp_w1_k_2, cmp_w2_k_2, cmp_w1_v_2, cmp_w2_v_2,
    w_branch_rwkv_2, w_branch_nsa_2, w_mix_out_2, norm_cross_2, norm_mem_2, ca_wq_2, ca_wkv_2,
    ca_q_gain_2, ca_k_gain_2, ca_wo_2, norm_ffn_2, ffn_up_2, ffn_conv_2, ffn_conv_b_2,
    ffn_down_2,
):
    x = first_block(
        x, norm_mix, w_in, w_pool, pool_scale, w_out, norm_mlp, w_up, w_down, norm_final,
    )
    return second_block(
        x, mem_2, rel_bias_2, norm_mix_2, w_in_2, rwkv_mu_2, rwkv_w0_2, rwkv_w2_2, rwkv_a0_2,
        rwkv_a2_2, rwkv_g2_2, rwkv_kk_2, rwkv_ka_2, rwkv_rk_2, rwkv_lnx_w_2, rwkv_lnx_b_2,
        nsa_q_gain_2, nsa_k_gain_2, cmp_pe_k_2, cmp_pe_v_2, cmp_w1_k_2, cmp_w2_k_2, cmp_w1_v_2,
        cmp_w2_v_2, w_branch_rwkv_2, w_branch_nsa_2, w_mix_out_2, norm_cross_2, norm_mem_2,
        ca_wq_2, ca_wkv_2, ca_q_gain_2, ca_k_gain_2, ca_wo_2, norm_ffn_2, ffn_up_2, ffn_conv_2,
        ffn_conv_b_2, ffn_down_2,
    )


_drawn_inputs = setup_inputs


def setup_inputs(seed=0):
    import zlib

    import numpy as np

    out = dict(_drawn_inputs(seed))
    spreads = {}
    factors = {'norm_mix': 3.377,
     'pool_scale': 4.211,
     'norm_mlp': 2.721,
     'rel_bias_2': 195.312,
     'norm_mix_2': 4.297,
     'rwkv_w2_2': 4.836,
     'rwkv_a0_2': 4.141,
     'rwkv_kk_2': 44.296,
     'rwkv_ka_2': 5.61,
     'rwkv_lnx_w_2': 64.0,
     'rwkv_lnx_b_2': 64.0,
     'nsa_q_gain_2': 26.073,
     'nsa_k_gain_2': 26.021,
     'cmp_pe_k_2': 8.0,
     'cmp_pe_v_2': 26.664,
     'norm_cross_2': 8.0,
     'norm_mem_2': 8.0,
     'ca_q_gain_2': 8.0,
     'ca_k_gain_2': 8.0,
     'norm_ffn_2': 28.702,
     'ffn_conv_b_2': 38.498}
    for name, (base, spread) in spreads.items():
        noise = np.random.default_rng([zlib.crc32(name.encode()), seed]).standard_normal(out[name].shape)
        drawn = base * np.exp(spread * noise) if base else spread * noise
        out[name] = __import__('jax').numpy.asarray(drawn.astype(out[name].dtype))
    for name, factor in factors.items():
        out[name] = (out[name] * factor).astype(out[name].dtype)
    return out
```

```python
from contextlib import ExitStack

import concourse.bass as bass
import numpy as np
from concourse import mybir

F32 = mybir.dt.float32
ACT = mybir.ActivationFunctionType
ALU = mybir.AluOpType
AX = mybir.AxisListType

P = 128
S = 512
D = 1024
DT_ = D // P
NT = S // P
HD = 64
H1 = 8
D_FF = 4096
N_MEM = 256
RH = 16
CH = 64
NCH = S // CH
NKV = 4
HQ = 16
NCMP = (S - 32) // 16 + 1
D_FF2 = 2816
FT2 = D_FF2 // P
RWKV_COLS = 3360
EPS = 1e-6
LNX_EPS = 64e-5
NEG = -1e30
DECAY = float(np.exp(np.float32(-0.5)))
RING = 8
UNIT = 1024
BUCKETS = 32
OH_OFF = 511


def bucket_of(dist):
    n = np.maximum(dist, 0)
    nf = np.maximum(n, 1).astype(np.float32)
    large = 16 + (np.log(nf / 16) / np.log(128 / 16) * 16).astype(np.int32)
    return np.where(n < 16, n, np.minimum(large, 31))


CONST = {}


def constants():
    p = np.arange(P)[:, None]
    c = np.arange(P)[None, :]
    t = np.arange(CH)[None, :]
    q = p % CH
    parts = {
        "ident": (p == c),
        "ones": np.full((P, P), 1.0 / D),
        "ones256": np.full((P, P), 1.0 / 256),
        "head_mean": (p // HD == c // HD) / HD,
        "head_sum": (p // HD == c // HD),
        "ident64": (q == t),
        "diag16": (q // 16 == t // 16) & (q > t),
        "off16": (q // 32 == t // 32) & (q // 16 > t // 16),
        "off32": (q // 32 > t // 32),
        "diag16T": (q // 16 == t // 16) & (q < t),
        "after": (q < t),
        "from": (q <= t),
        "restart": np.broadcast_to((np.arange(S) % CH != 0)[None], (P, S)),
    }
    w = np.arange(S)[None, :]
    neg_dist = (w - p - (S - P)).astype(np.float64)
    parts["neg_dist"] = np.where(neg_dist > 0, NEG, neg_dist)
    cnt = np.stack([1.0 / np.minimum(np.arange(16) + 1, 2 << g) for g in range(4)]).reshape(1, -1)
    parts["inv_count"] = np.broadcast_to(cnt, (P, 64))
    x = np.arange(1024)
    dist = x - OH_OFF
    hot = np.zeros((P, 1024))
    hot[:BUCKETS] = (bucket_of(dist)[None] == np.arange(BUCKETS)[:, None]) & (dist >= 0)[None]
    hot[BUCKETS] = dist < 0
    parts["bucket"] = hot
    at = 0
    for name, a in parts.items():
        CONST[name] = (at, a.shape[1])
        at += a.shape[1]
    return np.concatenate([np.asarray(a, np.float32) for a in parts.values()], axis=1)


N_CONST = constants().shape[1]

VECS = {}


def vec_columns():
    at = 0
    for name, n in (("norm_mix", 8), ("norm_mlp", 8), ("norm_final", 8), ("pool_scale", 4), ("norm_mix_2", 8),
                    ("mu", 27), ("w0", 8), ("a0", 8), ("k_k", 8), ("k_a", 8), ("r_k", 8), ("lnx_w", 8), ("lnx_b", 8),
                    ("norm_cross", 8), ("norm_mem", 8), ("norm_ffn", 8), ("conv", 3 * FT2), ("conv_b", FT2),
                    ("ca_q_gain", 2), ("ca_k_gain", 2), ("q_gain", 1), ("k_gain", 3), ("pe_k", 32), ("pe_v", 32)):
        VECS[name] = at
        at += n
    return at


N_VEC = vec_columns()


class Core:

    def __init__(self, nc, ctx):
        self.nc, self.ctx = nc, ctx
        self.units = []
        self.n_acc = 0
        self.n_aux = 0
        self.count = {}
        self.stages = []

    def sb(self, name, shape):
        return self.ctx.enter_context(self.nc.sbuf_tensor(name, shape, F32))

    def sem(self, name):
        return self.ctx.enter_context(self.nc.semaphore(name))

    def take_acc(self, n=1):
        a = self.n_acc
        self.n_acc += n
        return a

    def take_aux(self, n=1):
        a = self.n_aux
        self.n_aux += n
        return a

    def take_unit(self, acc, n=UNIT):
        self.units.append((len(self.units), n, acc))
        return len(self.units) - 1

    def reserve(self, name, n):
        a = self.count.get(name, 0)
        self.count[name] = a + n
        return a

    def set_up(self):
        sem = self.sem
        self.acc_full = sem("acc_full")
        self.acc_drained = [sem(f"acc_drained{b}") for b in range(4)]
        self.aux_full = sem("aux_full")
        self.aux_drained = [sem(f"aux_drained{b}") for b in range(4)]
        self.w_loaded = [sem(f"w_loaded{i}") for i in range(RING)]
        self.const_loaded = sem("const_loaded")
        self.vec_loaded = sem("vec_loaded")
        self.x_loaded = sem("x_loaded")
        self.x_updated = sem("x_updated")
        self.square_ready = sem("square_ready")
        self.square_used = sem("square_used")
        self.root_ready = sem("root_ready")
        self.xn_ready = sem("xn_ready")
        self.merged_ready = sem("merged_ready")
        self.act_step = sem("act_step")
        self.dve_step = sem("dve_step")
        self.pool_step = sem("pool_step")
        self.steps = {"act": 0, "dve": 0, "pool": 0}

    def after_act(self, act, ins):
        self.steps["act"] += 1
        ins.then_inc(self.act_step, 1)
        act.wait_ge(self.act_step, self.steps["act"])

    def after_dve(self, dve, ins):
        self.steps["dve"] += 1
        ins.then_inc(self.dve_step, 1)
        dve.wait_ge(self.dve_step, self.steps["dve"])

    def after_pool(self, pool, ins):
        self.steps["pool"] += 1
        ins.then_inc(self.pool_step, 1)
        pool.wait_ge(self.pool_step, self.steps["pool"])

    def acc(self, t):
        return self.ps[:, t % 4, :]

    def aux(self, t):
        return self.ps[:, 4 + t % 4, :]

    def wait_acc_full(self, eng, t):
        eng.wait_ge(self.acc_full, t + 1)

    def wait_acc_drained(self, eng, t):
        eng.wait_ge(self.acc_drained[t % 4], t // 4 + 1)

    def open_acc(self, pe, t):
        if t >= 4:
            self.wait_acc_drained(pe, t - 4)

    def wait_aux_full(self, eng, t):
        eng.wait_ge(self.aux_full, t + 1)

    def wait_aux_drained(self, eng, t):
        eng.wait_ge(self.aux_drained[t % 4], t // 4 + 1)

    def open_aux(self, pe, t):
        if t >= 4:
            self.wait_aux_drained(pe, t - 4)

    def weights(self, pe, g):
        pe.wait_ge(self.w_loaded[g % RING], 16 * (g // RING + 1))
        return self.wring[:, g % RING, :]

    def vec(self, name, i=0, lo=0, hi=P):
        c = VECS[name] + i
        return self.vecs[lo:hi, c:c + 1]

    def const(self, name, lo=0, hi=P):
        at, n = CONST[name]
        return self.consts[lo:hi, at:at + n]


def row(ap):
    return ap.rearrange("p a b -> p (a b)")


class Stage:
    def __init__(self, k):
        self.k = k
        k.stages.append(self)

    def sync(self, sp):
        pass

    def tensor(self, pe):
        pass

    def vector(self, dve):
        pass

    def scalar(self, act):
        pass

    def gpsimd(self, pool):
        pass


class InverseRoot:

    def __init__(self, k, t, n, eps, floor=False):
        self.k, self.t, self.n, self.eps, self.floor = k, t, n, eps, floor
        self.at = k.reserve("root", 1)

    def take_mean(self, dve):
        k = self.k
        k.wait_acc_full(dve, self.t)
        op = ALU.max if self.floor else ALU.add
        dve.tensor_scalar(k.root_in[:, 0:self.n], k.acc(self.t)[:, 0:self.n], self.eps, None, op).then_inc(
            k.acc_drained[self.t % 4], 1)

    def guess(self, act):
        k, n = self.k, self.n
        k.wait_acc_drained(act, self.t)
        k.after_act(act, act.activation(k.root_ln[:, 0:n], k.root_in[:, 0:n], ACT.Ln))
        act.activation(k.root_y[:, 0:n], k.root_ln[:, 0:n], ACT.Exp, scale=-0.5).then_inc(k.root_ready, 1)

    def refine(self, dve):
        k, n = self.k, self.n
        y, r, m = k.root_y[:, 0:n], k.root[:, 0:n], k.root_in[:, 0:n]
        dve.wait_ge(k.root_ready, self.at + 1)
        k.after_dve(dve, dve.tensor_tensor(r, y, y, ALU.mult))
        k.after_dve(dve, dve.scalar_tensor_tensor(r, r, -0.5, m, ALU.mult, ALU.mult))
        k.after_dve(dve, dve.scalar_tensor_tensor(r, r, 1.5, y, ALU.add, ALU.mult))
        return r


class Norm(Stage):

    def __init__(self, k, src, dst, gain, wait_src, n=S):
        super().__init__(k)
        self.src, self.dst, self.gain, self.wait_src, self.n = src, dst, gain, wait_src, n
        self.t = k.take_acc()
        self.root = InverseRoot(k, self.t, n, EPS)
        self.sq0 = k.reserve("square", DT_)
        self.used0 = k.reserve("used", DT_ - 1)
        self.ready0 = k.reserve("xn", DT_)

    def wait_dst(self, pe, j):
        pe.wait_ge(self.k.xn_ready, self.ready0 + j + 1)

    def scalar(self, act):
        k = self.k
        for j in range(DT_):
            self.wait_src(act, j)
            if j >= 2:
                act.wait_ge(k.square_used, self.used0 + j - 1)
            act.activation(k.square[:, j % 2, 0:self.n], self.src[:, j, :], ACT.Square).then_inc(k.square_ready, 1)
        self.root.guess(act)

    def tensor(self, pe):
        k = self.k
        pe.wait_ge(k.const_loaded, 16)
        k.open_acc(pe, self.t)
        for j in range(DT_):
            pe.wait_ge(k.square_ready, self.sq0 + j + 1)
            mm = pe.matmul(k.acc(self.t)[:, 0:self.n], k.const("ones"), k.square[:, j % 2, 0:self.n],
                           start=(j == 0), stop=(j == DT_ - 1))
            mm.then_inc(k.square_used if j < DT_ - 1 else k.acc_full, 1)

    def vector(self, dve):
        k = self.k
        self.root.take_mean(dve)
        dve.wait_ge(k.vec_loaded, 16)
        r = self.root.refine(dve)
        for j in range(DT_):
            dve.scalar_tensor_tensor(self.dst[:, j, :], self.src[:, j, :], k.vec(self.gain, j), r,
                                     ALU.mult, ALU.mult).then_inc(k.xn_ready, 1)


class Project(Stage):

    def __init__(self, k, outs, src, wait_src, drains, groups=(8,), kind="features", m=P, n=S):
        super().__init__(k)
        self.src, self.wait_src, self.drains, self.groups, self.kind, self.m, self.n = (
            src, wait_src, drains, groups, kind, m, n)
        self.outs = outs
        self.ts, self.us = [], []
        for _ in range(outs):
            t = k.take_acc()
            self.ts.append(t)
            self.us.append([k.take_unit(t, kc * m) for kc in groups])

    def tensor(self, pe):
        k = self.k
        total = sum(self.groups)
        for i, (t, units) in enumerate(zip(self.ts, self.us)):
            k.open_acc(pe, t)
            at = 0
            views = []
            for g, kc in zip(units, self.groups):
                w = k.weights(pe, g)[:, 0:kc * self.m].rearrange("p (c m) -> p c m", m=self.m)
                if self.kind == "features":
                    for c in range(kc):
                        if i == 0:
                            self.wait_src(pe, at + c)
                        mm = pe.matmul(k.acc(t)[0:self.m, 0:self.n], w[:, c, :], self.src(at + c),
                                       start=(at + c == 0), stop=(at + c == total - 1))
                else:
                    views.append(w)
                at += kc
            if self.kind == "tokens":
                w = views[0]
                if i == 0:
                    self.wait_src(pe, total - 1)
                for b in range(self.n // P):
                    for c in range(total):
                        mm = pe.matmul(k.acc(t)[:, b * self.m:(b + 1) * self.m], self.src(c)[:, b * P:(b + 1) * P],
                                       w[:, c, :], start=(c == 0), stop=(c == total - 1))
            mm.then_inc(k.acc_full, 1)

    def run(self, eng, name):
        for t, drain in zip(self.ts, self.drains):
            if name in drain:
                drain[name](eng, t)

    def vector(self, dve):
        self.run(dve, "vector")

    def scalar(self, act):
        self.run(act, "scalar")

    def gpsimd(self, pool):
        self.run(pool, "gpsimd")


def copy_out(k, dst, scale=1.0, m=P, n=S):
    def scalar(act, t):
        k.wait_acc_full(act, t)
        act.activation(dst, k.acc(t)[0:m, 0:n], ACT.Copy, scale=scale).then_inc(k.acc_drained[t % 4], 1)
    return {"scalar": scalar}


def copy_tokens(k, dst, m, blocks=NT):
    def scalar(act, t):
        k.wait_acc_full(act, t)
        src = k.acc(t)[:, 0:blocks * m].rearrange("p (b m) -> p b m", m=m)
        act.activation(dst, src, ACT.Copy).then_inc(k.acc_drained[t % 4], 1)
    return {"scalar": scalar}


def scale_out(k, dst, gain):
    def scalar(act, t):
        k.wait_acc_full(act, t)
        act.activation(dst, k.acc(t), ACT.Copy, scale=gain).then_inc(k.acc_drained[t % 4], 1)
    return {"scalar": scalar}


def add_residual(k, x):
    def vector(dve, t):
        k.wait_acc_full(dve, t)
        dve.tensor_tensor(x, x, k.acc(t), ALU.add).then_inc(k.acc_drained[t % 4], 1)
    return {"vector": vector}


class Load(Stage):

    def __init__(self, k, x, consts, vecs, weights):
        super().__init__(k)
        self.x, self.consts, self.vecs, self.w = x, consts, vecs, weights

    def sync(self, sp):
        k = self.k
        sp.dma_start(k.x[:, :, :], self.x).then_inc(k.x_loaded, 16)
        sp.dma_start(k.consts[:, :], self.consts).then_inc(k.const_loaded, 16)
        sp.dma_start(k.vecs[:, :], self.vecs).then_inc(k.vec_loaded, 16)
        for g, n, _ in k.units:
            if g >= RING:
                k.wait_acc_full(sp, k.units[g - RING][2])
            sp.dma_start(k.wring[:, g % RING, 0:n], self.w[g, :, 0:n]).then_inc(k.w_loaded[g % RING], 16)


class Pool(Stage):

    def __init__(self, k, u, sums, mixed, cat, u_ts):
        super().__init__(k)
        self.u, self.sums, self.mixed, self.cat, self.u_ts = u, sums, mixed, cat, u_ts
        self.ts = [k.take_acc() for _ in range(4)]
        self.g = k.take_unit(self.ts[-1], 4 * P)
        self.mixed_ready = k.sem("pool_mixed_ready")

    def gpsimd(self, pool):
        k, u, s = self.k, self.u, self.sums
        pool.memset(s[:, :, 0:16], 0.0)
        k.after_pool(pool, pool.memset(u[:, :, 0:16], 0.0))
        for g in range(4):
            k.wait_acc_drained(pool, self.u_ts[g])
            src = u[:, g, :]
            for r in range(g + 1):
                sh = 1 << r
                dst = s[:, r % 2, :]
                k.after_pool(pool, pool.tensor_tensor(dst[:, 16:], src[:, 16:], src[:, 16 - sh:16 + S - sh], ALU.add))
                src = dst
            w = 2 << g
            mean = s[:, (g + 1) % 2, :]
            k.after_pool(pool, pool.tensor_scalar(mean[:, 16:], src[:, 16:], 1.0 / w, None, ALU.mult))
            if g == 0:
                pool.wait_ge(k.const_loaded, 16)
            inv = k.const("inv_count")[:, 16 * g:16 * g + 16]
            k.after_pool(pool, pool.tensor_tensor(mean[:, 16:32], src[:, 16:32], inv, ALU.mult))
            pool.tensor_tensor(self.mixed[:, g, :], mean[:, 16:], u[:, g, 16:], ALU.subtract).then_inc(
                self.mixed_ready, 1)
            pool.wait_ge(self.mixed_ready, g + 1)

    def tensor(self, pe):
        k = self.k
        w = k.weights(pe, self.g)
        for g, t in enumerate(self.ts):
            pe.wait_ge(self.mixed_ready, g + 1)
            k.open_acc(pe, t)
            pe.matmul(k.acc(t), w[:, g * P:(g + 1) * P], self.mixed[:, g, :], start=True, stop=True).then_inc(
                k.acc_full, 1)

    def scalar(self, act):
        k = self.k
        act.wait_ge(k.vec_loaded, 16)
        for g, t in enumerate(self.ts):
            k.wait_acc_full(act, t)
            act.activation(self.cat[:, 4 + g, :], k.acc(t), ACT.Copy, scale=k.vec("pool_scale", g)).then_inc(
                k.acc_drained[t % 4], 1)


class Head:

    def __init__(self, q, keys, values, table, lo, compressed=False, gate=None, first=True, last=True, ready=()):
        self.q, self.keys, self.values, self.table, self.lo = q, keys, values, table, lo
        self.compressed, self.gate, self.first, self.last, self.ready = compressed, gate, first, last, ready


TRI = [0, 128, 384, 768]
TRI_N = 1280
COL = [0, 512, 896, 1152]


class Attention(Stage):

    def __init__(self, k, name, heads, dst, buf):
        super().__init__(k)
        self.heads, self.dst, self.b = heads, dst, buf
        self.aux0 = k.n_aux
        sem = lambda s: k.sem(f"{name}_{s}")
        self.s_full = sem("scores_full")
        self.s_drained = sem("scores_drained")
        self.max_ready = sem("max_ready")
        self.p_ready = sem("probs_ready")
        self.d_ready = sem("diag_ready")
        self.t_full = sem("probs_t_full")
        self.t_drained = sem("probs_t_drained")
        self.pv_done = sem("values_done")
        self.s_at, self.t_at, self.pair, self.pv_at = [], [], [], []
        s = t = v = 0
        acc = None
        opened = set()
        for u, h in enumerate(heads):
            self.s_at.append(s)
            self.t_at.append(t)
            s += 1 if h.compressed else NT
            t += 1 if h.compressed else 3
            if h.first and h.lo == 0:
                acc = k.take_acc()
            self.pair.append(acc)
            h.closes = h.last and h.lo == HD
            self.pv_at.append(v)
            v += 0 if h.closes else 1
        self.s_n, self.t_n = s, t

    def wait_values_done(self, eng, u):
        if self.heads[u].closes:
            self.k.wait_acc_full(eng, self.pair[u])
        else:
            eng.wait_ge(self.pv_done, self.pv_at[u] + 1)

    def scores(self, pe, u):
        k, h = self.k, self.heads[u]
        for wait in h.ready:
            wait(pe)
        if h.compressed:
            s = self.s_at[u]
            if s >= 2:
                pe.wait_ge(self.s_drained, s - 1)
            for i in range(NT):
                mm = pe.matmul(k.ps[:, 4 + s % 2, i * NCMP:(i + 1) * NCMP], h.q[:, i * P:(i + 1) * P], h.keys,
                               start=True, stop=True)
            mm.then_inc(self.s_full, 1)
            return
        for i in range(NT):
            s = self.s_at[u] + i
            n = P * (i + 1)
            if s >= 2:
                pe.wait_ge(self.s_drained, s - 1)
            pe.matmul(k.ps[:, 4 + s % 2, 0:n], h.q[:, i * P:(i + 1) * P], h.keys[:, 0:n],
                      start=True, stop=True).then_inc(self.s_full, 1)

    def probs_t(self, pe, u):
        k, h = self.k, self.heads[u]
        pe.wait_ge(self.d_ready, u + 1)
        p, dg = self.b.p[:, u % 2, :], self.b.diag[:, u % 2, :, :]
        if h.compressed:
            t = self.t_at[u]
            if t >= 2:
                pe.wait_ge(self.t_drained, t - 1)
            for i in range(NT):
                mm = pe.matmul(k.ps[0:NCMP, 6 + t % 2, i * P:(i + 1) * P], p[:, i * NCMP:(i + 1) * NCMP],
                               dg[:, i, :], start=True, stop=True)
            mm.then_inc(self.t_full, 1)
            return
        for part, blocks in enumerate(((0,), (1,), (2, 3))):
            t = self.t_at[u] + part
            if t >= 2:
                pe.wait_ge(self.t_drained, t - 1)
            for j in blocks:
                for i in range(j, NT):
                    at = COL[j] - COL[blocks[0]] + (i - j) * P
                    mm = pe.matmul(k.ps[:, 6 + t % 2, at:at + P], p[:, TRI[i] + j * P:TRI[i] + (j + 1) * P],
                                   dg[:, i, :], start=True, stop=True)
            mm.then_inc(self.t_full, 1)

    def values(self, pe, u):
        k, h = self.k, self.heads[u]
        acc = self.pair[u]
        if h.first and h.lo == 0:
            k.open_acc(pe, acc)
        out = k.acc(acc)[h.lo:h.lo + HD, :]
        pt = self.b.pt[:, u % 2, :]
        if h.compressed:
            pe.wait_ge(self.t_drained, self.t_at[u] + 1)
            mm = pe.matmul(out, h.values, pt[0:NCMP, 0:S], start=h.first, stop=h.last)
        else:
            for j in range(NT):
                pe.wait_ge(self.t_drained, self.t_at[u] + min(j, 2) + 1)
                n = S - j * P
                mm = pe.matmul(out[:, j * P:S], h.values(j), pt[:, COL[j]:COL[j] + n],
                               start=(h.first and j == 0), stop=(h.last and j == NT - 1))
        mm.then_inc(k.acc_full if h.closes else self.pv_done, 1)

    def tensor(self, pe):
        n = len(self.heads)
        for t in range(max(0, self.aux0 - 4), self.aux0):
            self.k.wait_aux_drained(pe, t)
        self.scores(pe, 0)
        for u in range(n):
            if u + 1 < n:
                self.scores(pe, u + 1)
            if u >= 1:
                self.values(pe, u - 1)
            self.probs_t(pe, u)
        self.values(pe, n - 1)

    def add_bias(self, dve, u):
        k, h = self.k, self.heads[u]
        p, mx = self.b.p[:, u % 2, :], self.b.max[:, u % 2, :]
        if u >= 2:
            dve.wait_ge(self.t_full, self.t_at[u - 2] + (1 if self.heads[u - 2].compressed else 3))
        if h.compressed:
            s = self.s_at[u]
            dve.wait_ge(self.s_full, s + 1)
            dst = p[:, 0:NT * NCMP]
            dve.tensor_tensor(dst, k.ps[:, 4 + s % 2, 0:NT * NCMP], h.table, ALU.add).then_inc(self.s_drained, 1)
            dve.wait_ge(self.s_drained, s + 1)
            k.after_dve(dve, dve.tensor_reduce(mx, dst.rearrange("p (i n) -> p i n", n=NCMP), AX.X, ALU.max))
        else:
            for i in range(NT):
                s = self.s_at[u] + i
                n = P * (i + 1)
                dve.wait_ge(self.s_full, s + 1)
                dve.tensor_tensor_reduce(p[:, TRI[i]:TRI[i] + n], k.ps[:, 4 + s % 2, 0:n], h.table[:, S - n:S],
                                         1.0, -3e38, ALU.add, ALU.max, mx[:, i:i + 1]).then_inc(self.s_drained, 1)
            dve.wait_ge(self.s_drained, self.s_at[u] + NT)
        dve.tensor_scalar(self.b.negmax[:, u % 2, :], mx, NEG * 1e-10, -1.0, ALU.max, ALU.mult).then_inc(
            self.max_ready, 1)

    def scale(self, dve, u):
        k, h = self.k, self.heads[u]
        rs = self.b.sum[:, u % 2, :]
        dve.wait_ge(self.p_ready, u + 1)
        k.after_dve(dve, dve.tensor_scalar(self.b.inv[:, 0, :], rs, 1e-30, None, ALU.max))
        k.after_dve(dve, dve.reciprocal(self.b.inv[:, 1, :], self.b.inv[:, 0, :]))
        inv = self.b.inv[:, 1, :]
        if h.gate is not None:
            k.after_dve(dve, dve.tensor_tensor(self.b.inv[:, 2, :], inv, h.gate, ALU.mult))
            inv = self.b.inv[:, 2, :]
        dve.tensor_tensor(self.b.diag[:, u % 2, :, :], k.const("ident").unsqueeze(1).to_broadcast([P, NT, P]),
                          inv.unsqueeze(2).to_broadcast([P, NT, P]), ALU.mult).then_inc(self.d_ready, 1)

    def drain(self, dve, u):
        k = self.k
        t = self.pair[u]
        k.wait_acc_full(dve, t)
        dve.tensor_copy(self.dst(u), k.acc(t)).then_inc(k.acc_drained[t % 4], 1)

    def vector(self, dve):
        n = len(self.heads)
        self.add_bias(dve, 0)
        for u in range(n):
            if u + 1 < n:
                self.add_bias(dve, u + 1)
            self.scale(dve, u)
            if u >= 2 and self.heads[u - 2].closes:
                self.drain(dve, u - 2)
        for u in (n - 2, n - 1):
            if self.heads[u].closes:
                self.drain(dve, u)

    def exps(self, act, u):
        h = self.heads[u]
        p, nm, rs = self.b.p[:, u % 2, :], self.b.negmax[:, u % 2, :], self.b.sum[:, u % 2, :]
        act.wait_ge(self.max_ready, u + 1)
        if u >= 2:
            act.wait_ge(self.d_ready, u - 1)
        for i in range(NT):
            at, n = (i * NCMP, NCMP) if h.compressed else (TRI[i], P * (i + 1))
            e = act.activation(p[:, at:at + n], p[:, at:at + n], ACT.Exp, bias=nm[:, i:i + 1], accum_out=rs[:, i:i + 1])
        e.then_inc(self.p_ready, 1)

    def move_t(self, act, u):
        k, h = self.k, self.heads[u]
        if u >= 2:
            self.wait_values_done(act, u - 2)
        pt = self.b.pt[:, u % 2, :]
        for part in range(1 if h.compressed else 3):
            t = self.t_at[u] + part
            act.wait_ge(self.t_full, t + 1)
            if h.compressed:
                src, dst = k.ps[0:NCMP, 6 + t % 2, :], pt[0:NCMP, 0:S]
            else:
                at, n = ((0, 512), (512, 384), (896, 384))[part]
                src, dst = k.ps[:, 6 + t % 2, 0:n], pt[:, at:at + n]
            act.activation(dst, src, ACT.Copy).then_inc(self.t_drained, 1)

    def scalar(self, act):
        n = len(self.heads)
        self.exps(act, 0)
        for u in range(n):
            if u + 1 < n:
                self.exps(act, u + 1)
            self.move_t(act, u)


class ProjectNorm(Stage):

    def __init__(self, k, outs, src, wait_src, raw, dst, gain, mean, span=1, n=S, eps=EPS):
        super().__init__(k)
        self.outs, self.src, self.wait_src, self.raw, self.dst, self.gain, self.mean, self.span, self.n = (
            outs, src, wait_src, raw, dst, gain, mean, span, n)
        self.ts, self.us, self.mt, self.roots = [], [], [], []
        for i in range(outs + 1):
            if i < outs:
                t = k.take_acc()
                self.ts.append(t)
                self.us.append(k.take_unit(t))
            if i >= 1 and i % span == 0:
                self.mt.append(k.take_acc())
                self.roots.append(InverseRoot(k, self.mt[-1], n, eps))
        self.sq0 = k.reserve("square", outs)
        self.ready0 = k.reserve("xn", outs)

    def wait_dst(self, eng, i):
        eng.wait_ge(self.k.xn_ready, self.ready0 + i + 1)

    def tensor(self, pe):
        k = self.k
        for i in range(self.outs + 1):
            if i < self.outs:
                t = self.ts[i]
                k.open_acc(pe, t)
                w = k.weights(pe, self.us[i]).rearrange("p (c m) -> p c m", m=P)
                for c in range(DT_):
                    if i == 0:
                        self.wait_src(pe, c)
                    mm = pe.matmul(k.acc(t)[:, 0:self.n], w[:, c, :], self.src(c), start=(c == 0), stop=(c == DT_ - 1))
                mm.then_inc(k.acc_full, 1)
            if i >= 1 and i % self.span == 0:
                t = self.mt[i // self.span - 1]
                k.open_acc(pe, t)
                for r in range(self.span):
                    j = i - self.span + r
                    pe.wait_ge(k.square_ready, self.sq0 + j + 1)
                    mm = pe.matmul(k.acc(t)[:, 0:self.n], k.const(self.mean), k.square[:, j % 4, 0:self.n],
                                   start=(r == 0), stop=(r == self.span - 1))
                mm.then_inc(k.acc_full, 1)

    def scalar(self, act):
        k = self.k
        for i in range(self.outs + 1):
            if i < self.outs:
                t = self.ts[i]
                k.wait_acc_full(act, t)
                act.activation(self.raw(i), k.acc(t)[:, 0:self.n], ACT.Copy)
                if i >= 4:
                    k.wait_acc_full(act, self.mt[(i - 4) // self.span])
                act.activation(k.square[:, i % 4, 0:self.n], k.acc(t)[:, 0:self.n], ACT.Square).then_inc(
                    k.square_ready, 1)
                act.wait_ge(k.square_ready, self.sq0 + i + 1)
                act.nop().then_inc(k.acc_drained[t % 4], 1)
            if i >= 1 and i % self.span == 0:
                self.roots[i // self.span - 1].guess(act)

    def vector(self, dve):
        k = self.k
        for a, root in enumerate(self.roots):
            root.take_mean(dve)
            r = root.refine(dve)
            for i in range(a * self.span, (a + 1) * self.span):
                dve.scalar_tensor_tensor(self.dst(i), self.raw(i), self.gain(i), r, ALU.mult, ALU.mult).then_inc(
                    k.xn_ready, 1)


class Tables(Stage):

    def __init__(self, k, rel, rel_last, wide, comp, tab):
        super().__init__(k)
        self.rel, self.rel_last, self.wide, self.comp, self.tab = rel, rel_last, wide, comp, tab
        self.loaded = k.sem("rel_bias_loaded")
        self.loaded2 = k.sem("rel_last_loaded")
        self.tab_ready = k.sem("bias_rows_ready")
        self.ts = [k.take_acc() for _ in range(8 + NT)]

    def gpsimd(self, pool):
        pool.dma_start(self.tab[0:BUCKETS, 0, :], self.rel).then_inc(self.loaded, 16)
        pool.dma_start(self.tab[0:BUCKETS, 1, :], self.rel_last).then_inc(self.loaded2, 16)

    def vector(self, dve):
        t = self.tab
        dve.wait_ge(self.loaded, 16)
        dve.wait_ge(self.loaded2, 16)
        dve.tensor_tensor(t[0:BUCKETS, 2, :], t[0:BUCKETS, 0, :], t[0:BUCKETS, 1, :], ALU.subtract).then_inc(
            self.tab_ready, 1)
        dve.memset(t[BUCKETS:BUCKETS + 1, 2, :], NEG).then_inc(self.tab_ready, 1)
        dve.memset(self.wide[:, :, 0:256], 0.0).then_inc(self.tab_ready, 1)

    def tensor(self, pe):
        k = self.k
        hot = k.const("bucket")
        pe.wait_ge(self.tab_ready, 3)
        rows = self.tab[0:BUCKETS + 1, 2, :]
        for s, t in enumerate(self.ts):
            k.open_acc(pe, t)
            n = 32 if s < 8 else NCMP
            for c in range(n):
                x0 = OH_OFF + (S - P) - (256 + 32 * s + c) if s < 8 else OH_OFF - 31 + P * (s - 8) - 16 * c
                mm = pe.matmul(k.acc(t)[:, c * HQ:(c + 1) * HQ], hot[0:BUCKETS + 1, x0:x0 + P], rows,
                               start=True, stop=True)
            mm.then_inc(k.acc_full, 1)

    def scalar(self, act):
        k = self.k
        act.wait_ge(self.tab_ready, 3)
        for s, t in enumerate(self.ts):
            k.wait_acc_full(act, t)
            if s < 8:
                dst = self.wide[:, :, 256 + 32 * s:288 + 32 * s]
                src = k.acc(t).rearrange("p (c h) -> p h c", h=HQ)
            else:
                dst = self.comp[:, :, (s - 8) * NCMP:(s - 7) * NCMP]
                src = k.acc(t)[:, 0:NCMP * HQ].rearrange("p (c h) -> p h c", h=HQ)
            act.activation(dst, src, ACT.Copy).then_inc(k.acc_drained[t % 4], 1)


class Compress(Stage):

    def __init__(self, k, kc, vc, raw_ready, staged, hid, tmp, keys_raw, keys, values):
        super().__init__(k)
        self.src, self.raw_ready, self.staged, self.hid, self.tmp = (kc, vc), raw_ready, staged, hid, tmp
        self.keys_raw, self.keys, self.values = keys_raw, keys, values
        self.staged_ready = k.sem("blocks_ready")
        self.tanh_in = k.sem("gelu_inner_ready")
        self.tanh_out = k.sem("gelu_tanh_ready")
        self.hid_ready = k.sem("hidden_ready")
        self.ht, self.hu = [], []
        for _ in range(2):
            ts = [k.take_acc() for _ in range(4)]
            self.ht.append(ts)
            self.hu.append([k.take_unit(ts[-1]) for _ in range(8)])
        self.kt, self.mt, self.vt = k.take_acc(), k.take_acc(), k.take_acc()
        self.u2 = k.take_unit(self.vt, 384)
        self.root = InverseRoot(k, self.mt, 124, EPS)
        self.sq0 = k.reserve("square", 1)
        self.ready0 = k.reserve("xn", 1)

    def vector(self, dve):
        k = self.k
        for b in range(2):
            self.raw_ready(dve)
            if b:
                k.wait_acc_full(dve, self.ht[0][3])
            src, pe_ = self.src[b], VECS[("pe_k", "pe_v")[b]]
            for half in range(2):
                for tl in range(2):
                    i0 = src[:, tl, 16 * half:16 * half + 16 * NCMP].rearrange("p (n l) -> p l n", l=16)
                    i1 = k.vecs[:, pe_ + 16 * half:pe_ + 16 * half + 16].unsqueeze(2).to_broadcast([P, 16, NCMP])
                    dve.tensor_tensor(self.staged[:, 16 * half:16 * half + 16, tl * NCMP:(tl + 1) * NCMP], i0, i1,
                                      ALU.add).then_inc(self.staged_ready, 1)
            x, t = self.hid[:, b, :], self.tmp[:, b, :]
            for ts in self.ht[b]:
                k.wait_acc_drained(dve, ts)
            k.after_dve(dve, dve.tensor_tensor(t, x, x, ALU.mult))
            k.after_dve(dve, dve.tensor_scalar(t, t, 0.044715, 1.0, ALU.mult, ALU.add))
            dve.tensor_tensor(t, t, x, ALU.mult).then_inc(self.tanh_in, 1)
            dve.wait_ge(self.tanh_out, b + 1)
            k.after_dve(dve, dve.scalar_tensor_tensor(t, t, 1.0, x, ALU.add, ALU.mult))
            dve.tensor_scalar(x, t, 0.5, None, ALU.mult).then_inc(self.hid_ready, 1)
        self.root.take_mean(dve)
        r = self.root.refine(dve)
        dve.scalar_tensor_tensor(self.keys, self.keys_raw, k.vec("k_gain", 0), r, ALU.mult, ALU.mult).then_inc(
            k.xn_ready, 1)

    def scalar(self, act):
        k = self.k
        for b in range(2):
            for i, t in enumerate(self.ht[b]):
                k.wait_acc_full(act, t)
                act.activation(self.hid[:, b, i * 62:(i + 1) * 62], k.acc(t)[:, 0:62], ACT.Copy).then_inc(
                    k.acc_drained[t % 4], 1)
            act.wait_ge(self.tanh_in, b + 1)
            t = self.tmp[:, b, :]
            act.activation(t, t, ACT.Tanh, scale=float(np.sqrt(2 / np.pi))).then_inc(self.tanh_out, 1)
        k.wait_acc_full(act, self.kt)
        act.activation(self.keys_raw, k.acc(self.kt)[:, 0:124], ACT.Copy)
        act.activation(k.square[:, 0, 0:124], k.acc(self.kt)[:, 0:124], ACT.Square).then_inc(k.square_ready, 1)
        act.wait_ge(k.square_ready, self.sq0 + 1)
        act.nop().then_inc(k.acc_drained[self.kt % 4], 1)
        self.root.guess(act)
        k.wait_acc_full(act, self.vt)
        act.activation(self.values, k.acc(self.vt)[0:NCMP, 0:256].rearrange("p (g d) -> p g d", d=HD),
                       ACT.Copy).then_inc(k.acc_drained[self.vt % 4], 1)

    def wait_done(self, eng):
        eng.wait_ge(self.k.xn_ready, self.ready0 + 1)
        self.k.wait_acc_drained(eng, self.vt)

    def tensor(self, pe):
        k = self.k
        for b in range(2):
            for t in self.ht[b]:
                k.open_acc(pe, t)
            pe.wait_ge(self.staged_ready, 4 * (b + 1))
            for u in range(8):
                w = k.weights(pe, self.hu[b][u]).rearrange("p (l c) -> p l c", c=256)
                for l in range(4):
                    for ch in range(2):
                        for e in range(2):
                            half = slice(e * HD, (e + 1) * HD)
                            mm = pe.matmul(k.acc(self.ht[b][2 * ch + e])[:, 0:62], w[half, l, ch * P:(ch + 1) * P],
                                           self.staged[half, 4 * u + l, :], start=(u == 0 and l == 0),
                                           stop=(u == 7 and l == 3))
                            if u == 7 and l == 3:
                                mm.then_inc(k.acc_full, 1)
        w = k.weights(pe, self.u2)
        wk = w[:, 0:256].rearrange("p (c m) -> p c m", c=2)
        wv = w[:, 256:384].rearrange("p (c m) -> p c m", c=2)
        pe.wait_ge(self.hid_ready, 2)
        k.open_acc(pe, self.kt)
        for ch in range(2):
            mm = pe.matmul(k.acc(self.kt)[:, 0:124], wk[:, ch, :], self.hid[:, 0, ch * 124:(ch + 1) * 124],
                           start=(ch == 0), stop=(ch == 1))
        mm.then_inc(k.acc_full, 1)
        k.open_acc(pe, self.mt)
        pe.wait_ge(k.square_ready, self.sq0 + 1)
        pe.matmul(k.acc(self.mt)[:, 0:124], k.const("head_mean"), k.square[:, 0, 0:124], start=True,
                  stop=True).then_inc(k.acc_full, 1)
        k.open_acc(pe, self.vt)
        for g in range(4):
            for ch in range(2):
                at = ch * 124 + g * NCMP
                mm = pe.matmul(k.acc(self.vt)[0:NCMP, g * HD:(g + 1) * HD], self.hid[:, 1, at:at + NCMP], wv[:, ch, :],
                               start=(ch == 0), stop=(ch == 1))
        mm.then_inc(k.acc_full, 1)


class Spread(Stage):

    def __init__(self, k, src, dst, waits):
        super().__init__(k)
        self.src, self.dst, self.waits = src, dst, waits
        self.done = k.sem("keys_spread")

    def gpsimd(self, pool):
        for b in range(2):
            for g in range(NKV):
                self.waits[b](pool, g // 2)
                e = g % 2
                for half in range(2):
                    pool.dma_start(self.dst[b][half * HD:(half + 1) * HD, g, :],
                                   self.src[b][e * HD:(e + 1) * HD, g // 2, :]).then_inc(self.done, 16)

    def wait_done(self, eng):
        eng.wait_ge(self.done, 16 * 16)


class Gates(Stage):

    def __init__(self, k, g, wait):
        super().__init__(k)
        self.g, self.wait = g, wait
        self.ready = k.sem("gates_ready")

    def vector(self, dve):
        self.wait(dve)
        dve.tensor_scalar(row(self.g), row(self.g), 0.5, 0.5, ALU.mult, ALU.add).then_inc(self.ready, 1)
        dve.wait_ge(self.ready, 1)


class Gated(Stage):

    def __init__(self, k, y, wait_y, xn, merged, tanh, first, wait_merged=None):
        super().__init__(k)
        self.y, self.wait_y, self.xn, self.merged, self.tanh, self.first, self.wait_merged = (
            y, wait_y, xn, merged, tanh, first, wait_merged)
        self.gt, self.bt, self.gu, self.bu = [], [], [], []
        for _ in range(DT_):
            self.gt.append(k.take_acc())
            self.gu.append(k.take_unit(self.gt[-1]))
            self.bt.append(k.take_acc())
            self.bu.append(k.take_unit(self.bt[-1]))

    def tensor(self, pe):
        k = self.k
        for m in range(DT_):
            for t, u, src in ((self.gt[m], self.gu[m], self.xn), (self.bt[m], self.bu[m], self.y)):
                k.open_acc(pe, t)
                w = k.weights(pe, u).rearrange("p (c m) -> p c m", m=P)
                for c in range(DT_):
                    if src is self.y and m == 0:
                        self.wait_y(pe, c)
                    mm = pe.matmul(k.acc(t), w[:, c, :], src[:, c, :], start=(c == 0), stop=(c == DT_ - 1))
                mm.then_inc(k.acc_full, 1)

    def scalar(self, act):
        k = self.k
        for m, t in enumerate(self.gt):
            k.wait_acc_full(act, t)
            if m >= 2:
                if self.first:
                    k.wait_acc_drained(act, self.bt[m - 2])
                else:
                    act.wait_ge(k.merged_ready, m - 1)
            act.activation(self.tanh[:, m % 2, :], k.acc(t), ACT.Tanh, scale=0.5).then_inc(k.acc_drained[t % 4], 1)

    def vector(self, dve):
        k = self.k
        if self.wait_merged:
            self.wait_merged(dve)
        for m, t in enumerate(self.bt):
            k.wait_acc_full(dve, t)
            k.wait_acc_drained(dve, self.gt[m])
            g = self.tanh[:, m % 2, :]
            dst = self.merged[:, m, :] if self.first else g
            ins = dve.scalar_tensor_tensor(dst, g, 1.0, k.acc(t), ALU.add, ALU.mult).then_inc(k.acc_drained[t % 4], 1)
            if not self.first:
                k.wait_acc_drained(dve, t)
                dve.tensor_tensor(self.merged[:, m, :], self.merged[:, m, :], g, ALU.add).then_inc(k.merged_ready, 1)


class RwkvInputs(Stage):

    ORDER = 27

    def __init__(self, k, xn, wait_xn, rkv, zwa, zg, shift, before):
        super().__init__(k)
        self.xn, self.wait_xn, self.rkv, self.zwa, self.zg, self.shift, self.before = (
            xn, wait_xn, rkv, zwa, zg, shift, before)
        self.m = [P] * 26 + [32]
        self.ts, self.us = [], []
        for m in self.m:
            self.ts.append(k.take_acc())
            self.us.append(k.take_unit(self.ts[-1], DT_ * m))
        self.padded = k.sem("shift_padded")
        self.done = k.sem("shifted")
        self.zg_ready = k.sem("zg_ready")
        self.zwa_ready = k.sem("zwa_ready")

    def dst(self, i):
        if i < 24:
            return self.rkv[i // 8][:, i % 8, :]
        if i == 24:
            return self.zwa
        return self.zg[0:self.m[i], i - 25, :]

    def tensor(self, pe):
        k = self.k
        for i, m in enumerate(self.m):
            t = self.ts[i]
            k.open_acc(pe, t)
            w = k.weights(pe, self.us[i])[:, 0:DT_ * m].rearrange("p (c m) -> p c m", m=m)
            for c in range(DT_):
                if i == 0:
                    self.wait_xn(pe, c)
                mm = pe.matmul(k.acc(t)[0:m, :], w[:, c, :], self.xn[:, c, :], start=(c == 0), stop=(c == DT_ - 1))
            mm.then_inc(k.acc_full, 1)

    def scalar(self, act):
        k = self.k
        act.wait_ge(self.padded, 1)
        for i, m in enumerate(self.m):
            t = self.ts[i]
            k.wait_acc_full(act, t)
            if i >= 3:
                act.wait_ge(self.done, i - 2)
            act.activation(self.shift[0:m, i % 3, 1:1 + S], k.acc(t)[0:m, :], ACT.Copy).then_inc(
                k.acc_drained[t % 4], 1)
        act.wait_ge(self.done, 27)
        z = self.zwa[0:64, :]
        act.activation(z, z, ACT.Tanh).then_inc(self.zwa_ready, 1)
        for i in (0, 1):
            z = self.zg[0:self.m[25 + i], i, :]
            k.after_act(act, act.activation(z, z, ACT.Tanh, scale=0.5))
            act.activation(z, z, ACT.Copy, scale=0.5, bias=0.5).then_inc(self.zg_ready, 1)

    def vector(self, dve):
        k = self.k
        self.before(dve)
        dve.memset(self.shift[:, :, 0:1], 0.0).then_inc(self.padded, 1)
        for i, m in enumerate(self.m):
            k.wait_acc_drained(dve, self.ts[i])
            z, prev, dst = self.shift[0:m, i % 3, 1:1 + S], self.shift[0:m, i % 3, 0:S], self.dst(i)
            k.after_dve(dve, dve.tensor_tensor(dst, prev, z, ALU.subtract))
            dve.scalar_tensor_tensor(dst, dst, k.vec("mu", i, 0, m), z, ALU.mult, ALU.add).then_inc(self.done, 1)


class RwkvPrepare(Stage):

    def __init__(self, k, inp, aa, bb, end, tmp, bonus_out):
        super().__init__(k)
        self.inp, self.aa, self.bb, self.end, self.tmp, self.bonus_out = inp, aa, bb, end, tmp, bonus_out
        self.wt, self.at, self.nt, self.bt, self.roots = [], [], [], [], []
        first = k.n_acc
        self.u = None
        for p in range(8):
            self.wt.append(k.take_acc())
            self.at.append(k.take_acc())
            self.nt.append(k.take_acc())
            self.roots.append(InverseRoot(k, self.nt[-1], S, 1e-24, floor=True))
            self.bt.append(k.take_acc())
        self.u = k.take_unit(self.at[-1], 1024)
        self.sq0 = k.reserve("square", 8)
        sem = k.sem
        self.decay_ready = sem("log_decay_sum_ready")
        self.exps_ready = sem("decay_products_ready")
        self.prev_ready = sem("log_decay_before_ready")
        self.kk_ready = sem("kk_ready")
        self.rk_ready = sem("rkk_ready")
        self.bonus_ready = sem("bonus_ready")
        self.bonus_saved = [sem(f"bonus_saved{i}") for i in range(2)]
        self.done = sem("scaled_ready")

    def tensor(self, pe):
        k = self.k
        w = k.weights(pe, self.u)
        z = self.inp.zwa
        pe.wait_ge(self.inp.zwa_ready, 1)
        for p in range(8):
            k.open_acc(pe, self.wt[p])
            pe.matmul(k.acc(self.wt[p]), w[0:64, p * P:(p + 1) * P], z[0:64, :], start=True, stop=True).then_inc(
                k.acc_full, 1)
            k.open_acc(pe, self.at[p])
            pe.matmul(k.acc(self.at[p]), w[64:128, p * P:(p + 1) * P], z[64:128, :], start=True, stop=True).then_inc(
                k.acc_full, 1)
            k.open_acc(pe, self.nt[p])
            pe.wait_ge(k.square_ready, self.sq0 + p + 1)
            pe.matmul(k.acc(self.nt[p]), k.const("head_sum"), k.square[:, p % 4, :], start=True, stop=True).then_inc(
                k.acc_full, 1)
            k.open_acc(pe, self.bt[p])
            pe.wait_ge(self.rk_ready, p + 1)
            pe.matmul(k.acc(self.bt[p]), k.const("head_sum"), self.tmp["rkk"], start=True, stop=True).then_inc(
                k.acc_full, 1)

    def scalar(self, act):
        k, tm = self.k, self.tmp
        for p in range(8):
            k.wait_acc_full(act, self.wt[p])
            act.wait_ge(self.kk_ready, p + 1)
            if p:
                act.wait_ge(self.done, p)
            act.activation(tm["decay"], k.acc(self.wt[p]), ACT.Tanh, scale=0.5, bias=tm["w0h"][:, p:p + 1]).then_inc(
                k.acc_drained[self.wt[p] % 4], 1)
            k.wait_acc_full(act, self.at[p])
            act.activation(tm["a"], k.acc(self.at[p]), ACT.Tanh, scale=0.5, bias=tm["a0h"][:, p:p + 1]).then_inc(
                k.acc_drained[self.at[p] % 4], 1)
            act.activation(k.square[:, p % 4, :], tm["kk"], ACT.Square).then_inc(k.square_ready, 1)
            self.roots[p].guess(act)
            act.wait_ge(self.decay_ready, p + 1)
            act.activation(tm["p"], tm["sum"], ACT.Exp)
            act.activation(tm["inv"], tm["sum"], ACT.Exp, scale=-1.0).then_inc(self.exps_ready, 1)
            act.wait_ge(self.prev_ready, p + 1)
            act.activation(tm["before"], tm["before"], ACT.Exp).then_inc(self.exps_ready, 1)

    def gpsimd(self, pool):
        for p in range(8):
            pool.wait_ge(self.bonus_ready, p + 1)
            pool.dma_start(self.bonus_out[:, p, :], self.tmp["bonus"][:, p % 2, :]).then_inc(
                self.bonus_saved[p % 2], 16)

    def vector(self, dve):
        k, tm = self.k, self.tmp
        (r, kx, v), seq = self.inp.rkv, k.after_dve
        dve.tensor_scalar(tm["w0h"], k.vecs[:, VECS["w0"]:VECS["w0"] + 8], 0.5, None, ALU.mult)
        seq(dve, dve.tensor_scalar(tm["a0h"], k.vecs[:, VECS["a0"]:VECS["a0"] + 8], 0.5, None, ALU.mult))
        for p in range(8):
            rp, kp, vp = r[:, p, :], kx[:, p, :], v[:, p, :]
            dve.tensor_scalar(tm["kk"], kp, k.vec("k_k", p), None, ALU.mult).then_inc(self.kk_ready, 1)
            k.wait_acc_drained(dve, self.wt[p])
            seq(dve, dve.tensor_scalar(tm["decay"], tm["decay"], 1.0, -0.5 * DECAY, ALU.add, ALU.mult))
            dve.tensor_tensor_scan(tm["sum"], k.const("restart"), tm["decay"], 0.0, ALU.mult, ALU.add).then_inc(
                self.decay_ready, 1)
            dve.wait_ge(self.decay_ready, p + 1)
            dve.tensor_tensor(tm["before"], tm["sum"], tm["decay"], ALU.subtract).then_inc(self.prev_ready, 1)
            k.wait_acc_drained(dve, self.at[p])
            seq(dve, dve.tensor_scalar(tm["a"], tm["a"], 0.5, 0.5, ALU.mult, ALU.add))
            seq(dve, dve.tensor_scalar(tm["mix"], tm["a"], 1.0, k.vec("k_a", p), ALU.subtract, ALU.mult))
            seq(dve, dve.scalar_tensor_tensor(kp, tm["mix"], 1.0, kp, ALU.add, ALU.mult))
            if p:
                k.wait_acc_full(dve, self.bt[p - 1])
            dve.scalar_tensor_tensor(tm["rkk"], rp, k.vec("r_k", p), kp, ALU.mult, ALU.mult).then_inc(self.rk_ready, 1)
            dve.wait_ge(self.rk_ready, p + 1)
            self.roots[p].take_mean(dve)
            root = self.roots[p].refine(dve)
            seq(dve, dve.tensor_tensor(tm["kk"], tm["kk"], root, ALU.mult))
            seq(dve, dve.tensor_tensor(tm["a"], tm["a"], tm["kk"], ALU.mult))
            dve.wait_ge(self.exps_ready, 2 * p + 2)
            dve.tensor_tensor(self.bb[:, p, :], tm["a"], tm["inv"], ALU.mult)
            dve.scalar_tensor_tensor(self.aa[:, p, :], tm["kk"], -1.0, tm["before"], ALU.mult, ALU.mult)
            dve.tensor_tensor(rp, rp, tm["p"], ALU.mult)
            dve.tensor_copy(self.end[:, p, :], tm["p"][:, CH - 1:S:CH])
            dve.tensor_tensor(kp, kp, tm["inv"], ALU.mult).then_inc(self.done, 1)
            dve.wait_ge(self.done, p + 1)
            k.wait_acc_full(dve, self.bt[p])
            if p >= 2:
                dve.wait_ge(self.bonus_saved[p % 2], 16 * (p // 2))
            dve.tensor_tensor(tm["bonus"][:, p % 2, :], vp, k.acc(self.bt[p]), ALU.mult).then_inc(
                k.acc_drained[self.bt[p] % 4], 1)
            k.wait_acc_drained(dve, self.bt[p])
            dve.nop().then_inc(self.bonus_ready, 1)


class RwkvScan(Stage):

    STEPS = ("an", "bn", "kn", "vn", "x", "xt", "akt", "rbt", "rkt", "d2", "d2t", "d4", "d4t", "m1", "d8", "m2",
             "m3", "mn", "g", "m4", "mn2", "g2", "m5", "q", "u", "wt", "sa", "y", "z")

    def __init__(self, k, prep, buf):
        super().__init__(k)
        self.prep, self.buf = prep, buf
        self.t = [{s: k.take_aux() for s in self.STEPS} for _ in range(NCH)]
        self.state_cleared = k.sem("scan_state_cleared")
        self.state_ready = k.sem("scan_state_ready")

    def chunk(self, ap, c):
        return ap[:, :, c * CH:(c + 1) * CH]

    def tensor(self, pe):
        k, b = self.k, self.buf
        r, kx, v = self.prep.inp.rkv
        aa, bb = self.prep.aa, self.prep.bb
        ident = k.const("ident64")
        pe.wait_ge(self.prep.done, 8)
        pe.wait_ge(self.state_cleared, 1)

        def cut(ap, p, e):
            return ap[e * HD:(e + 1) * HD, p, :]

        def product(t, *terms):
            k.open_aux(pe, t)
            out = k.aux(t).rearrange("p (a b) -> p a b", b=CH)
            for p in range(8):
                for e in range(2):
                    for i, (lhs, rhs) in enumerate(terms):
                        rr = ident[e * HD:(e + 1) * HD, :] if rhs is None else cut(rhs, p, e)
                        mm = pe.matmul(cut(out, p, e), cut(lhs, p, e), rr, start=(i == 0), stop=(i == len(terms) - 1))
            mm.then_inc(k.aux_full, 1)

        for c in range(NCH):
            t = self.t[c]
            ac, bc, rc, kc, vc = (self.chunk(x, c) for x in (aa, bb, r, kx, v))
            product(t["an"], (ac, None))
            product(t["bn"], (bc, None))
            product(t["kn"], (kc, None))
            product(t["vn"], (vc, None))
            product(t["x"], (ac, bc))
            product(t["xt"], (bc, ac))
            product(t["akt"], (kc, ac))
            product(t["rbt"], (bc, rc))
            product(t["rkt"], (kc, rc))
            k.wait_aux_drained(pe, t["x"])
            k.wait_aux_drained(pe, t["xt"])
            product(t["d2"], (b["dt"], b["d"]))
            product(t["d2t"], (b["d"], b["dt"]))
            k.wait_aux_drained(pe, t["d2"])
            k.wait_aux_drained(pe, t["d2t"])
            product(t["d4"], (b["d2t"], b["d2"]))
            product(t["d4t"], (b["d2"], b["d2t"]))
            product(t["m1"], (b["d2"], b["m0"]))
            k.wait_aux_drained(pe, t["d4"])
            k.wait_aux_drained(pe, t["d4t"])
            product(t["d8"], (b["d4t"], b["d4"]))
            k.wait_aux_drained(pe, t["m1"])
            product(t["m2"], (b["d4"], b["m1"]))
            k.wait_aux_drained(pe, t["d8"])
            k.wait_aux_drained(pe, t["m2"])
            product(t["m3"], (b["d8"], b["m0"]))
            k.wait_aux_drained(pe, t["m3"])
            product(t["mn"], (b["m1"], None))
            product(t["g"], (b["x32"], b["m1"]))
            k.wait_aux_drained(pe, t["mn"])
            k.wait_aux_drained(pe, t["g"])
            product(t["m4"], (b["mn"], b["g"]))
            k.wait_aux_drained(pe, t["m4"])
            product(t["mn2"], (b["m0"], None))
            product(t["g2"], (b["x64"], b["m0"]))
            k.wait_aux_drained(pe, t["mn2"])
            k.wait_aux_drained(pe, t["g2"])
            product(t["m5"], (b["mn"], b["g"]))
            k.wait_aux_drained(pe, t["akt"])
            k.wait_aux_drained(pe, t["vn"])
            product(t["q"], (b["akt"], b["vn"]))
            k.wait_aux_drained(pe, t["q"])
            k.wait_aux_drained(pe, t["m5"])
            product(t["u"], (b["m1"], b["q"]))
            k.wait_aux_drained(pe, t["an"])
            product(t["wt"], (b["an"], b["m1"]))
            k.wait_aux_drained(pe, t["wt"])
            if c:
                pe.wait_ge(self.state_ready, c)
            product(t["sa"], (b["wt"], b["z"]))
            k.wait_aux_drained(pe, t["sa"])
            k.wait_aux_drained(pe, t["rbt"])
            k.wait_aux_drained(pe, t["rkt"])
            product(t["y"], (b["z"], rc), (b["sa"], b["rbt"]), (b["vn"], b["rkt"]))
            k.wait_aux_drained(pe, t["bn"])
            k.wait_aux_drained(pe, t["kn"])
            product(t["z"], (b["bn"], b["sa"]), (b["kn"], b["vn"]))

    def scalar(self, act):
        k, b = self.k, self.buf

        def copy(t, dst):
            k.wait_aux_full(act, t)
            act.activation(dst, k.aux(t).rearrange("p (a b) -> p a b", b=CH), ACT.Copy).then_inc(
                k.aux_drained[t % 4], 1)

        for c in range(NCH):
            t = self.t[c]
            copy(t["an"], b["an"])
            copy(t["bn"], b["bn"])
            copy(t["kn"], b["kn"])
            copy(t["vn"], b["vn"])
            copy(t["d2"], b["d2"])
            copy(t["d2t"], b["d2t"])
            copy(t["d4"], b["d4"])
            copy(t["d4t"], b["d4t"])
            copy(t["d8"], b["d8"])
            copy(t["mn"], b["mn"])
            copy(t["g"], b["g"])
            copy(t["mn2"], b["mn"])
            copy(t["g2"], b["g"])
            copy(t["q"], b["q"])
            copy(t["wt"], b["wt"])
            copy(t["y"], self.chunk(self.prep.inp.rkv[0], c))

    def vector(self, dve):
        k, b = self.k, self.buf
        for s in self.prep.bonus_saved:
            dve.wait_ge(s, 16 * 4)
        dve.memset(row(b["z"]), 0.0).then_inc(self.state_cleared, 1)

        def mask(name):
            return k.const(name).unsqueeze(1).to_broadcast([P, 8, CH])

        def src(t):
            return k.aux(t).rearrange("p (a b) -> p a b", b=CH)

        for c in range(NCH):
            tt = self.t[c]

            def done(ins, step):
                ins.then_inc(k.aux_drained[tt[step] % 4], 1)

            def full(step):
                k.wait_aux_full(dve, tt[step])

            full("x")
            dve.tensor_tensor(b["x32"], src(tt["x"]), mask("off16"), ALU.mult)
            dve.tensor_tensor(b["x64"], src(tt["x"]), mask("off32"), ALU.mult)
            done(dve.tensor_tensor(b["d"], src(tt["x"]), mask("diag16"), ALU.mult), "x")
            full("xt")
            k.after_dve(dve, dve.tensor_tensor(b["dt"], src(tt["xt"]), mask("diag16T"), ALU.mult))
            done(dve.tensor_tensor(b["m0"], b["dt"], mask("ident64"), ALU.add), "xt")
            for step, name in (("akt", "after"), ("rbt", "from"), ("rkt", "from")):
                full(step)
                done(dve.tensor_tensor(b[step], src(tt[step]), mask(name), ALU.mult), step)
            k.wait_aux_drained(dve, tt["xt"])
            full("m1")
            done(dve.tensor_tensor(row(b["m1"]), row(b["m0"]), k.aux(tt["m1"]), ALU.add), "m1")
            for step, dst, old, before in (("m2", "m0", "m1", "m1"), ("m3", "m1", "m0", "m2"),
                                           ("m4", "m0", "m1", "m3"), ("m5", "m1", "m0", "m4")):
                k.wait_aux_drained(dve, tt[before])
                full(step)
                done(dve.tensor_tensor(row(b[dst]), row(b[old]), k.aux(tt[step]), ALU.add), step)
            full("u")
            k.after_dve(dve, dve.tensor_copy(row(b["u"]), k.aux(tt["u"])))
            dve.nop().then_inc(k.aux_drained[tt["u"] % 4], 1)
            full("sa")
            done(dve.tensor_tensor(row(b["sa"]), row(b["u"]), k.aux(tt["sa"]), ALU.add), "sa")
            full("z")
            if c:
                dve.wait_ge(self.state_ready, c)
            done(dve.tensor_tensor(row(b["z"]), row(b["z"]), k.aux(tt["z"]), ALU.add), "z")
            k.wait_aux_drained(dve, tt["z"])
            end = self.prep.end[:, :, c:c + 1].to_broadcast([P, 8, CH])
            dve.tensor_tensor(b["z"], b["z"], end, ALU.mult).then_inc(self.state_ready, 1)

    def wait_y(self, eng):
        self.k.wait_aux_drained(eng, self.t[NCH - 1]["y"])


class RwkvOutput(Stage):

    def __init__(self, k, scan, zg, zg_ready, y, bonus, bonus_in, bonus_saved, tmp):
        super().__init__(k)
        self.scan, self.zg, self.zg_ready, self.y, self.bonus, self.bonus_in, self.bonus_saved, self.tmp = (
            scan, zg, zg_ready, y, bonus, bonus_in, bonus_saved, tmp)
        self.mt, self.vt, self.gt, self.roots = [], [], [], []
        for p in range(8):
            self.mt.append(k.take_acc())
            self.gt.append(k.take_acc())
            self.vt.append(k.take_acc())
            self.roots.append(InverseRoot(k, self.vt[-1], S, LNX_EPS))
        self.us = [k.take_unit(self.gt[-1]), k.take_unit(self.gt[-1])]
        self.sq0 = k.reserve("square", 8)
        self.bonus_loaded = k.sem("bonus_loaded")
        self.centred = k.sem("centred")
        self.ready = k.sem("rwkv_y_ready")

    def gpsimd(self, pool):
        self.scan.wait_y(pool)
        for s in self.bonus_saved:
            pool.wait_ge(s, 16 * 4)
        pool.dma_start(self.bonus, self.bonus_in).then_inc(self.bonus_loaded, 16)

    def tensor(self, pe):
        k = self.k
        self.scan.wait_y(pe)
        pe.wait_ge(self.zg_ready, 2)
        w = [k.weights(pe, u) for u in self.us]
        for p in range(8):
            k.open_acc(pe, self.mt[p])
            pe.matmul(k.acc(self.mt[p]), k.const("head_mean"), self.y[:, p, :], start=True, stop=True).then_inc(
                k.acc_full, 1)
            k.open_acc(pe, self.gt[p])
            pe.matmul(k.acc(self.gt[p]), w[0][:, p * P:(p + 1) * P], self.zg[:, 0, :], start=True, stop=False)
            pe.matmul(k.acc(self.gt[p]), w[1][0:32, p * P:(p + 1) * P], self.zg[0:32, 1, :], start=False,
                      stop=True).then_inc(k.acc_full, 1)
            k.open_acc(pe, self.vt[p])
            pe.wait_ge(k.square_ready, self.sq0 + p + 1)
            pe.matmul(k.acc(self.vt[p]), k.const("head_mean"), k.square[:, p % 4, :], start=True, stop=True).then_inc(
                k.acc_full, 1)

    def scalar(self, act):
        k = self.k
        for p in range(8):
            act.wait_ge(self.centred, p + 1)
            act.activation(k.square[:, p % 4, :], self.y[:, p, :], ACT.Square).then_inc(k.square_ready, 1)
            self.roots[p].guess(act)

    def vector(self, dve):
        k = self.k
        dve.wait_ge(self.bonus_loaded, 16)
        for p in range(8):
            y, t = self.y[:, p, :], self.mt[p]
            k.wait_acc_full(dve, t)
            dve.tensor_tensor(y, y, k.acc(t), ALU.subtract).then_inc(k.acc_drained[t % 4], 1)
            k.wait_acc_drained(dve, t)
            dve.nop().then_inc(self.centred, 1)
            self.roots[p].take_mean(dve)
            root = self.roots[p].refine(dve)
            k.after_dve(dve, dve.scalar_tensor_tensor(y, y, k.vec("lnx_w", p), root, ALU.mult, ALU.mult))
            k.after_dve(dve, dve.scalar_tensor_tensor(y, y, k.vec("lnx_b", p), self.bonus[:, p, :], ALU.add, ALU.add))
            t = self.gt[p]
            k.wait_acc_full(dve, t)
            dve.tensor_tensor(y, y, k.acc(t), ALU.mult).then_inc(k.acc_drained[t % 4], 1)

    def wait_out(self, eng, c):
        self.k.wait_acc_drained(eng, self.gt[c])


class CrossAttention(Stage):

    def __init__(self, k, q, keys, values, out, buf, waits):
        super().__init__(k)
        self.q, self.keys, self.values, self.out, self.buf, self.waits = q, keys, values, out, buf, waits
        self.st, self.tt, self.ot = [], [], []
        for _ in range(4):
            self.st.append([k.take_acc(), k.take_acc()])
            self.tt.append([k.take_acc(), k.take_acc()])
            self.ot.append([k.take_acc(), k.take_acc()])
        self.max_ready = k.sem("cross_max_ready")
        self.p_ready = k.sem("cross_probs_ready")
        self.d_ready = k.sem("cross_diag_ready")

    def tensor(self, pe):
        k, b = self.k, self.buf
        for w in self.waits:
            w(pe)
        for h in range(4):
            for i, t in enumerate(self.st[h]):
                k.open_acc(pe, t)
                for j in range(2):
                    for c in range(2):
                        tok = slice((2 * i + j) * P, (2 * i + j + 1) * P)
                        mm = pe.matmul(k.acc(t)[:, j * N_MEM:(j + 1) * N_MEM], self.q[:, 2 * h + c, tok],
                                       self.keys[:, 2 * h + c, :], start=(c == 0), stop=(c == 1))
                mm.then_inc(k.acc_full, 1)
            pe.wait_ge(self.d_ready, h + 1)
            for j, t in enumerate(self.tt[h]):
                k.open_acc(pe, t)
                for i in range(NT):
                    mm = pe.matmul(k.acc(t)[:, i * P:(i + 1) * P], b.p[:, i * N_MEM + j * P:i * N_MEM + (j + 1) * P],
                                   b.diag[:, i, :], start=True, stop=True)
                mm.then_inc(k.acc_full, 1)
            for c, t in enumerate(self.ot[h]):
                k.open_acc(pe, t)
                for j in range(2):
                    if c == 0:
                        k.wait_acc_drained(pe, self.tt[h][j])
                    at = h * 256 + c * P
                    mm = pe.matmul(k.acc(t), self.values[:, j, at:at + P], b.pt[:, j * S:(j + 1) * S],
                                   start=(j == 0), stop=(j == 1))
                mm.then_inc(k.acc_full, 1)

    def vector(self, dve):
        k, b = self.k, self.buf
        for h in range(4):
            for i, t in enumerate(self.st[h]):
                k.wait_acc_full(dve, t)
                m = dve.tensor_reduce(b.max[:, 0, 2 * i:2 * i + 2],
                                      k.acc(t).rearrange("p (j n) -> p j n", n=N_MEM), AX.X, ALU.max)
                k.after_dve(dve, m)
            dve.tensor_scalar(b.negmax[:, 0, :], b.max[:, 0, :], -1.0 / 16, None, ALU.mult).then_inc(self.max_ready, 1)
            dve.wait_ge(self.p_ready, 4 * (h + 1))
            k.after_dve(dve, dve.reciprocal(b.inv[:, 0, :], b.sum[:, 0, :]))
            dve.tensor_tensor(b.diag, k.const("ident").unsqueeze(1).to_broadcast([P, NT, P]),
                              b.inv[:, 0, :].unsqueeze(2).to_broadcast([P, NT, P]), ALU.mult).then_inc(self.d_ready, 1)
            for c, t in enumerate(self.ot[h]):
                k.wait_acc_full(dve, t)
                dve.tensor_copy(self.out[:, 2 * h + c, :], k.acc(t)).then_inc(k.acc_drained[t % 4], 1)

    def scalar(self, act):
        k, b = self.k, self.buf
        for h in range(4):
            act.wait_ge(self.max_ready, h + 1)
            for i in range(NT):
                t = self.st[h][i // 2]
                src = k.acc(t)[:, (i % 2) * N_MEM:(i % 2 + 1) * N_MEM]
                act.activation(b.p[:, i * N_MEM:(i + 1) * N_MEM], src, ACT.Exp, scale=1.0 / 16,
                               bias=b.negmax[:, 0, i:i + 1], accum_out=b.sum[:, 0, i:i + 1]).then_inc(self.p_ready, 1)
                if i % 2:
                    act.wait_ge(self.p_ready, 4 * h + i + 1)
                    act.nop().then_inc(k.acc_drained[t % 4], 1)
            for j, t in enumerate(self.tt[h]):
                k.wait_acc_full(act, t)
                act.activation(b.pt[:, j * S:(j + 1) * S], k.acc(t), ACT.Copy).then_inc(k.acc_drained[t % 4], 1)

    def wait_out(self, eng, c):
        self.k.wait_acc_drained(eng, self.ot[c // 2][c % 2])


class ConvFfn(Stage):

    def __init__(self, k, xn, wait_xn, hidden, abuf, t0, t1, before):
        super().__init__(k)
        self.xn, self.wait_xn, self.hidden, self.abuf, self.t0, self.t1, self.before = (
            xn, wait_xn, hidden, abuf, t0, t1, before)
        self.at, self.bt, self.au, self.bu = [], [], [], []
        for _ in range(FT2):
            self.at.append(k.take_acc())
            self.au.append(k.take_unit(self.at[-1]))
            self.bt.append(k.take_acc())
            self.bu.append(k.take_unit(self.bt[-1]))
        self.padded = k.sem("conv_padded")
        self.conv_ready = k.sem("conv_ready")
        self.tanh_ready = k.sem("silu_tanh_ready")

    def tensor(self, pe):
        k = self.k
        for m in range(FT2):
            for t, u in ((self.at[m], self.au[m]), (self.bt[m], self.bu[m])):
                k.open_acc(pe, t)
                w = k.weights(pe, u).rearrange("p (c m) -> p c m", m=P)
                for c in range(DT_):
                    if m == 0:
                        self.wait_xn(pe, c)
                    mm = pe.matmul(k.acc(t), w[:, c, :], self.xn[:, c, :], start=(c == 0), stop=(c == DT_ - 1))
                mm.then_inc(k.acc_full, 1)

    def scalar(self, act):
        k = self.k
        act.wait_ge(self.padded, 1)
        for m, t in enumerate(self.at):
            k.wait_acc_full(act, t)
            if m >= 2:
                act.wait_ge(self.conv_ready, m - 1)
            act.activation(self.abuf[:, m % 2, 2:2 + S], k.acc(t), ACT.Copy).then_inc(k.acc_drained[t % 4], 1)
            act.wait_ge(self.conv_ready, m + 1)
            if m >= 2:
                k.wait_acc_drained(act, self.bt[m - 2])
            act.activation(self.t1[:, m % 2, :], self.t0[:, m % 2, :], ACT.Tanh, scale=0.5).then_inc(self.tanh_ready, 1)

    def vector(self, dve):
        k = self.k
        self.before(dve)
        dve.memset(self.abuf[:, :, 0:2], 0.0).then_inc(self.padded, 1)
        for m, t in enumerate(self.bt):
            k.wait_acc_drained(dve, self.at[m])
            a, c = self.abuf[:, m % 2, :], self.t0[:, m % 2, :]
            k.after_dve(dve, dve.tensor_scalar(c, a[:, 2:2 + S], k.vec("conv", 2 * FT2 + m), k.vec("conv_b", m),
                                               ALU.mult, ALU.add))
            k.after_dve(dve, dve.scalar_tensor_tensor(c, a[:, 1:1 + S], k.vec("conv", FT2 + m), c, ALU.mult, ALU.add))
            dve.scalar_tensor_tensor(c, a[:, 0:S], k.vec("conv", m), c, ALU.mult, ALU.add).then_inc(self.conv_ready, 1)
            dve.wait_ge(self.tanh_ready, m + 1)
            k.after_dve(dve, dve.scalar_tensor_tensor(c, self.t1[:, m % 2, :], 1.0, c, ALU.add, ALU.mult))
            k.wait_acc_full(dve, t)
            dve.scalar_tensor_tensor(self.hidden[:, m, :], c, 0.5, k.acc(t), ALU.mult, ALU.mult).then_inc(
                k.acc_drained[t % 4], 1)


class Move(Stage):

    def __init__(self, k, name, dst, src, waits):
        super().__init__(k)
        self.dst, self.src, self.waits = dst, src, waits
        self.done = k.sem(name)

    def gpsimd(self, pool):
        for w in self.waits:
            w(pool)
        pool.dma_start(self.dst, self.src).then_inc(self.done, 16)

    def wait_done(self, eng):
        eng.wait_ge(self.done, 16)


class Alibi(Stage):

    def __init__(self, k, table):
        super().__init__(k)
        self.table = table
        self.ready = k.sem("alibi_ready")

    def scalar(self, act):
        k = self.k
        act.wait_ge(k.const_loaded, 16)
        for h in range(H1):
            act.activation(self.table[:, h, :], k.const("neg_dist"), ACT.Copy,
                           scale=float(2.0 ** (-8.0 * (h + 1) / H1))).then_inc(self.ready, 1)


class Store(Stage):

    def __init__(self, k, out, wait_x):
        super().__init__(k)
        self.out, self.wait_x = out, wait_x
        self.stored = k.sem("out_stored")

    def sync(self, sp):
        for j in range(DT_):
            self.wait_x(sp, j)
            sp.dma_start(self.out[:, j, :], self.k.x[:, j, :]).then_inc(self.stored, 16)
        sp.wait_ge(self.stored, 16 * DT_)


class Buffers:

    def __init__(self, view, p, pt, diag, small, steps=2):
        n = TRI_N if steps == 2 else NT * N_MEM
        self.p = view(p, [steps, n]) if steps == 2 else view(p, [n])
        self.pt = view(pt, [steps, n]) if steps == 2 else view(pt, [2 * S])
        self.diag = view(diag, [steps, NT, P]) if steps == 2 else view(diag, [NT, P])
        self.max, self.negmax, self.sum = (view(small + 8 * i, [2, NT]) for i in range(3))
        self.inv = view(small + 24, [3, NT])


def build(nc, x, consts, vecs, weights, rel, rel_last, mem, out):
    with ExitStack() as ctx:
        k = Core(nc, ctx)
        k.set_up()
        ARENA = 37884
        arena = k.sb("arena", [P, ARENA])
        k.wring = k.sb("wring", [P, RING, UNIT])
        k.consts = k.sb("consts_sb", [P, N_CONST])
        k.vecs = k.sb("vecs_sb", [P, N_VEC])
        k.square = k.sb("square", [P, 4, S])
        k.root_in = k.sb("root_in", [P, S])
        k.root_ln = k.root_y = k.sb("root_y", [P, S])
        k.root = k.sb("root", [P, S])
        k.ps = ctx.enter_context(nc.psum_tensor("ps", [P, 8, S], F32))
        bonus_dram = nc.dram_tensor("bonus_scratch", (P, DT_, S), F32, kind="Internal").ap()
        x_dram = nc.dram_tensor("x_scratch", (P, DT_, S), F32, kind="Internal").ap()

        def view(at, shape, parts=P):
            n = int(np.prod(shape))
            assert at + n <= ARENA, (at, shape)
            a = arena[0:parts, at:at + n]
            if len(shape) == 1:
                return a
            if len(shape) == 2:
                return a.rearrange("p (a b) -> p a b", b=shape[1])
            return a.rearrange("p (a b c) -> p a b c", b=shape[1], c=shape[2])

        k.x = view(0, [DT_, S])
        xn = view(4096, [DT_, S])
        free = 8192

        def drained(stage):
            return lambda eng, j: k.wait_acc_drained(eng, stage.ts[j])

        def tiles(ap):
            return lambda j: ap[:, j, :]

        Load(k, x, consts, vecs, weights)
        cat = view(free, [DT_, S])
        qk = view(12288, [8, S])
        v1 = view(16384, [NT, S])
        u1 = view(18432, [4, 16 + S])
        sums = view(20544, [2, 16 + S])
        mixed = view(21600, [4, S])
        alibi = view(23648, [H1, S])
        buf1 = Buffers(view, 27744, 30304, 32864, 33888)
        al = Alibi(k, alibi)
        n1 = Norm(k, k.x, xn, "norm_mix", lambda eng, j: eng.wait_ge(k.x_loaded, 16))
        pq = Project(k, 8, tiles(xn), n1.wait_dst,
                     [copy_out(k, qk[:, i, :], 0.125 if i < 4 else 1.0) for i in range(8)])
        pv = Project(k, 4, tiles(xn), n1.wait_dst,
                     [copy_tokens(k, v1[:, :, i * P:(i + 1) * P], P) for i in range(4)], kind="tokens")
        pu = Project(k, 4, tiles(xn), n1.wait_dst, [copy_out(k, u1[:, i, 16:16 + S]) for i in range(4)])
        pool = Pool(k, u1, sums, mixed, cat, pu.ts)
        heads = []
        for h in range(H1):
            lo, p = HD * (h % 2), h // 2
            ready = [lambda pe, p=p: k.wait_acc_drained(pe, pq.ts[p]),
                     lambda pe, p=p: k.wait_acc_drained(pe, pq.ts[4 + p]),
                     lambda pe, p=p: k.wait_acc_drained(pe, pv.ts[p])]
            if h == 0:
                ready.append(lambda pe: pe.wait_ge(al.ready, H1))
            heads.append(Head(qk[lo:lo + HD, p, :], qk[lo:lo + HD, 4 + p, :],
                              lambda j, h=h: v1[:, j, h * HD:(h + 1) * HD], alibi[:, h, :], lo, ready=ready))
        at1 = Attention(k, "moba", heads, lambda u: cat[:, u // 2, :], buf1)

        def wait_cat(pe, c):
            k.wait_acc_drained(pe, at1.pair[2 * c] if c < 4 else pool.ts[c - 4])

        po = Project(k, 8, tiles(cat), wait_cat, [add_residual(k, k.x[:, i, :]) for i in range(8)])
        n2 = Norm(k, k.x, xn, "norm_mlp", drained(po))
        hid = view(free, [32, S])
        hid_ready = k.sem("mlp_hidden_ready")

        def relu2(i):
            def scalar(act, t):
                k.wait_acc_full(act, t)
                act.activation(hid[:, i, :], k.acc(t), ACT.Relu).then_inc(k.acc_drained[t % 4], 1)

            def vector(dve, t):
                k.wait_acc_drained(dve, t)
                dve.tensor_tensor(hid[:, i, :], hid[:, i, :], hid[:, i, :], ALU.mult).then_inc(hid_ready, 1)
            return {"scalar": scalar, "vector": vector}

        Project(k, 32, tiles(xn), n2.wait_dst, [relu2(i) for i in range(32)])
        pd = Project(k, 8, tiles(hid), lambda pe, c: pe.wait_ge(hid_ready, c + 1),
                     [add_residual(k, k.x[:, i, :]) for i in range(8)], groups=(8, 8, 8, 8))
        n3 = Norm(k, k.x, k.x, "norm_final", drained(pd))

        n4 = Norm(k, k.x, xn, "norm_mix_2", n3.wait_dst)
        save_x = Move(k, "x_saved", x_dram, k.x, [lambda e: n4.wait_dst(e, 7)])
        rr, kk, vv, aa, bb = (view(free + 4096 * i, [DT_, S]) for i in range(5))
        zwa, zg, end = view(28672, [S]), view(29184, [2, S]), view(30208, [DT_, NCH])
        tail = 30272
        shift = view(tail + 6000, [3, 1 + S])
        inp = RwkvInputs(k, xn, n4.wait_dst, (rr, kk, vv), zwa, zg, shift, lambda e: n4.wait_dst(e, 7))
        tmp = {n: view(tail + S * i, [S]) for i, n in enumerate(("decay", "a", "kk", "sum", "before", "p", "inv", "mix", "rkk"))}
        tmp["bonus"] = view(tail + 9 * S, [2, S])
        tmp["w0h"], tmp["a0h"] = view(tail + 11 * S, [8]), view(tail + 11 * S + 8, [8])
        prep = RwkvPrepare(k, inp, aa, bb, end, tmp, bonus_dram)
        names = ("an", "bn", "kn", "vn", "d", "dt", "x32", "x64", "m0", "m1", "akt", "rbt", "rkt", "d2",
                 "d2t", "d4", "d4t", "d8", "mn", "wt", "sa", "z")
        sbuf = {n: view(tail + S * i if i < 14 else S * (i - 14), [DT_, CH]) for i, n in enumerate(names)}
        sbuf["q"], sbuf["u"], sbuf["g"] = sbuf["d8"], sbuf["d4t"], sbuf["d2t"]
        scan = RwkvScan(k, prep, sbuf)
        outp = RwkvOutput(k, scan, zg, inp.zg_ready, rr, vv, bonus_dram, prep.bonus_saved, None)
        merged = aa
        tanh = view(34944, [2, S])
        br = Gated(k, rr, outp.wait_out, xn, merged, tanh, first=True)

        wide = view(8192, [HQ, S])
        q2 = view(16384, [DT_, S])
        kd = [view(24576 + 2048 * i, [NKV, S]) for i in range(2)]
        vs = [view(28672 + 1024 * i, [NT, 256]) for i in range(2)]
        comp = view(30720, [HQ, NT * NCMP])
        gate = view(32704, [NT, 48])
        kraw = [view(32896 + 1024 * i, [2, S]) for i in range(2)]
        kc, vc = view(0, [2, S]), view(1024, [2, S])
        staged = view(2048, [32, 62])
        chid, ctmp, keys_raw = view(34944, [2, 248]), view(35440, [2, 248]), view(35936, [124])
        keys, values = view(37504, [124]), view(37628, [NKV, HD], parts=NCMP)
        tab = view(36100, [3, HQ], parts=BUCKETS + 1)
        buf2 = Buffers(view, 0, 34944, 2560, 3584)

        tb = Tables(k, rel, rel_last, wide, comp, tab)
        gain8 = k.sb("q_gain_scaled", [P, 1])
        gain_ready = k.sem("q_gain_ready")
        nq = ProjectNorm(k, 8, tiles(xn), lambda pe, c: None, tiles(q2), tiles(q2), lambda i: gain8[:, 0:1], "head_mean")
        pkv = Project(k, 4, tiles(xn), lambda pe, c: None,
                      [copy_out(k, (kc, vc)[i // 2][:, i % 2, :]) for i in range(4)])
        cmp_ = Compress(k, kc, vc, lambda e: [k.wait_acc_drained(e, t) for t in pkv.ts], staged, chid, ctmp,
                        keys_raw, keys, values)
        nk = [ProjectNorm(k, 2, tiles(xn), lambda pe, c: None, tiles(kraw[b]), tiles(kraw[b]),
                          lambda i, b=b: k.vec("k_gain", 1 + b), "head_mean") for b in range(2)]
        spread = Spread(k, kraw, kd, [nk[0].wait_dst, nk[1].wait_dst])
        pvs = [Project(k, 2, tiles(xn), lambda pe, c: None,
                       [copy_tokens(k, vs[b][:, :, i * P:(i + 1) * P], P) for i in range(2)], kind="tokens")
               for b in range(2)]

        def gate_tanh():
            def scalar(act, t):
                k.wait_acc_full(act, t)
                act.activation(gate, k.acc(t)[:, 0:NT * 48].rearrange("p (b m) -> p b m", m=48), ACT.Tanh,
                               scale=0.5).then_inc(k.acc_drained[t % 4], 1)
            return {"scalar": scalar}

        pg = Project(k, 1, tiles(xn), lambda pe, c: None, [gate_tanh()], kind="tokens", m=48)
        gates = Gates(k, gate, lambda e: k.wait_acc_drained(e, pg.ts[0]))
        heads = []
        for pair in range(DT_):
            g = pair // 2
            slot = (g % 2) * 2 + g // 2
            for e in range(2):
                h, lo = 2 * pair + e, HD * e
                hf = slice(lo, lo + HD)
                qh = q2[hf, pair, :]
                gt = lambda b, h=h: gate[:, :, 3 * h + b:3 * h + b + 1].rearrange("p a b -> p (a b)")
                ready = []
                if h == 0:
                    ready = [lambda pe: nq.wait_dst(pe, 7), spread.wait_done, cmp_.wait_done,
                             lambda pe: pe.wait_ge(gates.ready, 1),
                             lambda pe: [k.wait_acc_drained(pe, t) for p_ in pvs for t in p_.ts],
                             lambda pe: [k.wait_acc_drained(pe, t) for t in tb.ts]]
                for b in range(2):
                    heads.append(Head(qh, kd[b][hf, g, :], lambda j, b=b, g=g: vs[b][:, j, g * HD:(g + 1) * HD],
                                      wide[:, h, :], lo, gate=gt(1 + b), first=(b == 0), last=False,
                                      ready=ready if b == 0 else ()))
                heads.append(Head(qh, keys[hf, slot * NCMP:(slot + 1) * NCMP], values[:, slot, :], comp[:, h, :], lo,
                                  compressed=True, gate=gt(0), first=False, last=True))
        at2 = Attention(k, "nsa", heads, lambda u: q2[:, u // 6, :], buf2)
        bn = Gated(k, q2, lambda pe, c: k.wait_acc_drained(pe, at2.pair[6 * c]), xn, merged, tanh, first=False,
                   wait_merged=lambda e: [k.wait_acc_drained(e, t) for t in br.bt])
        load_x = Move(k, "x_back", k.x, x_dram, [save_x.wait_done, lambda e: k.wait_acc_drained(e, at2.pair[-1])])

        def add_half(i):
            def vector(dve, t):
                if i == 0:
                    load_x.wait_done(dve)
                k.wait_acc_full(dve, t)
                dve.scalar_tensor_tensor(k.x[:, i, :], k.acc(t), 0.5, k.x[:, i, :], ALU.mult, ALU.add).then_inc(
                    k.acc_drained[t % 4], 1)
            return {"vector": vector}

        pm = Project(k, 8, tiles(merged), lambda pe, c: pe.wait_ge(k.merged_ready, c + 1), [add_half(i) for i in range(8)])

        mem_t = view(8192, [DT_, N_MEM])
        load_mem = Move(k, "mem_loaded", mem_t, mem, [lambda e: k.wait_acc_drained(e, at2.pair[-1])])
        nm = Norm(k, mem_t, mem_t, "norm_mem", lambda e, j: load_mem.wait_done(e), n=N_MEM)
        q3, k3 = view(12288, [DT_, S]), view(16384, [DT_, N_MEM])
        v3, o3 = view(18432, [2, D]), view(24576, [DT_, S])
        pk = ProjectNorm(k, 8, tiles(mem_t), nm.wait_dst, tiles(k3), tiles(k3),
                         lambda i: k.vec("ca_k_gain", i % 2), "ones256", span=2, n=N_MEM)
        pv3 = Project(k, 8, tiles(mem_t), nm.wait_dst,
                      [copy_tokens(k, v3[:, :, i * P:(i + 1) * P], P, blocks=2) for i in range(8)], kind="tokens",
                      n=N_MEM)
        nx = Norm(k, k.x, xn, "norm_cross", drained(pm))
        pq3 = ProjectNorm(k, 8, tiles(xn), nx.wait_dst, tiles(q3), tiles(q3), lambda i: k.vec("ca_q_gain", i % 2),
                          "ones256", span=2)
        buf3 = Buffers(view, 28672, 29696, 30720, 31232, steps=1)
        ca = CrossAttention(k, q3, k3, v3, o3, buf3,
                            [lambda pe: pk.wait_dst(pe, 7), lambda pe: pq3.wait_dst(pe, 7),
                             lambda pe: [k.wait_acc_drained(pe, t) for t in pv3.ts]])
        pco = Project(k, 8, tiles(o3), ca.wait_out, [add_residual(k, k.x[:, i, :]) for i in range(8)])

        nf = Norm(k, k.x, xn, "norm_ffn", drained(pco))
        hid2 = view(8192, [FT2, S])
        abuf, t0, t1 = view(20480, [2, 2 + S]), view(21600, [2, S]), view(22624, [2, S])
        ff = ConvFfn(k, xn, nf.wait_dst, hid2, abuf, t0, t1, lambda e: nf.wait_dst(e, 7))
        pf = Project(k, 8, tiles(hid2), lambda pe, c: k.wait_acc_drained(pe, ff.bt[c]),
                     [add_residual(k, k.x[:, i, :]) for i in range(8)], groups=(8, 8, 6))
        Store(k, out, drained(pf))

        def scaled_gain(dve):
            dve.tensor_scalar(gain8[:, :], k.vec("q_gain"), 0.125, None, ALU.mult).then_inc(gain_ready, 1)
            dve.wait_ge(gain_ready, 1)

        stages = k.stages
        block = ctx.enter_context(nc.Block())

        @block.sync
        def _(sp):
            for s in stages:
                s.sync(sp)

        @block.tensor
        def _(pe):
            for s in stages:
                s.tensor(pe)

        @block.vector
        def _(dve):
            dve.wait_ge(k.vec_loaded, 16)
            scaled_gain(dve)
            for s in stages:
                s.vector(dve)

        @block.scalar
        def _(act):
            for s in stages:
                s.scalar(act)

        @block.gpsimd
        def _(pool_engine):
            for s in stages:
                s.gpsimd(pool_engine)
        return [u[1] for u in k.units]


def tiled(w, m=P):
    kt = w.shape[0] // P
    return [w[:, i:i + m].reshape(kt, P, -1).transpose(1, 0, 2).reshape(P, -1) for i in range(0, w.shape[1], m)]


def cut_units(tile, sizes):
    out, at = [], 0
    for n in sizes:
        out.append(tile[:, at * P:(at + n) * P])
        at += n
    return out


def stream(a):
    units = []
    w = a["w_in"][0]
    units += tiled(w[:, 0:1024]) + tiled(w[:, 1024:1536]) + tiled(w[:, 1536:2048])
    units.append(a["w_pool"][0].transpose(1, 0, 2).reshape(P, 4 * P))
    units += tiled(a["w_out"][0]) + tiled(a["w_up"][0])
    for t in tiled(a["w_down"][0]):
        units += cut_units(t, (8, 8, 8, 8))
    w2 = a["w_in_2"][0]
    units += tiled(w2[:, 0:RWKV_COLS])
    units.append(np.concatenate([a["rwkv_w2_2"][0], a["rwkv_a2_2"][0]], axis=0))
    g2 = a["rwkv_g2_2"][0]
    units += [g2[0:P], np.concatenate([g2[P:], np.zeros((P - 32, D), g2.dtype)], axis=0)]
    at = RWKV_COLS
    part = {}
    for name, n in (("q", 1024), ("kc", 256), ("vc", 256), ("ks", 256), ("vs", 256), ("kw", 256), ("vw", 256),
                    ("g", 48), ("m0", 1024), ("m1", 1024)):
        part[name] = w2[:, at:at + n]
        at += n
    for gw, bw in zip(tiled(part["m0"]), tiled(a["w_branch_rwkv_2"][0])):
        units += [gw, bw]
    units += tiled(part["q"]) + tiled(part["kc"]) + tiled(part["vc"])
    for s in "kv":
        w1 = a[f"cmp_w1_{s}_2"][0].reshape(8, 4, HD, 256).transpose(0, 2, 1, 3).reshape(8, HD, 1024)
        units += [np.concatenate([u, u], axis=0) for u in w1]
    ck = a["cmp_w2_k_2"][0].reshape(2, P, HD)
    ck = np.concatenate([ck, ck], axis=2).transpose(1, 0, 2).reshape(P, 256)
    cv = a["cmp_w2_v_2"][0].reshape(2, P, HD).transpose(1, 0, 2).reshape(P, 128)
    units.append(np.concatenate([ck, cv], axis=1))
    units += tiled(part["ks"]) + tiled(part["kw"]) + tiled(part["vs"]) + tiled(part["vw"]) + tiled(part["g"], 48)
    for gw, bw in zip(tiled(part["m1"]), tiled(a["w_branch_nsa_2"][0])):
        units += [gw, bw]
    units += tiled(a["w_mix_out_2"][0])
    wkv = a["ca_wkv_2"][0]
    units += tiled(wkv[:, 0:1024]) + tiled(wkv[:, 1024:2048]) + tiled(a["ca_wq_2"][0]) + tiled(a["ca_wo_2"][0])
    up = a["ffn_up_2"][0]
    for gw, bw in zip(tiled(up[:, 0:D_FF2]), tiled(up[:, D_FF2:])):
        units += [gw, bw]
    for t in tiled(a["ffn_down_2"][0]):
        units += cut_units(t, (8, 8, 6))
    return units


def vectors(a):
    def cols(v):
        v = np.asarray(v).reshape(-1)
        pad = (-len(v)) % P
        return np.concatenate([v, np.zeros(pad, v.dtype)]).reshape(-1, P).T

    def twice(v):
        return np.concatenate([v, v], axis=-1)

    parts = {
        "norm_mix": a["norm_mix"], "norm_mlp": a["norm_mlp"], "norm_final": a["norm_final"],
        "pool_scale": a["pool_scale"], "norm_mix_2": a["norm_mix_2"], "mu": a["rwkv_mu_2"], "w0": a["rwkv_w0_2"],
        "a0": a["rwkv_a0_2"], "k_k": a["rwkv_kk_2"], "k_a": a["rwkv_ka_2"], "r_k": a["rwkv_rk_2"],
        "lnx_w": a["rwkv_lnx_w_2"], "lnx_b": a["rwkv_lnx_b_2"], "norm_cross": a["norm_cross_2"],
        "norm_mem": a["norm_mem_2"], "norm_ffn": a["norm_ffn_2"], "conv": a["ffn_conv_2"], "conv_b": a["ffn_conv_b_2"],
        "ca_q_gain": a["ca_q_gain_2"], "ca_k_gain": a["ca_k_gain_2"], "q_gain": twice(a["nsa_q_gain_2"][0]),
        "k_gain": twice(a["nsa_k_gain_2"][0]), "pe_k": twice(a["cmp_pe_k_2"][0]), "pe_v": twice(a["cmp_pe_v_2"][0]),
    }
    return np.concatenate([cols(parts[n]) for n in VECS], axis=1)


def feature_tiles(x):
    return x.T.reshape(-1, P, x.shape[0]).transpose(1, 0, 2)


def kernel(**inputs):
    import concourse.bacc as bacc
    from concourse.bass_utils import run_bass_kernel_spmd

    a = {name: np.asarray(v) for name, v in inputs.items()}
    units = stream(a)
    w = np.zeros((len(units), P, UNIT), a["w_in"].dtype)
    for g, u in enumerate(units):
        w[g, :, 0:u.shape[1]] = u
    rel = a["rel_bias_2"]
    arrays = {
        "x_t": feature_tiles(a["x"][0]), "consts": constants(), "vectors": vectors(a), "weights": w,
        "rel_bias": rel, "rel_last": np.repeat(rel[BUCKETS - 1:], BUCKETS, axis=0), "mem_t": feature_tiles(a["mem_2"][0]),
    }
    arrays = {n: np.ascontiguousarray(v) for n, v in arrays.items()}
    nc = bacc.Bacc("TRN2", target_bir_lowering=False, num_devices=1)
    args = [nc.dram_tensor(n, v.shape, F32, kind="ExternalInput").ap() for n, v in arrays.items()]
    out = nc.dram_tensor("out_t", (P, DT_, S), F32, kind="ExternalOutput").ap()
    sizes = build(nc, *args, out)
    assert sizes == [u.shape[1] for u in units]
    r = run_bass_kernel_spmd(nc, [arrays], core_ids=[0])
    return r.results[0]["out_t"].transpose(1, 0, 2).reshape(D, S).T.reshape(1, S, D)
```

```python
from contextlib import ExitStack

import concourse.bass as bass
import numpy as np
from concourse import mybir

F32 = mybir.dt.float32
F32R = mybir.dt.float32r
ACT = mybir.ActivationFunctionType
ALU = mybir.AluOpType
AX = mybir.AxisListType

P = 128
S = 512
D = 1024
DT_ = D // P
NT = S // P
HD = 64
H1 = 8
D_FF = 4096
N_MEM = 256
RH = 16
CH = 64
NCH = S // CH
NKV = 4
HQ = 16
NCMP = (S - 32) // 16 + 1
D_FF2 = 2816
FT2 = D_FF2 // P
RWKV_COLS = 3360
EPS = 1e-6
LNX_EPS = 64e-5
NEG = -1e30
DECAY = float(np.exp(np.float32(-0.5)))
RING = 4
SPLIT = 2
NA, NX = 3, 5
UNIT = 1024
BUCKETS = 32
OH_OFF = 511


def bucket_of(dist):
    n = np.maximum(dist, 0)
    nf = np.maximum(n, 1).astype(np.float32)
    large = 16 + (np.log(nf / 16) / np.log(128 / 16) * 16).astype(np.int32)
    return np.where(n < 16, n, np.minimum(large, 31))


CONST = {}


def constants():
    p = np.arange(P)[:, None]
    c = np.arange(P)[None, :]
    t = np.arange(CH)[None, :]
    q = p % CH
    parts = {
        "ident": (p == c),
        "ones": np.full((P, P), 1.0 / D),
        "ones256": np.full((P, P), 1.0 / 256),
        "head_mean": (p // HD == c // HD) / HD,
        "head_sum": (p // HD == c // HD),
        "ident64": (q == t),
        "diag16": (q // 16 == t // 16) & (q > t),
        "off16": (q // 32 == t // 32) & (q // 16 > t // 16),
        "off32": (q // 32 > t // 32),
        "diag16T": (q // 16 == t // 16) & (q < t),
        "after": (q < t),
        "from": (q <= t),
        "restart": np.broadcast_to((np.arange(S) % CH != 0)[None], (P, S)),
    }
    w = np.arange(S)[None, :]
    neg_dist = (w - p - (S - P)).astype(np.float64)
    parts["neg_dist"] = np.where(neg_dist > 0, NEG, neg_dist)
    cnt = np.stack([1.0 / np.minimum(np.arange(16) + 1, 2 << g) for g in range(4)]).reshape(1, -1)
    parts["inv_count"] = np.broadcast_to(cnt, (P, 64))
    at = 0
    for name, a in parts.items():
        CONST[name] = (at, a.shape[1])
        at += a.shape[1]
    return np.concatenate([np.asarray(a, np.float32) for a in parts.values()], axis=1)


N_CONST = constants().shape[1]


def one_hot():
    dist = np.arange(1024) - OH_OFF
    hot = np.zeros((BUCKETS + 1, 1024), np.float32)
    hot[:BUCKETS] = (bucket_of(dist)[None] == np.arange(BUCKETS)[:, None]) & (dist >= 0)[None]
    hot[BUCKETS] = dist < 0
    return hot


VECS = {}


def vec_columns():
    at = 0
    for name, n in (("norm_mix", 8), ("norm_mlp", 8), ("norm_final", 8), ("pool_scale", 4), ("norm_mix_2", 8),
                    ("mu", 27), ("w0", 8), ("a0", 8), ("k_k", 8), ("k_a", 8), ("r_k", 8), ("lnx_w", 8), ("lnx_b", 8),
                    ("norm_cross", 8), ("norm_mem", 8), ("norm_ffn", 8), ("conv", 3 * FT2), ("conv_b", FT2),
                    ("ca_q_gain", 2), ("ca_k_gain", 2), ("q_gain", 1), ("k_gain", 3), ("pe_k", 32), ("pe_v", 32)):
        VECS[name] = at
        at += n
    return at


N_VEC = vec_columns()


class Core:

    def __init__(self, nc, ctx):
        self.nc, self.ctx = nc, ctx
        self.units = []
        self.split = []
        self.n_used = 0
        self.n_acc = 0
        self.n_aux = 0
        self.count = {}
        self.stages = []

    def sb(self, name, shape):
        return self.ctx.enter_context(self.nc.sbuf_tensor(name, shape, F32))

    def sem(self, name):
        return self.ctx.enter_context(self.nc.semaphore(name))

    def take_acc(self, n=1):
        a = self.n_acc
        self.n_acc += n
        return a

    def take_aux(self, n=1):
        a = self.n_aux
        self.n_aux += n
        return a

    def take_unit(self, acc, n=UNIT):
        self.units.append((len(self.units), n, acc, None))
        return len(self.units) - 1

    def take_split(self, acc, n=UNIT, last=True):
        self.units.append((len(self.units), n, acc, len(self.split)))
        self.n_used += 0 if last else 1
        self.split.append((len(self.units) - 1, acc, last, self.n_used))
        return len(self.split) - 1

    def reserve(self, name, n):
        a = self.count.get(name, 0)
        self.count[name] = a + n
        return a

    def set_up(self):
        sem = self.sem
        self.acc_full = sem("acc_full")
        self.acc_drained = [sem(f"acc_drained{b}") for b in range(NA)]
        self.aux_full = sem("aux_full")
        self.aux_drained = [sem(f"aux_drained{b}") for b in range(NX)]
        self.w_loaded = [sem(f"w_loaded{i}") for i in range(RING)]
        self.w_hi_ready = sem("w_hi_ready")
        self.w_lo_ready = sem("w_lo_ready")
        self.split_used = sem("split_used")
        self.const_loaded = sem("const_loaded")
        self.vec_loaded = sem("vec_loaded")
        self.x_loaded = sem("x_loaded")
        self.x_updated = sem("x_updated")
        self.square_ready = sem("square_ready")
        self.square_used = sem("square_used")
        self.root_ready = sem("root_ready")
        self.xn_ready = sem("xn_ready")
        self.merged_ready = sem("merged_ready")
        self.act_step = sem("act_step")
        self.dve_step = sem("dve_step")
        self.pool_step = sem("pool_step")
        self.steps = {"act": 0, "dve": 0, "pool": 0}

    def after_act(self, act, ins):
        self.steps["act"] += 1
        ins.then_inc(self.act_step, 1)
        act.wait_ge(self.act_step, self.steps["act"])

    def after_dve(self, dve, ins):
        self.steps["dve"] += 1
        ins.then_inc(self.dve_step, 1)
        dve.wait_ge(self.dve_step, self.steps["dve"])

    def after_pool(self, pool, ins):
        self.steps["pool"] += 1
        ins.then_inc(self.pool_step, 1)
        pool.wait_ge(self.pool_step, self.steps["pool"])

    def acc(self, t):
        return self.ps[:, t % NA, :]

    def aux(self, t):
        return self.ps[:, NA + t % NX, :]

    def wait_acc_full(self, eng, t):
        eng.wait_ge(self.acc_full, t + 1)

    def wait_acc_drained(self, eng, t):
        eng.wait_ge(self.acc_drained[t % NA], t // NA + 1)

    def open_acc(self, pe, t):
        if t >= NA:
            self.wait_acc_drained(pe, t - NA)

    def wait_aux_full(self, eng, t):
        eng.wait_ge(self.aux_full, t + 1)

    def wait_aux_drained(self, eng, t):
        eng.wait_ge(self.aux_drained[t % NX], t // NX + 1)

    def open_aux(self, pe, t):
        if t >= NX:
            self.wait_aux_drained(pe, t - NX)

    def weights(self, pe, g):
        pe.wait_ge(self.w_loaded[g % RING], 16 * (g // RING + 1))
        return self.wring[:, g % RING, :]

    def wait_split_used(self, eng, m):
        _, acc, last, used = self.split[m]
        if last:
            self.wait_acc_full(eng, acc)
        else:
            eng.wait_ge(self.split_used, used)

    def convert_hi(self, act, m):
        g = self.split[m][0]
        n = self.units[g][1]
        act.wait_ge(self.w_loaded[g % RING], 16 * (g // RING + 1))
        if m >= SPLIT:
            self.wait_split_used(act, m - SPLIT)
        act.activation(self.w_hi[:, m % SPLIT, 0:n], self.wring[:, g % RING, 0:n], ACT.Copy).then_inc(self.w_hi_ready, 1)

    def convert_lo(self, dve, m):
        g = self.split[m][0]
        n = self.units[g][1]
        dve.wait_ge(self.w_hi_ready, m + 1)
        dve.tensor_tensor(self.w_lo[:, m % SPLIT, 0:n], self.wring[:, g % RING, 0:n],
                          self.w_hi[:, m % SPLIT, 0:n].bitcast(F32), ALU.subtract).then_inc(self.w_lo_ready, 1)

    def split_product(self, pe, out, units, src, wait=False, m=P):
        at = 0
        for u in units:
            g, _, last, _ = self.split[u]
            kc = self.units[g][1] // m
            hi, lo = (w[:, u % SPLIT, 0:kc * m].rearrange("p (c m) -> p c m", m=m) for w in (self.w_hi, self.w_lo))
            pe.wait_ge(self.w_lo_ready, u + 1)
            for c in range(kc):
                if wait:
                    src.wait_hi(pe, at + c)
                pe.matmul(out, hi[:, c, :], src.hi[:, at + c, :], start=(at + c == 0), stop=False)
                pe.matmul(out, lo[:, c, :], src.hi[:, at + c, :], start=False, stop=False)
            for c in range(kc):
                if wait:
                    src.wait_lo(pe, at + c)
                mm = pe.matmul(out, hi[:, c, :], src.lo[:, at + c, :], start=False, stop=(last and c == kc - 1))
            mm.then_inc(self.acc_full if last else self.split_used, 1)
            at += kc

    def vec(self, name, i=0, lo=0, hi=P):
        c = VECS[name] + i
        return self.vecs[lo:hi, c:c + 1]

    def const(self, name, lo=0, hi=P):
        at, n = CONST[name]
        return self.consts[lo:hi, at:at + n]


def row(ap):
    return ap.rearrange("p a b -> p (a b)")


class Stage:
    def __init__(self, k):
        self.k = k
        k.stages.append(self)

    def sync(self, sp):
        pass

    def tensor(self, pe):
        pass

    def vector(self, dve):
        pass

    def scalar(self, act):
        pass

    def gpsimd(self, pool):
        pass


class InverseRoot:

    def __init__(self, k, t, n, eps, floor=False):
        self.k, self.t, self.n, self.eps, self.floor = k, t, n, eps, floor
        self.at = k.reserve("root", 1)

    def take_mean(self, dve):
        k = self.k
        k.wait_acc_full(dve, self.t)
        op = ALU.max if self.floor else ALU.add
        dve.tensor_scalar(k.root_in[:, 0:self.n], k.acc(self.t)[:, 0:self.n], self.eps, None, op).then_inc(
            k.acc_drained[self.t % NA], 1)

    def guess(self, act):
        k, n = self.k, self.n
        k.wait_acc_drained(act, self.t)
        k.after_act(act, act.activation(k.root_ln[:, 0:n], k.root_in[:, 0:n], ACT.Ln))
        act.activation(k.root_y[:, 0:n], k.root_ln[:, 0:n], ACT.Exp, scale=-0.5).then_inc(k.root_ready, 1)

    def refine(self, dve):
        k, n = self.k, self.n
        y, r, m = k.root_y[:, 0:n], k.root[:, 0:n], k.root_in[:, 0:n]
        dve.wait_ge(k.root_ready, self.at + 1)
        k.after_dve(dve, dve.tensor_tensor(r, y, y, ALU.mult))
        k.after_dve(dve, dve.scalar_tensor_tensor(r, r, -0.5, m, ALU.mult, ALU.mult))
        k.after_dve(dve, dve.scalar_tensor_tensor(r, r, 1.5, y, ALU.add, ALU.mult))
        return r


class Norm(Stage):

    def __init__(self, k, src, dst, gain, wait_src, n=S):
        super().__init__(k)
        self.src, self.dst, self.gain, self.wait_src, self.n = src, dst, gain, wait_src, n
        self.t = k.take_acc()
        self.root = InverseRoot(k, self.t, n, EPS)
        self.sq0 = k.reserve("square", DT_)
        self.used0 = k.reserve("used", DT_ - 1)
        self.ready0 = k.reserve("xn", DT_)

    def wait_dst(self, pe, j):
        pe.wait_ge(self.k.xn_ready, self.ready0 + j + 1)

    def scalar(self, act):
        k = self.k
        for j in range(DT_):
            self.wait_src(act, j)
            if j >= 2:
                act.wait_ge(k.square_used, self.used0 + j - 1)
            act.activation(k.square[:, j % 2, 0:self.n], self.src[:, j, :], ACT.Square).then_inc(k.square_ready, 1)
        self.root.guess(act)

    def tensor(self, pe):
        k = self.k
        pe.wait_ge(k.const_loaded, 16)
        k.open_acc(pe, self.t)
        for j in range(DT_):
            pe.wait_ge(k.square_ready, self.sq0 + j + 1)
            mm = pe.matmul(k.acc(self.t)[:, 0:self.n], k.const("ones"), k.square[:, j % 2, 0:self.n],
                           start=(j == 0), stop=(j == DT_ - 1))
            mm.then_inc(k.square_used if j < DT_ - 1 else k.acc_full, 1)

    def vector(self, dve):
        k = self.k
        self.root.take_mean(dve)
        dve.wait_ge(k.vec_loaded, 16)
        r = self.root.refine(dve)
        for j in range(DT_):
            dve.scalar_tensor_tensor(self.dst[:, j, :], self.src[:, j, :], k.vec(self.gain, j), r,
                                     ALU.mult, ALU.mult).then_inc(k.xn_ready, 1)


class Project(Stage):

    def __init__(self, k, outs, src, wait_src, drains, groups=(8,), kind="features", m=P, n=S):
        super().__init__(k)
        self.src, self.wait_src, self.drains, self.groups, self.kind, self.m, self.n = (
            src, wait_src, drains, groups, kind, m, n)
        self.outs = outs
        self.ts, self.us = [], []
        for _ in range(outs):
            t = k.take_acc()
            self.ts.append(t)
            self.us.append([k.take_unit(t, kc * m) for kc in groups])

    def tensor(self, pe):
        k = self.k
        total = sum(self.groups)
        for i, (t, units) in enumerate(zip(self.ts, self.us)):
            k.open_acc(pe, t)
            at = 0
            views = []
            for g, kc in zip(units, self.groups):
                w = k.weights(pe, g)[:, 0:kc * self.m].rearrange("p (c m) -> p c m", m=self.m)
                if self.kind == "features":
                    for c in range(kc):
                        if i == 0:
                            self.wait_src(pe, at + c)
                        mm = pe.matmul(k.acc(t)[0:self.m, 0:self.n], w[:, c, :], self.src(at + c),
                                       start=(at + c == 0), stop=(at + c == total - 1))
                else:
                    views.append(w)
                at += kc
            if self.kind == "tokens":
                w = views[0]
                if i == 0:
                    self.wait_src(pe, total - 1)
                for b in range(self.n // P):
                    for c in range(total):
                        mm = pe.matmul(k.acc(t)[:, b * self.m:(b + 1) * self.m], self.src(c)[:, b * P:(b + 1) * P],
                                       w[:, c, :], start=(c == 0), stop=(c == total - 1))
            mm.then_inc(k.acc_full, 1)

    def run(self, eng, name):
        for t, drain in zip(self.ts, self.drains):
            if name in drain:
                drain[name](eng, t)

    def vector(self, dve):
        self.run(dve, "vector")

    def scalar(self, act):
        self.run(act, "scalar")

    def gpsimd(self, pool):
        self.run(pool, "gpsimd")


class SplitTiles(Stage):

    def __init__(self, k, name, src, hi, lo, wait_src, alone=False):
        super().__init__(k)
        self.alone = alone
        self.src, self.hi, self.lo, self.wait_src = src, hi, lo, wait_src
        self.tiles = src.shape[1]
        self.hi_ready = k.sem(f"{name}_hi_ready")
        self.lo_ready = [k.sem(f"{name}_lo_even_ready"), k.sem(f"{name}_lo_odd_ready")]

    def wait_hi(self, eng, j):
        eng.wait_ge(self.hi_ready, j + 1)

    def wait_lo(self, eng, j):
        eng.wait_ge(self.lo_ready[j % 2], j // 2 + 1)

    def scalar(self, act):
        for j in range(self.tiles):
            self.wait_src(act, j)
            act.activation(self.hi[:, j, :], self.src[:, j, :], ACT.Copy).then_inc(self.hi_ready, 1)

    def rest(self, eng, j):
        self.wait_hi(eng, j)
        eng.tensor_tensor(self.lo[:, j, :], self.src[:, j, :], self.hi[:, j, :].bitcast(F32), ALU.subtract).then_inc(
            self.lo_ready[j % 2], 1)

    def gpsimd(self, pool):
        for j in range(0, self.tiles, 1 if self.alone else 2):
            self.rest(pool, j)

    def vector(self, dve):
        for j in range(1, self.tiles, 2):
            if not self.alone:
                self.rest(dve, j)


class SplitStage(Stage):

    def __init__(self, k, after):
        super().__init__(k)
        self.ts, self.us = [], []
        self.begun, self.then = after is not None, None
        if after is not None:
            after.then = self

    def take(self, n=UNIT, groups=1):
        t = self.k.take_acc()
        self.ts.append(t)
        sizes = [n] if groups == 1 else [kc * P for kc in groups]
        self.us.append([self.k.take_split(t, size, last=(i == len(sizes) - 1)) for i, size in enumerate(sizes)])
        return t

    def tensor(self, pe):
        pass

    def convert_first(self, eng, convert):
        if not self.begun:
            for u in self.us[0]:
                convert(eng, u)

    def convert_next(self, eng, convert, i):
        for u in self.us[i + 1] if i + 1 < len(self.us) else self.then.us[0] if self.then else []:
            convert(eng, u)


class Begin(SplitStage):

    def __init__(self, k):
        super().__init__(k, None)

    def vector(self, dve):
        self.convert_next(dve, self.k.convert_lo, -1)

    def scalar(self, act):
        self.convert_next(act, self.k.convert_hi, -1)


class SplitProject(SplitStage):

    def __init__(self, k, outs, src, drains, groups=1, wait=True, after=None):
        super().__init__(k, after)
        self.src, self.drains, self.wait = src, drains, wait
        for _ in range(outs):
            self.take(groups=groups)

    def tensor(self, pe):
        k = self.k
        for i, t in enumerate(self.ts):
            k.open_acc(pe, t)
            k.split_product(pe, k.acc(t), self.us[i], self.src, self.wait and i == 0)

    def run(self, eng, name, convert):
        self.convert_first(eng, convert)
        for i, t in enumerate(self.ts):
            self.convert_next(eng, convert, i)
            if name in self.drains[i]:
                self.drains[i][name](eng, t)

    def vector(self, dve):
        self.run(dve, "vector", self.k.convert_lo)

    def scalar(self, act):
        self.run(act, "scalar", self.k.convert_hi)


def copy_out(k, dst, scale=1.0, m=P, n=S):
    def scalar(act, t):
        k.wait_acc_full(act, t)
        act.activation(dst, k.acc(t)[0:m, 0:n], ACT.Copy, scale=scale).then_inc(k.acc_drained[t % NA], 1)
    return {"scalar": scalar}


def copy_tokens(k, dst, m, blocks=NT):
    def scalar(act, t):
        k.wait_acc_full(act, t)
        src = k.acc(t)[:, 0:blocks * m].rearrange("p (b m) -> p b m", m=m)
        act.activation(dst, src, ACT.Copy).then_inc(k.acc_drained[t % NA], 1)
    return {"scalar": scalar}


def scale_out(k, dst, gain):
    def scalar(act, t):
        k.wait_acc_full(act, t)
        act.activation(dst, k.acc(t), ACT.Copy, scale=gain).then_inc(k.acc_drained[t % NA], 1)
    return {"scalar": scalar}


def add_residual(k, x):
    def vector(dve, t):
        k.wait_acc_full(dve, t)
        dve.tensor_tensor(x, x, k.acc(t), ALU.add).then_inc(k.acc_drained[t % NA], 1)
    return {"vector": vector}


class Hidden:

    def __init__(self, k, hi, lo, tmp):
        self.k, self.hi, self.lo, self.tmp = k, hi, lo, tmp
        self.relu_ready = k.sem("mlp_relu_ready")
        self.hi_ready = k.sem("mlp_hi_ready")
        self.squared = k.sem("mlp_squared")
        self.lo_ready = k.sem("mlp_lo_ready")

    def drain(self, n):
        k = self.k
        relu, square = self.tmp[:, n % 2, :], self.tmp[:, 2 + n % 2, :]
        hi, lo = self.hi[n // 8 % 2][:, n % 8, :], self.lo[n // 8 % 2][:, n % 8, :]

        def scalar(act, t):
            k.wait_acc_full(act, t)
            if n >= 2:
                act.wait_ge(self.lo_ready, n - 1)
            act.activation(relu, k.acc(t), ACT.Relu).then_inc(k.acc_drained[t % NA], 1)
            k.wait_acc_drained(act, t)
            act.activation(hi, relu, ACT.Square).then_inc(self.hi_ready, 1)

        def vector(dve, t):
            k.wait_acc_drained(dve, t)
            dve.tensor_tensor(square, relu, relu, ALU.mult).then_inc(self.squared, 1)
            dve.wait_ge(self.squared, n + 1)
            dve.wait_ge(self.hi_ready, n + 1)
            dve.tensor_tensor(lo, square, hi.bitcast(F32), ALU.subtract).then_inc(self.lo_ready, 1)
        return {"scalar": scalar, "vector": vector}

    def group(self, g):
        return HiddenGroup(self, g)


class HiddenGroup:

    def __init__(self, hidden, g):
        self.hidden, self.first = hidden, 8 * g
        self.hi, self.lo = hidden.hi[g % 2], hidden.lo[g % 2]
        self.drains = [hidden.drain(8 * g + i) for i in range(8)]

    def wait_hi(self, eng, j):
        eng.wait_ge(self.hidden.hi_ready, self.first + j + 1)

    def wait_lo(self, eng, j):
        eng.wait_ge(self.hidden.lo_ready, self.first + j + 1)


class Load(Stage):

    def __init__(self, k, x, consts, vecs, weights):
        super().__init__(k)
        self.x, self.consts, self.vecs, self.w = x, consts, vecs, weights

    def sync(self, sp):
        k = self.k
        sp.dma_start(k.x[:, :, :], self.x).then_inc(k.x_loaded, 16)
        sp.dma_start(k.consts[:, :], self.consts).then_inc(k.const_loaded, 16)
        sp.dma_start(k.vecs[:, :], self.vecs).then_inc(k.vec_loaded, 16)
        for g, n, _, _ in k.units:
            if g >= RING:
                _, _, acc, split = k.units[g - RING]
                if split is None:
                    k.wait_acc_full(sp, acc)
                else:
                    sp.wait_ge(k.w_lo_ready, split + 1)
            sp.dma_start(k.wring[:, g % RING, 0:n], self.w[g, :, 0:n]).then_inc(k.w_loaded[g % RING], 16)


class Pool(Stage):

    def __init__(self, k, u, sums, mixed, cat, u_ts):
        super().__init__(k)
        self.u, self.sums, self.mixed, self.cat, self.u_ts = u, sums, mixed, cat, u_ts
        self.ts = [k.take_acc() for _ in range(4)]
        self.g = k.take_unit(self.ts[-1], 4 * P)
        self.mixed_ready = k.sem("pool_mixed_ready")

    def gpsimd(self, pool):
        k, u, s = self.k, self.u, self.sums
        pool.memset(s[:, :, 0:16], 0.0)
        k.after_pool(pool, pool.memset(u[:, :, 0:16], 0.0))
        for g in range(4):
            k.wait_acc_drained(pool, self.u_ts[g])
            src = u[:, g, :]
            for r in range(g + 1):
                sh = 1 << r
                dst = s[:, r % 2, :]
                k.after_pool(pool, pool.tensor_tensor(dst[:, 16:], src[:, 16:], src[:, 16 - sh:16 + S - sh], ALU.add))
                src = dst
            w = 2 << g
            mean = s[:, (g + 1) % 2, :]
            k.after_pool(pool, pool.tensor_scalar(mean[:, 16:], src[:, 16:], 1.0 / w, None, ALU.mult))
            if g == 0:
                pool.wait_ge(k.const_loaded, 16)
            inv = k.const("inv_count")[:, 16 * g:16 * g + 16]
            k.after_pool(pool, pool.tensor_tensor(mean[:, 16:32], src[:, 16:32], inv, ALU.mult))
            pool.tensor_tensor(self.mixed[:, g, :], mean[:, 16:], u[:, g, 16:], ALU.subtract).then_inc(
                self.mixed_ready, 1)
            pool.wait_ge(self.mixed_ready, g + 1)

    def tensor(self, pe):
        k = self.k
        w = k.weights(pe, self.g)
        for g, t in enumerate(self.ts):
            pe.wait_ge(self.mixed_ready, g + 1)
            k.open_acc(pe, t)
            pe.matmul(k.acc(t), w[:, g * P:(g + 1) * P], self.mixed[:, g, :], start=True, stop=True).then_inc(
                k.acc_full, 1)

    def scalar(self, act):
        k = self.k
        act.wait_ge(k.vec_loaded, 16)
        for g, t in enumerate(self.ts):
            k.wait_acc_full(act, t)
            act.activation(self.cat[:, 4 + g, :], k.acc(t), ACT.Copy, scale=k.vec("pool_scale", g)).then_inc(
                k.acc_drained[t % NA], 1)


class Head:

    def __init__(self, q, keys, values, table, lo, gate=None, compressed=None, last=True, ready=()):
        self.q, self.keys, self.values, self.table, self.lo = q, keys, values, table, lo
        self.gate, self.compressed, self.last, self.ready = gate, compressed, last, ready


TRI = [0, 128, 384, 768]
TRI_N = 1280
COL = [0, 512, 896, 1152]


class Attention(Stage):

    def __init__(self, k, name, heads, dst, buf):
        super().__init__(k)
        self.heads, self.dst, self.b = heads, dst, buf
        self.aux0 = k.n_aux
        sem = lambda s: k.sem(f"{name}_{s}")
        self.s_full = sem("scores_full")
        self.s_drained = sem("scores_drained")
        self.max_ready = sem("max_ready")
        self.p_ready = sem("probs_ready")
        self.scaled = sem("probs_scaled")
        self.t_full = sem("probs_t_full")
        self.t_drained = sem("probs_t_drained")
        self.pv_done = sem("values_done")
        self.t_at, self.pair, self.pv_at = [], [], []
        t = v = 0
        fresh = True
        for h in heads:
            self.t_at.append(t)
            t += 3 if h.compressed is None else 4
            if fresh and h.lo == 0:
                acc = k.take_acc()
            h.first = fresh
            fresh = h.last
            self.pair.append(acc)
            h.closes = h.last and h.lo == HD
            self.pv_at.append(v)
            v += 0 if h.closes else 1

    def wait_values_done(self, eng, u):
        if self.heads[u].closes:
            self.k.wait_acc_full(eng, self.pair[u])
        else:
            eng.wait_ge(self.pv_done, self.pv_at[u] + 1)

    def scores(self, pe, u):
        k, h = self.k, self.heads[u]
        for wait in h.ready:
            wait(pe)
        for i in range(NT):
            s = NT * u + i
            n = P * (i + 1)
            if s >= 3:
                pe.wait_ge(self.s_drained, s - 2)
            pe.matmul(k.ps[:, 3 + s % 3, 0:n], h.q[:, i * P:(i + 1) * P], h.keys[:, 0:n],
                      start=True, stop=True).then_inc(self.s_full, 1)

    def open_t(self, pe, t):
        if t >= 2:
            pe.wait_ge(self.t_drained, t - 1)
        return self.k.ps[:, 6 + t % 2, :]

    def compressed_t(self, pe, u):
        k, h = self.k, self.heads[u]
        out = self.open_t(pe, self.t_at[u])
        for i in range(NT):
            mm = pe.transpose(out[0:NCMP, i * P:(i + 1) * P], h.compressed[0][:, i * NCMP:(i + 1) * NCMP],
                              k.const("ident"))
        mm.then_inc(self.t_full, 1)

    def probs_t(self, pe, u):
        h = self.heads[u]
        pe.wait_ge(self.scaled, u + 1)
        p, ident = self.b.p[:, u % 3, :], self.k.const("ident")
        for part, blocks in enumerate(((0,), (1,), (2, 3))):
            out = self.open_t(pe, self.t_at[u] + (h.compressed is not None) + part)
            for j in blocks:
                for i in range(j, NT):
                    at = COL[j] - COL[blocks[0]] + (i - j) * P
                    mm = pe.transpose(out[:, at:at + P], p[:, TRI[i] + j * P:TRI[i] + (j + 1) * P], ident)
            mm.then_inc(self.t_full, 1)

    def values(self, pe, u):
        k, h = self.k, self.heads[u]
        acc = self.pair[u]
        if h.first and h.lo == 0:
            k.open_acc(pe, acc)
        out = k.acc(acc)[h.lo:h.lo + HD, :]
        pt = self.b.pt[:, u % 2, :]
        t = self.t_at[u]
        if h.compressed is not None:
            pe.wait_ge(self.t_drained, t + 1)
            pe.matmul(out, h.compressed[1], self.b.ct[:, 0:S], start=True, stop=False)
            t += 1
        for j in range(NT):
            if j < 3:
                pe.wait_ge(self.t_drained, t + j + 1)
            mm = pe.matmul(out[:, j * P:S], h.values(j), pt[:, COL[j]:COL[j] + S - j * P],
                           start=(h.first and h.compressed is None and j == 0), stop=(h.last and j == NT - 1))
        mm.then_inc(k.acc_full if h.closes else self.pv_done, 1)

    def tensor(self, pe):
        n = len(self.heads)
        for t in range(max(0, self.aux0 - NX), self.aux0):
            self.k.wait_aux_drained(pe, t)
        self.scores(pe, 0)
        self.scores(pe, 1)
        for u in range(n):
            if u + 2 < n:
                self.scores(pe, u + 2)
            if u >= 1:
                self.values(pe, u - 1)
            if self.heads[u].compressed is not None:
                self.compressed_t(pe, u)
            self.probs_t(pe, u)
        self.values(pe, n - 1)

    def add_bias(self, dve, u):
        k, h = self.k, self.heads[u]
        p, mx = self.b.p[:, u % 3, :], self.b.max[:, u % 3, :]
        if u >= 3:
            dve.wait_ge(self.t_full, self.t_at[u - 2])
        for i in range(NT):
            s = NT * u + i
            n = P * (i + 1)
            dve.wait_ge(self.s_full, s + 1)
            dve.tensor_tensor_reduce(p[:, TRI[i]:TRI[i] + n], k.ps[:, 3 + s % 3, 0:n], h.table[:, S - n:S],
                                     1.0, -3e38, ALU.add, ALU.max, mx[:, i:i + 1]).then_inc(self.s_drained, 1)
        dve.wait_ge(self.s_drained, NT * (u + 1))
        dve.tensor_scalar(self.b.negmax[:, u % 3, :], mx, -1.0, None, ALU.mult).then_inc(self.max_ready, 1)

    def scale(self, dve, u):
        k, h = self.k, self.heads[u]
        dve.wait_ge(self.p_ready, u + 1)
        inv = self.b.inv[:, u % 3, :]
        k.after_dve(dve, dve.reciprocal(inv, self.b.sum[:, u % 3, :]))
        if h.gate is not None:
            gated = self.b.inv[:, 3 + u % 3, :]
            k.after_dve(dve, dve.tensor_tensor(gated, inv, h.gate, ALU.mult))
            inv = gated
        p = self.b.p[:, u % 3, :]
        for i in range(NT):
            seg = p[:, TRI[i]:TRI[i] + P * (i + 1)]
            last = dve.tensor_scalar(seg, seg, inv[:, i:i + 1], None, ALU.mult)
        last.then_inc(self.scaled, 1)

    def drain(self, dve, u):
        k = self.k
        t = self.pair[u]
        k.wait_acc_full(dve, t)
        dve.tensor_copy(self.dst(u), k.acc(t)).then_inc(k.acc_drained[t % NA], 1)

    def vector(self, dve):
        n = len(self.heads)
        self.add_bias(dve, 0)
        self.add_bias(dve, 1)
        self.scale(dve, 0)
        for u in range(n):
            if u + 2 < n:
                self.add_bias(dve, u + 2)
            if u + 1 < n:
                self.scale(dve, u + 1)
            if u >= 2 and self.heads[u - 2].closes:
                self.drain(dve, u - 2)
        for u in (n - 2, n - 1):
            if self.heads[u].closes:
                self.drain(dve, u)

    def exps(self, act, u):
        p, nm, rs = self.b.p[:, u % 3, :], self.b.negmax[:, u % 3, :], self.b.sum[:, u % 3, :]
        act.wait_ge(self.max_ready, u + 1)
        if u >= 3:
            act.wait_ge(self.scaled, u - 2)
        for i in range(NT):
            at, n = TRI[i], P * (i + 1)
            e = act.activation(p[:, at:at + n], p[:, at:at + n], ACT.Exp, bias=nm[:, i:i + 1], accum_out=rs[:, i:i + 1])
        e.then_inc(self.p_ready, 1)

    def move_t(self, act, u, part):
        k = self.k
        c = self.heads[u].compressed is not None
        t = self.t_at[u] + c + part
        if part == 0 and u >= 2:
            self.wait_values_done(act, u - 2)
        if part == -1 and u >= 1:
            self.wait_values_done(act, u - 1)
        act.wait_ge(self.t_full, t + 1)
        if part == -1:
            src, dst = k.ps[0:NCMP, 6 + t % 2, :], self.b.ct
        else:
            at, n = ((0, 512), (512, 384), (896, 384))[part]
            src, dst = k.ps[:, 6 + t % 2, 0:n], self.b.pt[:, u % 2, at:at + n]
        act.activation(dst, src, ACT.Copy).then_inc(self.t_drained, 1)

    def scalar(self, act):
        n = len(self.heads)
        self.exps(act, 0)
        for u in range(n):
            if u + 1 < n:
                self.exps(act, u + 1)
            if self.heads[u].compressed is not None:
                self.move_t(act, u, -1)
            for part in range(3):
                self.move_t(act, u, part)


class CompressedSoftmax(Stage):

    def __init__(self, k, q, keys, table, gates, mx, wait_q, waits):
        super().__init__(k)
        self.q, self.keys, self.table, self.gates, self.mx, self.wait_q, self.waits = (
            q, keys, table, gates, mx, wait_q, waits)
        self.ts = [k.take_acc() for _ in range(4)]
        self.shifted = k.sem("compressed_shifted")
        self.p_ready = k.sem("compressed_probs")
        self.done = k.sem("compressed_scaled")

    def tensor(self, pe):
        k = self.k
        self.waits(pe)
        for half in range(2):
            banks = self.ts[2 * half:2 * half + 2]
            for t in banks:
                k.open_acc(pe, t)
            for j in range(4):
                pair = 4 * half + j
                self.wait_q(pe, pair)
                g = pair // 2
                slot = (g % 2) * 2 + g // 2
                for i in range(NT):
                    for e in range(2):
                        at = (j * NT + i) * NCMP
                        mm = pe.matmul(k.acc(banks[e])[:, at:at + NCMP],
                                       self.q[e * HD:(e + 1) * HD, pair, i * P:(i + 1) * P],
                                       self.keys[e * HD:(e + 1) * HD, slot * NCMP:(slot + 1) * NCMP],
                                       start=True, stop=True)
                        if j == 3 and i == NT - 1:
                            mm.then_inc(k.acc_full, 1)

    def vector(self, dve):
        k, n = self.k, HQ * NT
        for b, t in enumerate(self.ts):
            k.wait_acc_full(dve, t)
            x = self.table[:, 8 * (b // 2) + b % 2:8 * (b // 2) + 8:2, :]
            dve.tensor_tensor(x, x, k.acc(t)[:, 0:4 * NT * NCMP].rearrange("p (h n) -> p h n", h=4), ALU.add).then_inc(k.acc_drained[t % NA], 1)
        for t in self.ts:
            k.wait_acc_drained(dve, t)
        x = self.table.rearrange("p h (i n) -> p (h i) n", n=NCMP)
        m = self.mx[:, 0, :]
        k.after_dve(dve, dve.tensor_reduce(m, x, AX.X, ALU.max))
        k.after_dve(dve, dve.tensor_scalar(m, m, NEG * 1e-10, None, ALU.max))
        dve.tensor_tensor(x, x, m.unsqueeze(2).to_broadcast([P, n, NCMP]), ALU.subtract).then_inc(self.shifted, 1)
        dve.wait_ge(self.p_ready, 1)
        k.after_dve(dve, dve.tensor_reduce(m, x, AX.X, ALU.add))
        k.after_dve(dve, dve.tensor_scalar(m, m, 1e-30, None, ALU.max))
        inv = self.mx[:, 1, :]
        k.after_dve(dve, dve.reciprocal(inv, m))
        gate = self.gates.rearrange("p i (h b) -> p h i b", b=3)[:, :, :, 0]
        k.after_dve(dve, dve.tensor_tensor(self.mx[:, 0, :].rearrange("p (h i) -> p h i", i=NT),
                                           inv.rearrange("p (h i) -> p h i", i=NT), gate, ALU.mult))
        dve.tensor_tensor(x, x, m.unsqueeze(2).to_broadcast([P, n, NCMP]), ALU.mult).then_inc(self.done, 1)

    def scalar(self, act):
        act.wait_ge(self.shifted, 1)
        x = row(self.table)
        act.activation(x, x, ACT.Exp).then_inc(self.p_ready, 1)


class ProjectNorm(Stage):

    def __init__(self, k, outs, src, wait_src, raw, dst, gain, mean, span=1, n=S, eps=EPS):
        super().__init__(k)
        self.outs, self.src, self.wait_src, self.raw, self.dst, self.gain, self.mean, self.span, self.n = (
            outs, src, wait_src, raw, dst, gain, mean, span, n)
        self.ts, self.us, self.mt, self.roots = [], [], [], []
        for i in range(outs + 1):
            if i < outs:
                t = k.take_acc()
                self.ts.append(t)
                self.us.append(k.take_unit(t))
            if i >= 1 and i % span == 0:
                self.mt.append(k.take_acc())
                self.roots.append(InverseRoot(k, self.mt[-1], n, eps))
        self.sq0 = k.reserve("square", outs)
        self.ready0 = k.reserve("xn", outs)

    def wait_dst(self, eng, i):
        eng.wait_ge(self.k.xn_ready, self.ready0 + i + 1)

    def tensor(self, pe):
        k = self.k
        for i in range(self.outs + 1):
            if i < self.outs:
                t = self.ts[i]
                k.open_acc(pe, t)
                w = k.weights(pe, self.us[i]).rearrange("p (c m) -> p c m", m=P)
                for c in range(DT_):
                    if i == 0:
                        self.wait_src(pe, c)
                    mm = pe.matmul(k.acc(t)[:, 0:self.n], w[:, c, :], self.src(c), start=(c == 0), stop=(c == DT_ - 1))
                mm.then_inc(k.acc_full, 1)
            if i >= 1 and i % self.span == 0:
                t = self.mt[i // self.span - 1]
                k.open_acc(pe, t)
                for r in range(self.span):
                    j = i - self.span + r
                    pe.wait_ge(k.square_ready, self.sq0 + j + 1)
                    mm = pe.matmul(k.acc(t)[:, 0:self.n], k.const(self.mean), k.square[:, j % 4, 0:self.n],
                                   start=(r == 0), stop=(r == self.span - 1))
                mm.then_inc(k.acc_full, 1)

    def scalar(self, act):
        k = self.k
        for i in range(self.outs + 1):
            if i < self.outs:
                t = self.ts[i]
                k.wait_acc_full(act, t)
                act.activation(self.raw(i), k.acc(t)[:, 0:self.n], ACT.Copy)
                if i >= 4:
                    k.wait_acc_full(act, self.mt[(i - 4) // self.span])
                act.activation(k.square[:, i % 4, 0:self.n], k.acc(t)[:, 0:self.n], ACT.Square).then_inc(
                    k.square_ready, 1)
                act.wait_ge(k.square_ready, self.sq0 + i + 1)
                act.nop().then_inc(k.acc_drained[t % NA], 1)
            if i >= 1 and i % self.span == 0:
                self.roots[i // self.span - 1].guess(act)

    def vector(self, dve):
        k = self.k
        for a, root in enumerate(self.roots):
            root.take_mean(dve)
            r = root.refine(dve)
            for i in range(a * self.span, (a + 1) * self.span):
                dve.scalar_tensor_tensor(self.dst(i), self.raw(i), self.gain(i), r, ALU.mult, ALU.mult).then_inc(
                    k.xn_ready, 1)


class SplitProjectNorm(SplitStage):

    def __init__(self, k, outs, src, raw, dst, gain, mean, span=1, after=None):
        super().__init__(k, after)
        self.outs, self.src, self.raw, self.dst, self.gain, self.mean, self.span = outs, src, raw, dst, gain, mean, span
        self.mt, self.roots = [], []
        for i in range(outs + 1):
            if i < outs:
                self.take()
            if i >= 1 and i % span == 0:
                self.mt.append(k.take_acc())
                self.roots.append(InverseRoot(k, self.mt[-1], S, EPS))
        self.sq0 = k.reserve("square", outs)
        self.ready0 = k.reserve("xn", outs)

    def wait_dst(self, eng, i):
        eng.wait_ge(self.k.xn_ready, self.ready0 + i + 1)

    def tensor(self, pe):
        k = self.k
        for i in range(self.outs + 1):
            if i < self.outs:
                k.open_acc(pe, self.ts[i])
                k.split_product(pe, k.acc(self.ts[i]), self.us[i], self.src, wait=(i == 0))
            if i >= 1 and i % self.span == 0:
                t = self.mt[i // self.span - 1]
                k.open_acc(pe, t)
                for r in range(self.span):
                    j = i - self.span + r
                    pe.wait_ge(k.square_ready, self.sq0 + j + 1)
                    mm = pe.matmul(k.acc(t), k.const(self.mean), k.square[:, j % 4, :], start=(r == 0),
                                   stop=(r == self.span - 1))
                mm.then_inc(k.acc_full, 1)

    def scalar(self, act):
        k = self.k
        self.convert_first(act, k.convert_hi)
        for i in range(self.outs + 1):
            if i < self.outs:
                self.convert_next(act, k.convert_hi, i)
                t = self.ts[i]
                k.wait_acc_full(act, t)
                act.activation(self.raw(i), k.acc(t), ACT.Copy)
                if i >= 4:
                    k.wait_acc_full(act, self.mt[(i - 4) // self.span])
                act.activation(k.square[:, i % 4, :], k.acc(t), ACT.Square).then_inc(k.square_ready, 1)
                act.wait_ge(k.square_ready, self.sq0 + i + 1)
                act.nop().then_inc(k.acc_drained[t % NA], 1)
            if i >= 1 and i % self.span == 0:
                self.roots[i // self.span - 1].guess(act)

    def vector(self, dve):
        k = self.k
        self.convert_first(dve, k.convert_lo)
        for i in range(self.outs + 1):
            if i < self.outs:
                self.convert_next(dve, k.convert_lo, i)
            if i >= 1 and i % self.span == 0:
                root = self.roots[i // self.span - 1]
                root.take_mean(dve)
                r = root.refine(dve)
                for j in range(i - self.span, i):
                    dve.scalar_tensor_tensor(self.dst(j), self.raw(j), self.gain(j), r, ALU.mult, ALU.mult).then_inc(
                        k.xn_ready, 1)


class TableRows(Stage):

    def __init__(self, k, rel, rel_last, bucket, tab, hot_in, hot, rows, wait_free):
        super().__init__(k)
        self.rel, self.rel_last, self.bucket, self.tab, self.hot_in, self.hot, self.rows, self.wait_free = (
            rel, rel_last, bucket, tab, hot_in, hot, rows, wait_free)
        self.loaded = k.sem("rel_bias_loaded")
        self.loaded2 = k.sem("rel_last_loaded")
        self.hot_loaded = k.sem("one_hot_loaded")
        self.tab_ready = k.sem("bias_rows_ready")
        self.hi_ready = k.sem("bias_rows_hi_ready")
        self.ready = k.sem("table_operands_ready")

    def gpsimd(self, pool):
        self.wait_free(pool)
        pool.dma_start(self.tab[0:BUCKETS, 0, :], self.rel).then_inc(self.loaded, 16)
        pool.dma_start(self.tab[0:BUCKETS, 1, :], self.rel_last).then_inc(self.loaded2, 16)
        pool.dma_start(self.hot_in, self.bucket).then_inc(self.hot_loaded, 16)

    def vector(self, dve):
        t = self.tab
        dve.wait_ge(self.loaded, 16)
        dve.wait_ge(self.loaded2, 16)
        dve.tensor_tensor(t[0:BUCKETS, 2, :], t[0:BUCKETS, 0, :], t[0:BUCKETS, 1, :], ALU.subtract).then_inc(
            self.tab_ready, 1)
        dve.memset(t[BUCKETS:BUCKETS + 1, 2, :], NEG).then_inc(self.tab_ready, 1)
        dve.wait_ge(self.hi_ready, 1)
        dve.tensor_tensor(self.rows[:, HQ:2 * HQ], t[:, 2, :], self.rows[:, 0:HQ].bitcast(F32), ALU.subtract).then_inc(
            self.ready, 1)

    def scalar(self, act):
        act.wait_ge(self.tab_ready, 2)
        act.activation(self.rows[:, 0:HQ], self.tab[:, 2, :], ACT.Copy).then_inc(self.hi_ready, 1)
        act.wait_ge(self.hot_loaded, 16)
        act.activation(self.hot[:, :], self.hot_in, ACT.Copy).then_inc(self.ready, 1)


class Tables(Stage):

    def __init__(self, k, rows, wide, comp):
        super().__init__(k)
        self.rows, self.wide, self.comp = rows, wide, comp
        self.cleared = k.sem("wide_table_cleared")
        self.hi_moved = k.sem("table_hi_moved")
        self.banks = []
        for c0 in range(S // 2, S, 16):
            self.banks.append((wide[:, :, c0:c0 + 16], [OH_OFF + (S - P) - c for c in range(c0, c0 + 16)]))
        for i in range(NT):
            for c0, c1 in ((0, 16), (16, NCMP)):
                self.banks.append((comp[:, :, i * NCMP + c0:i * NCMP + c1],
                                   [OH_OFF - 31 + P * i - 16 * c for c in range(c0, c1)]))
        self.ts = [k.take_acc() for _ in self.banks]

    def tensor(self, pe):
        k = self.k
        pe.wait_ge(self.rows.ready, 2)
        for t, (_, starts) in zip(self.ts, self.banks):
            k.open_acc(pe, t)
            for c, x0 in enumerate(starts):
                mm = pe.matmul(k.acc(t)[:, 2 * c * HQ:2 * (c + 1) * HQ], self.rows.hot[:, x0:x0 + P],
                               self.rows.rows[:, :], start=True, stop=True)
            mm.then_inc(k.acc_full, 1)

    def vector(self, dve):
        k = self.k
        dve.memset(self.wide[:, :, 0:S // 2], 0.0).then_inc(self.cleared, 1)
        for i, (t, (dst, starts)) in enumerate(zip(self.ts, self.banks)):
            dve.wait_ge(self.hi_moved, i + 1)
            dve.tensor_tensor(dst, dst, self.part(t, starts, 1), ALU.add).then_inc(k.acc_drained[t % NA], 1)

    def scalar(self, act):
        k = self.k
        for t, (dst, starts) in zip(self.ts, self.banks):
            k.wait_acc_full(act, t)
            act.activation(dst, self.part(t, starts, 0), ACT.Copy).then_inc(self.hi_moved, 1)

    def part(self, t, starts, half):
        return self.k.acc(t)[:, 0:2 * len(starts) * HQ].rearrange("p (c s h) -> p s h c", s=2, h=HQ)[:, half]


class Compress(Stage):

    def __init__(self, k, src, swapped, raw_ready, staged, raw, tmp, hid, keys_raw, keys, values):
        super().__init__(k)
        self.src, self.swapped, self.raw_ready, self.staged = src, swapped, raw_ready, staged
        self.raw, self.tmp, self.hid = raw, tmp, hid
        self.keys_raw, self.keys, self.values = keys_raw, keys, values
        self.swap_done = [k.sem(f"halves_swapped_{n}") for n in "kv"]
        self.staged_ready = k.sem("blocks_ready")
        self.tanh_in = k.sem("gelu_inner_ready")
        self.tanh_out = k.sem("gelu_tanh_ready")
        self.hid_ready = k.sem("hidden_ready")
        self.ht, self.hu = [], []
        for _ in range(2):
            self.ht.append(k.take_acc())
            self.hu.append([k.take_unit(self.ht[-1]) for _ in range(4)])
        self.tt = [k.take_acc() for _ in range(2)]
        self.kt, self.mt, self.vt = k.take_acc(), k.take_acc(), k.take_acc()
        self.u2 = k.take_unit(self.vt, 384)
        self.root = InverseRoot(k, self.mt, 124, EPS)
        self.sq0 = k.reserve("square", 1)
        self.ready0 = k.reserve("xn", 1)

    def gpsimd(self, pool):
        for b in range(2):
            self.raw_ready(pool, b)
            for e in range(2):
                pool.dma_start(self.swapped[b][(1 - e) * HD:(2 - e) * HD], self.src[b][e * HD:(e + 1) * HD]).then_inc(
                    self.swap_done[b], 16)

    def vector(self, dve):
        k = self.k
        for b in range(2):
            self.raw_ready(dve, b)
            first = VECS[("pe_k", "pe_v")[b]]
            for swap in range(2):
                if swap:
                    dve.wait_ge(self.swap_done[b], 32)
                for parity in range(2):
                    e = parity ^ swap
                    at = slice(parity * HD, (parity + 1) * HD)
                    src = (self.src, self.swapped)[swap][b][at]
                    for tl in range(2):
                        for late in range(2):
                            i0 = src[:, tl, 16 * late:16 * late + 16 * NCMP].rearrange("p (n l) -> p l n", l=16)
                            c = first + 16 * late + parity
                            i1 = k.vecs[at, c:c + 15:2].unsqueeze(2).to_broadcast([HD, 8, NCMP])
                            slot = (2 * e + tl) * NCMP
                            dve.tensor_tensor(self.staged[b][at, 8 * late:8 * late + 8, slot:slot + NCMP],
                                              i0[:, parity::2, :], i1, ALU.add).then_inc(self.staged_ready, 1)
        for b in range(2):
            x, t = self.raw[:, b, :], self.tmp[:, b, :]
            k.wait_acc_drained(dve, self.ht[b])
            k.after_dve(dve, dve.tensor_tensor(t, x, x, ALU.mult))
            k.after_dve(dve, dve.tensor_scalar(t, t, 0.044715, 1.0, ALU.mult, ALU.add))
            dve.tensor_tensor(t, t, x, ALU.mult).then_inc(self.tanh_in, 1)
        for b in range(2):
            x, t = self.raw[:, b, :], self.tmp[:, b, :]
            dve.wait_ge(self.tanh_out, b + 1)
            k.after_dve(dve, dve.scalar_tensor_tensor(t, t, 1.0, x, ALU.add, ALU.mult))
            dve.tensor_scalar(x, t, 0.5, None, ALU.mult).then_inc(self.hid_ready, 1)
        self.root.take_mean(dve)
        r = self.root.refine(dve)
        dve.scalar_tensor_tensor(self.keys, self.keys_raw, k.vec("k_gain", 0), r, ALU.mult, ALU.mult).then_inc(
            k.xn_ready, 1)

    def scalar(self, act):
        k = self.k
        for b in range(2):
            t = self.ht[b]
            k.wait_acc_full(act, t)
            act.activation(self.raw[:, b, :], k.acc(t)[0:124, 0:256], ACT.Copy).then_inc(k.acc_drained[t % NA], 1)
        for b in range(2):
            act.wait_ge(self.tanh_in, b + 1)
            t = self.tmp[:, b, :]
            act.activation(t, t, ACT.Tanh, scale=float(np.sqrt(2 / np.pi))).then_inc(self.tanh_out, 1)
        for b, t in enumerate(self.tt):
            k.wait_acc_full(act, t)
            act.activation(self.hid[:, b, :], k.acc(t)[:, 0:248], ACT.Copy).then_inc(k.acc_drained[t % NA], 1)
        k.wait_acc_full(act, self.kt)
        act.activation(self.keys_raw, k.acc(self.kt)[:, 0:124], ACT.Copy)
        act.activation(k.square[:, 0, 0:124], k.acc(self.kt)[:, 0:124], ACT.Square).then_inc(k.square_ready, 1)
        act.wait_ge(k.square_ready, self.sq0 + 1)
        act.nop().then_inc(k.acc_drained[self.kt % NA], 1)
        self.root.guess(act)
        k.wait_acc_full(act, self.vt)
        act.activation(self.values, k.acc(self.vt)[0:NCMP, 0:256].rearrange("p (g d) -> p g d", d=HD),
                       ACT.Copy).then_inc(k.acc_drained[self.vt % NA], 1)

    def wait_done(self, eng):
        eng.wait_ge(self.k.xn_ready, self.ready0 + 1)
        self.k.wait_acc_drained(eng, self.vt)

    def tensor(self, pe):
        k = self.k
        for b, t in enumerate(self.ht):
            k.open_acc(pe, t)
            pe.wait_ge(self.staged_ready, 16 * (b + 1))
            for u in range(4):
                w = k.weights(pe, self.hu[b][u]).rearrange("p (l c) -> p l c", c=256)
                for l in range(4):
                    mm = pe.matmul(k.acc(t)[0:124, 0:256], self.staged[b][:, 4 * u + l, :], w[:, l, :],
                                   start=(u == 0 and l == 0), stop=(u == 3 and l == 3))
            mm.then_inc(k.acc_full, 1)
        for b, t in enumerate(self.tt):
            k.open_acc(pe, t)
            pe.wait_ge(self.hid_ready, b + 1)
            for ch in range(2):
                mm = pe.transpose(k.acc(t)[:, ch * 124:(ch + 1) * 124], self.raw[:, b, ch * P:(ch + 1) * P],
                                  k.const("ident")[0:124, 0:124])
            mm.then_inc(k.acc_full, 1)
        w = k.weights(pe, self.u2)
        wk = w[:, 0:256].rearrange("p (c m) -> p c m", c=2)
        wv = w[:, 256:384].rearrange("p (c m) -> p c m", c=2)
        k.wait_acc_drained(pe, self.tt[0])
        k.open_acc(pe, self.kt)
        for ch in range(2):
            mm = pe.matmul(k.acc(self.kt)[:, 0:124], wk[:, ch, :], self.hid[:, 0, ch * 124:(ch + 1) * 124],
                           start=(ch == 0), stop=(ch == 1))
        mm.then_inc(k.acc_full, 1)
        k.open_acc(pe, self.mt)
        pe.wait_ge(k.square_ready, self.sq0 + 1)
        pe.matmul(k.acc(self.mt)[:, 0:124], k.const("head_mean"), k.square[:, 0, 0:124], start=True,
                  stop=True).then_inc(k.acc_full, 1)
        k.open_acc(pe, self.vt)
        k.wait_acc_drained(pe, self.tt[1])
        for g in range(4):
            for ch in range(2):
                at = ch * 124 + g * NCMP
                mm = pe.matmul(k.acc(self.vt)[0:NCMP, g * HD:(g + 1) * HD], self.hid[:, 1, at:at + NCMP], wv[:, ch, :],
                               start=(ch == 0), stop=(ch == 1))
        mm.then_inc(k.acc_full, 1)


class Spread(Stage):

    def __init__(self, k, src, dst, waits):
        super().__init__(k)
        self.src, self.dst, self.waits = src, dst, waits
        self.done = k.sem("keys_spread")

    def gpsimd(self, pool):
        for b in range(2):
            for g in range(NKV):
                self.waits[b](pool, g // 2)
                e = g % 2
                for half in range(2):
                    pool.dma_start(self.dst[b][half * HD:(half + 1) * HD, g, :],
                                   self.src[b][e * HD:(e + 1) * HD, g // 2, :]).then_inc(self.done, 16)

    def wait_done(self, eng):
        eng.wait_ge(self.done, 16 * 16)


class Gates(Stage):

    def __init__(self, k, g, wait):
        super().__init__(k)
        self.g, self.wait = g, wait
        self.ready = k.sem("gates_ready")

    def vector(self, dve):
        self.wait(dve)
        dve.tensor_scalar(row(self.g), row(self.g), 0.5, 0.5, ALU.mult, ALU.add).then_inc(self.ready, 1)
        dve.wait_ge(self.ready, 1)


class Gated(SplitStage):

    def __init__(self, k, y, xn, merged, tanh, first, wait_merged=None, after=None):
        super().__init__(k, after)
        self.y, self.xn, self.merged, self.tanh, self.first, self.wait_merged = y, xn, merged, tanh, first, wait_merged
        for _ in range(2 * DT_):
            self.take()
        self.gt, self.bt = self.ts[0::2], self.ts[1::2]

    def tensor(self, pe):
        k = self.k
        for i, t in enumerate(self.ts):
            k.open_acc(pe, t)
            k.split_product(pe, k.acc(t), self.us[i], (self.xn, self.y)[i % 2], wait=(i < 2))

    def scalar(self, act):
        k = self.k
        self.convert_first(act, k.convert_hi)
        for m, t in enumerate(self.gt):
            self.convert_next(act, k.convert_hi, 2 * m)
            k.wait_acc_full(act, t)
            if m >= 2:
                if self.first:
                    k.wait_acc_drained(act, self.bt[m - 2])
                else:
                    act.wait_ge(k.merged_ready, m - 1)
            act.activation(self.tanh[:, m % 2, :], k.acc(t), ACT.Tanh, scale=0.5).then_inc(k.acc_drained[t % NA], 1)
            self.convert_next(act, k.convert_hi, 2 * m + 1)

    def vector(self, dve):
        k = self.k
        self.convert_first(dve, k.convert_lo)
        if self.wait_merged:
            self.wait_merged(dve)
        for m, t in enumerate(self.bt):
            self.convert_next(dve, k.convert_lo, 2 * m)
            self.convert_next(dve, k.convert_lo, 2 * m + 1)
            k.wait_acc_full(dve, t)
            k.wait_acc_drained(dve, self.gt[m])
            g = self.tanh[:, m % 2, :]
            dst = self.merged[:, m, :] if self.first else g
            ins = dve.scalar_tensor_tensor(dst, g, 1.0, k.acc(t), ALU.add, ALU.mult).then_inc(k.acc_drained[t % NA], 1)
            if not self.first:
                k.wait_acc_drained(dve, t)
                dve.tensor_tensor(self.merged[:, m, :], self.merged[:, m, :], g, ALU.add).then_inc(k.merged_ready, 1)


class RwkvInputs(SplitStage):

    ORDER = 27

    def __init__(self, k, xn, rkv, zwa, zg, shift, before, after=None):
        super().__init__(k, after)
        self.xn, self.rkv, self.zwa, self.zg, self.shift, self.before = xn, rkv, zwa, zg, shift, before
        self.m = [P] * 26 + [32]
        for m in self.m:
            self.take(DT_ * m)
        self.padded = k.sem("shift_padded")
        self.done = k.sem("shifted")
        self.zg_ready = k.sem("zg_ready")
        self.zwa_ready = k.sem("zwa_ready")

    def dst(self, i):
        if i < 24:
            return self.rkv[i // 8][:, i % 8, :]
        if i == 24:
            return self.zwa
        return self.zg[0:self.m[i], i - 25, :]

    def tensor(self, pe):
        k = self.k
        for i, m in enumerate(self.m):
            t = self.ts[i]
            k.open_acc(pe, t)
            k.split_product(pe, k.acc(t)[0:m, :], self.us[i], self.xn, wait=(i == 0), m=m)

    def scalar(self, act):
        k = self.k
        self.convert_first(act, k.convert_hi)
        act.wait_ge(self.padded, 1)
        for i, m in enumerate(self.m):
            self.convert_next(act, k.convert_hi, i)
            t = self.ts[i]
            k.wait_acc_full(act, t)
            if i >= 3:
                act.wait_ge(self.done, i - 2)
            act.activation(self.shift[0:m, i % 3, 1:1 + S], k.acc(t)[0:m, :], ACT.Copy).then_inc(
                k.acc_drained[t % NA], 1)
        act.wait_ge(self.done, 27)
        z = self.zwa[0:64, :]
        act.activation(z, z, ACT.Tanh).then_inc(self.zwa_ready, 1)
        for i in (0, 1):
            z = self.zg[0:self.m[25 + i], i, :]
            k.after_act(act, act.activation(z, z, ACT.Tanh, scale=0.5))
            act.activation(z, z, ACT.Copy, scale=0.5, bias=0.5).then_inc(self.zg_ready, 1)

    def vector(self, dve):
        k = self.k
        self.before(dve)
        dve.memset(self.shift[:, :, 0:1], 0.0).then_inc(self.padded, 1)
        self.convert_first(dve, k.convert_lo)
        for i, m in enumerate(self.m):
            self.convert_next(dve, k.convert_lo, i)
            k.wait_acc_drained(dve, self.ts[i])
            z, prev, dst = self.shift[0:m, i % 3, 1:1 + S], self.shift[0:m, i % 3, 0:S], self.dst(i)
            k.after_dve(dve, dve.tensor_tensor(dst, prev, z, ALU.subtract))
            dve.scalar_tensor_tensor(dst, dst, k.vec("mu", i, 0, m), z, ALU.mult, ALU.add).then_inc(self.done, 1)


class RwkvPrepare(Stage):

    def __init__(self, k, inp, aa, bb, end, tmp, bonus_out):
        super().__init__(k)
        self.inp, self.aa, self.bb, self.end, self.tmp, self.bonus_out = inp, aa, bb, end, tmp, bonus_out
        self.wt, self.at, self.nt, self.bt, self.roots = [], [], [], [], []
        first = k.n_acc
        self.u = None
        for p in range(8):
            self.wt.append(k.take_acc())
            self.at.append(k.take_acc())
            self.nt.append(k.take_acc())
            self.roots.append(InverseRoot(k, self.nt[-1], S, 1e-24, floor=True))
            self.bt.append(k.take_acc())
        self.u = k.take_unit(self.at[-1], 1024)
        self.sq0 = k.reserve("square", 8)
        sem = k.sem
        self.decay_ready = sem("log_decay_sum_ready")
        self.exps_ready = sem("decay_products_ready")
        self.prev_ready = sem("log_decay_before_ready")
        self.kk_ready = sem("kk_ready")
        self.rk_ready = sem("rkk_ready")
        self.bonus_ready = sem("bonus_ready")
        self.bonus_saved = [sem(f"bonus_saved{i}") for i in range(2)]
        self.done = sem("scaled_ready")

    def tensor(self, pe):
        k = self.k
        w = k.weights(pe, self.u)
        z = self.inp.zwa
        pe.wait_ge(self.inp.zwa_ready, 1)
        for p in range(8):
            k.open_acc(pe, self.wt[p])
            pe.matmul(k.acc(self.wt[p]), w[0:64, p * P:(p + 1) * P], z[0:64, :], start=True, stop=True).then_inc(
                k.acc_full, 1)
            k.open_acc(pe, self.at[p])
            pe.matmul(k.acc(self.at[p]), w[64:128, p * P:(p + 1) * P], z[64:128, :], start=True, stop=True).then_inc(
                k.acc_full, 1)
            k.open_acc(pe, self.nt[p])
            pe.wait_ge(k.square_ready, self.sq0 + p + 1)
            pe.matmul(k.acc(self.nt[p]), k.const("head_sum"), k.square[:, p % 4, :], start=True, stop=True).then_inc(
                k.acc_full, 1)
            k.open_acc(pe, self.bt[p])
            pe.wait_ge(self.rk_ready, p + 1)
            pe.matmul(k.acc(self.bt[p]), k.const("head_sum"), self.tmp["rkk"], start=True, stop=True).then_inc(
                k.acc_full, 1)

    def scalar(self, act):
        k, tm = self.k, self.tmp
        for p in range(8):
            k.wait_acc_full(act, self.wt[p])
            act.wait_ge(self.kk_ready, p + 1)
            if p:
                act.wait_ge(self.done, p)
            act.activation(tm["decay"], k.acc(self.wt[p]), ACT.Tanh, scale=0.5, bias=tm["w0h"][:, p:p + 1]).then_inc(
                k.acc_drained[self.wt[p] % NA], 1)
            k.wait_acc_full(act, self.at[p])
            act.activation(tm["a"], k.acc(self.at[p]), ACT.Tanh, scale=0.5, bias=tm["a0h"][:, p:p + 1]).then_inc(
                k.acc_drained[self.at[p] % NA], 1)
            act.activation(k.square[:, p % 4, :], tm["kk"], ACT.Square).then_inc(k.square_ready, 1)
            self.roots[p].guess(act)
            act.wait_ge(self.decay_ready, p + 1)
            act.activation(tm["p"], tm["sum"], ACT.Exp)
            act.activation(tm["inv"], tm["sum"], ACT.Exp, scale=-1.0).then_inc(self.exps_ready, 1)
            act.wait_ge(self.prev_ready, p + 1)
            act.activation(tm["before"], tm["before"], ACT.Exp).then_inc(self.exps_ready, 1)

    def gpsimd(self, pool):
        for p in range(8):
            pool.wait_ge(self.bonus_ready, p + 1)
            pool.dma_start(self.bonus_out[:, p, :], self.tmp["bonus"][:, p % 2, :]).then_inc(
                self.bonus_saved[p % 2], 16)

    def vector(self, dve):
        k, tm = self.k, self.tmp
        (r, kx, v), seq = self.inp.rkv, k.after_dve
        dve.tensor_scalar(tm["w0h"], k.vecs[:, VECS["w0"]:VECS["w0"] + 8], 0.5, None, ALU.mult)
        seq(dve, dve.tensor_scalar(tm["a0h"], k.vecs[:, VECS["a0"]:VECS["a0"] + 8], 0.5, None, ALU.mult))
        for p in range(8):
            rp, kp, vp = r[:, p, :], kx[:, p, :], v[:, p, :]
            dve.tensor_scalar(tm["kk"], kp, k.vec("k_k", p), None, ALU.mult).then_inc(self.kk_ready, 1)
            k.wait_acc_drained(dve, self.wt[p])
            seq(dve, dve.tensor_scalar(tm["decay"], tm["decay"], 1.0, -0.5 * DECAY, ALU.add, ALU.mult))
            dve.tensor_tensor_scan(tm["sum"], k.const("restart"), tm["decay"], 0.0, ALU.mult, ALU.add).then_inc(
                self.decay_ready, 1)
            dve.wait_ge(self.decay_ready, p + 1)
            dve.tensor_tensor(tm["before"], tm["sum"], tm["decay"], ALU.subtract).then_inc(self.prev_ready, 1)
            k.wait_acc_drained(dve, self.at[p])
            seq(dve, dve.tensor_scalar(tm["a"], tm["a"], 0.5, 0.5, ALU.mult, ALU.add))
            seq(dve, dve.tensor_scalar(tm["mix"], tm["a"], 1.0, k.vec("k_a", p), ALU.subtract, ALU.mult))
            seq(dve, dve.scalar_tensor_tensor(kp, tm["mix"], 1.0, kp, ALU.add, ALU.mult))
            if p:
                k.wait_acc_full(dve, self.bt[p - 1])
            dve.scalar_tensor_tensor(tm["rkk"], rp, k.vec("r_k", p), kp, ALU.mult, ALU.mult).then_inc(self.rk_ready, 1)
            dve.wait_ge(self.rk_ready, p + 1)
            self.roots[p].take_mean(dve)
            root = self.roots[p].refine(dve)
            seq(dve, dve.tensor_tensor(tm["kk"], tm["kk"], root, ALU.mult))
            seq(dve, dve.tensor_tensor(tm["a"], tm["a"], tm["kk"], ALU.mult))
            dve.wait_ge(self.exps_ready, 2 * p + 2)
            dve.tensor_tensor(self.bb[:, p, :], tm["a"], tm["inv"], ALU.mult)
            dve.scalar_tensor_tensor(self.aa[:, p, :], tm["kk"], -1.0, tm["before"], ALU.mult, ALU.mult)
            dve.tensor_tensor(rp, rp, tm["p"], ALU.mult)
            dve.tensor_copy(self.end[:, p, :], tm["p"][:, CH - 1:S:CH])
            dve.tensor_tensor(kp, kp, tm["inv"], ALU.mult).then_inc(self.done, 1)
            dve.wait_ge(self.done, p + 1)
            k.wait_acc_full(dve, self.bt[p])
            if p >= 2:
                dve.wait_ge(self.bonus_saved[p % 2], 16 * (p // 2))
            dve.tensor_tensor(tm["bonus"][:, p % 2, :], vp, k.acc(self.bt[p]), ALU.mult).then_inc(
                k.acc_drained[self.bt[p] % NA], 1)
            k.wait_acc_drained(dve, self.bt[p])
            dve.nop().then_inc(self.bonus_ready, 1)


class RwkvScan(Stage):

    STEPS = ("x", "b_ra0", "b_ra1", "an", "d2", "d2t", "bn", "d4", "d2_dm0", "d2_dm1", "d8", "m2", "kn", "m3", "vn",
             "mn", "g", "k_ra0", "k_ra1", "m4", "mn2", "g2", "m5", "q", "wt", "u", "sa", "y", "z")

    def __init__(self, k, prep, buf, ra):
        super().__init__(k)
        self.prep, self.buf, self.ra = prep, buf, ra
        self.t = [{s: k.take_aux() for s in self.STEPS} for _ in range(NCH)]
        self.state_cleared = k.sem("scan_state_cleared")
        self.state_ready = k.sem("scan_state_ready")

    def chunk(self, ap, c):
        return ap[:, :, c * CH:(c + 1) * CH]

    def tensor(self, pe):
        k, b = self.k, self.buf
        r, kx, v = self.prep.inp.rkv
        aa, bb = self.prep.aa, self.prep.bb
        ident = k.const("ident64")
        pe.wait_ge(self.prep.done, 8)
        pe.wait_ge(self.state_cleared, 1)

        def cut(ap, p, e):
            return ap[e * HD:(e + 1) * HD, p, :]

        def product(t, *terms):
            k.open_aux(pe, t)
            out = k.aux(t).rearrange("p (a b) -> p a b", b=CH)
            for p in range(8):
                for e in range(2):
                    for i, (lhs, rhs) in enumerate(terms):
                        right = ident[e * HD:(e + 1) * HD, :] if rhs is None else cut(rhs, p, e)
                        if rhs is None and e == 0:
                            mm = pe.transpose(cut(out, p, e), cut(lhs, p, e), right)
                        else:
                            mm = pe.matmul(cut(out, p, e), cut(lhs, p, e), right, start=(i == 0),
                                           stop=(i == len(terms) - 1))
            mm.then_inc(k.aux_full, 1)

        def twin(t, name, lhs, rhs):
            for half in range(2):
                bank = t[f"{name}{half}"]
                k.open_aux(pe, bank)
                out = k.aux(bank).rearrange("p (a s b) -> p a s b", s=2, b=CH)
                for p in range(4 * half, 4 * half + 4):
                    for e in range(2):
                        part = slice(e * HD, (e + 1) * HD)
                        mm = pe.matmul(out[part, p - 4 * half], lhs[part, p, :], rhs(p)[part], start=True, stop=True)
                mm.then_inc(k.aux_full, 1)

        for c in range(NCH):
            ra = lambda p, c=c: self.ra[:, :, p * S + c * CH:p * S + (c + 1) * CH]
            t = self.t[c]
            ac, bc, rc, kc, vc = (self.chunk(x, c) for x in (aa, bb, r, kx, v))
            product(t["x"], (ac, bc))
            twin(t, "b_ra", bc, ra)
            product(t["an"], (ac, None))
            k.wait_aux_drained(pe, t["x"])
            k.wait_aux_drained(pe, t["b_ra0"])
            k.wait_aux_drained(pe, t["b_ra1"])
            product(t["d2"], (b["dt"], b["d"]))
            product(t["d2t"], (b["d"], b["dt"]))
            product(t["bn"], (bc, None))
            k.wait_aux_drained(pe, t["d2"])
            k.wait_aux_drained(pe, t["d2t"])
            product(t["d4"], (b["d2t"], b["d2"]))
            twin(t, "d2_dm", b["d2"], lambda p: b["d2t_m0"][:, :, p, :])
            k.wait_aux_drained(pe, t["d4"])
            k.wait_aux_drained(pe, t["d2_dm0"])
            k.wait_aux_drained(pe, t["d2_dm1"])
            product(t["d8"], (b["d4t"], b["d4"]))
            product(t["m2"], (b["d4"], b["m1"]))
            product(t["kn"], (kc, None))
            k.wait_aux_drained(pe, t["d8"])
            k.wait_aux_drained(pe, t["m2"])
            product(t["m3"], (b["d8"], b["m0"]))
            product(t["vn"], (vc, None))
            k.wait_aux_drained(pe, t["m3"])
            product(t["mn"], (b["m1"], None))
            product(t["g"], (b["x32"], b["m1"]))
            twin(t, "k_ra", kc, ra)
            k.wait_aux_drained(pe, t["mn"])
            k.wait_aux_drained(pe, t["g"])
            product(t["m4"], (b["mn"], b["g"]))
            k.wait_aux_drained(pe, t["m4"])
            product(t["mn2"], (b["m0"], None))
            product(t["g2"], (b["x64"], b["m0"]))
            k.wait_aux_drained(pe, t["mn2"])
            k.wait_aux_drained(pe, t["g2"])
            product(t["m5"], (b["mn"], b["g"]))
            k.wait_aux_drained(pe, t["k_ra0"])
            k.wait_aux_drained(pe, t["k_ra1"])
            k.wait_aux_drained(pe, t["vn"])
            product(t["q"], (b["akt"], b["vn"]))
            k.wait_aux_drained(pe, t["an"])
            k.wait_aux_drained(pe, t["m5"])
            product(t["wt"], (b["an"], b["m1"]))
            k.wait_aux_drained(pe, t["q"])
            product(t["u"], (b["m1"], b["q"]))
            k.wait_aux_drained(pe, t["wt"])
            if c:
                pe.wait_ge(self.state_ready, c)
            product(t["sa"], (b["wt"], b["z"]))
            k.wait_aux_drained(pe, t["sa"])
            product(t["y"], (b["z"], rc), (b["sa"], b["rbt"]), (b["vn"], b["rkt"]))
            k.wait_aux_drained(pe, t["bn"])
            k.wait_aux_drained(pe, t["kn"])
            product(t["z"], (b["bn"], b["sa"]), (b["kn"], b["vn"]))

    def scalar(self, act):
        k, b = self.k, self.buf

        def copy(t, dst):
            k.wait_aux_full(act, t)
            act.activation(dst, k.aux(t).rearrange("p (a b) -> p a b", b=CH), ACT.Copy).then_inc(
                k.aux_drained[t % NX], 1)

        for c in range(NCH):
            t = self.t[c]
            copy(t["an"], b["an"])
            copy(t["d2"], b["d2"])
            copy(t["d2t"], b["d2t"])
            copy(t["bn"], b["bn"])
            copy(t["d4"], b["d4"])
            copy(t["d8"], b["d8"])
            copy(t["kn"], b["kn"])
            copy(t["vn"], b["vn"])
            copy(t["mn"], b["mn"])
            copy(t["g"], b["g"])
            copy(t["mn2"], b["mn"])
            copy(t["g2"], b["g"])
            copy(t["q"], b["q"])
            copy(t["wt"], b["wt"])
            copy(t["y"], self.chunk(self.prep.inp.rkv[0], c))

    def vector(self, dve):
        k, b = self.k, self.buf
        for s in self.prep.bonus_saved:
            dve.wait_ge(s, 16 * 4)
        dve.memset(row(b["z"]), 0.0).then_inc(self.state_cleared, 1)

        def mask(name):
            return k.const(name).unsqueeze(1).to_broadcast([P, 8, CH])

        def src(t):
            return k.aux(t).rearrange("p (a b) -> p a b", b=CH)

        for c in range(NCH):
            tt = self.t[c]

            def done(ins, step):
                ins.then_inc(k.aux_drained[tt[step] % NX], 1)

            def full(step):
                k.wait_aux_full(dve, tt[step])

            full("x")
            dve.tensor_tensor(b["x32"], src(tt["x"]), mask("off16"), ALU.mult)
            dve.tensor_tensor(b["x64"], src(tt["x"]), mask("off32"), ALU.mult)
            done(dve.tensor_tensor(b["d"], src(tt["x"]), mask("diag16"), ALU.mult), "x")

            def twin(step):
                full(step)
                return k.aux(tt[step]).rearrange("p (a s b) -> p a s b", s=2, b=CH)

            def half_mask(name):
                return k.const(name).unsqueeze(1).to_broadcast([P, 4, CH])

            for half in range(2):
                step, ps = f"b_ra{half}", slice(4 * half, 4 * half + 4)
                both = twin(step)
                k.after_dve(dve, dve.tensor_tensor(b["dt"][:, ps], both[:, :, 1], half_mask("diag16T"), ALU.mult))
                dve.tensor_tensor(b["m0"][:, ps], b["dt"][:, ps], half_mask("ident64"), ALU.add)
                done(dve.tensor_tensor(b["rbt"][:, ps], both[:, :, 0], half_mask("from"), ALU.mult), step)

            def summed(step, dst, old, before):
                k.wait_aux_drained(dve, tt[before])
                full(step)
                done(dve.tensor_tensor(row(b[dst]), row(b[old]), k.aux(tt[step]), ALU.add), step)

            for half in range(2):
                step, ps = f"d2_dm{half}", slice(4 * half, 4 * half + 4)
                both = twin(step)
                dve.tensor_copy(b["d4t"][:, ps], both[:, :, 0])
                done(dve.tensor_tensor(b["m1"][:, ps], b["m0"][:, ps], both[:, :, 1], ALU.add), step)
            k.wait_aux_drained(dve, tt["d2_dm0"])
            summed("m2", "m0", "m1", "d2_dm1")
            summed("m3", "m1", "m0", "m2")
            for half in range(2):
                step, ps = f"k_ra{half}", slice(4 * half, 4 * half + 4)
                both = twin(step)
                dve.tensor_tensor(b["akt"][:, ps], both[:, :, 1], half_mask("after"), ALU.mult)
                done(dve.tensor_tensor(b["rkt"][:, ps], both[:, :, 0], half_mask("from"), ALU.mult), step)
            summed("m4", "m0", "m1", "m3")
            summed("m5", "m1", "m0", "m4")
            full("u")
            k.after_dve(dve, dve.tensor_copy(row(b["u"]), k.aux(tt["u"])))
            dve.nop().then_inc(k.aux_drained[tt["u"] % NX], 1)
            full("sa")
            done(dve.tensor_tensor(row(b["sa"]), row(b["u"]), k.aux(tt["sa"]), ALU.add), "sa")
            full("z")
            if c:
                dve.wait_ge(self.state_ready, c)
            done(dve.tensor_tensor(row(b["z"]), row(b["z"]), k.aux(tt["z"]), ALU.add), "z")
            k.wait_aux_drained(dve, tt["z"])
            end = self.prep.end[:, :, c:c + 1].to_broadcast([P, 8, CH])
            dve.tensor_tensor(b["z"], b["z"], end, ALU.mult).then_inc(self.state_ready, 1)

    def wait_y(self, eng):
        self.k.wait_aux_drained(eng, self.t[NCH - 1]["y"])

    def wait_end(self, eng):
        eng.wait_ge(self.state_ready, NCH)


class RwkvOutput(Stage):

    def __init__(self, k, scan, zg, zg_ready, y, bonus, bonus_in, bonus_saved, var, guess, root):
        super().__init__(k)
        self.scan, self.zg, self.zg_ready, self.y, self.bonus, self.bonus_in, self.bonus_saved = (
            scan, zg, zg_ready, y, bonus, bonus_in, bonus_saved)
        self.var, self.guess, self.root = var, guess, root
        self.mt, self.vt = [], []
        for p in range(9):
            if p < 8:
                self.mt.append(k.take_acc())
            if p:
                self.vt.append(k.take_acc())
        self.gt = [k.take_acc() for _ in range(8)]
        self.us = [k.take_unit(self.gt[-1]), k.take_unit(self.gt[-1])]
        self.sq0 = k.reserve("square", 8)
        self.bonus_loaded = k.sem("bonus_loaded")
        self.guess_ready = k.sem("rwkv_guess_ready")
        self.var_ready = k.sem("rwkv_var_ready")

    def gpsimd(self, pool):
        self.scan.wait_y(pool)
        for s in self.bonus_saved:
            pool.wait_ge(s, 16 * 4)
        pool.dma_start(self.bonus, self.bonus_in).then_inc(self.bonus_loaded, 16)

    def tensor(self, pe):
        k = self.k
        self.scan.wait_y(pe)
        for p in range(9):
            if p < 8:
                k.open_acc(pe, self.mt[p])
                pe.matmul(k.acc(self.mt[p]), k.const("head_mean"), self.y[:, p, :], start=True, stop=True).then_inc(
                    k.acc_full, 1)
            if p:
                k.open_acc(pe, self.vt[p - 1])
                pe.wait_ge(k.square_ready, self.sq0 + p)
                pe.matmul(k.acc(self.vt[p - 1]), k.const("head_mean"), k.square[:, (p - 1) % 4, :], start=True,
                          stop=True).then_inc(k.acc_full, 1)
        pe.wait_ge(self.zg_ready, 2)
        w = [k.weights(pe, u) for u in self.us]
        for p in range(8):
            k.open_acc(pe, self.gt[p])
            pe.matmul(k.acc(self.gt[p]), w[0][:, p * P:(p + 1) * P], self.zg[:, 0, :], start=True, stop=False)
            pe.matmul(k.acc(self.gt[p]), w[1][0:32, p * P:(p + 1) * P], self.zg[0:32, 1, :], start=False,
                      stop=True).then_inc(k.acc_full, 1)

    def scalar(self, act):
        k = self.k
        for p in range(8):
            k.wait_acc_drained(act, self.mt[p])
            if p >= 4:
                k.wait_acc_full(act, self.vt[p - 4])
            act.activation(k.square[:, p % 4, :], self.y[:, p, :], ACT.Square).then_inc(k.square_ready, 1)
        for half in range(2):
            ps = slice(4 * half, 4 * half + 4)
            act.wait_ge(self.var_ready, 4 * half + 4)
            k.after_act(act, act.activation(row(self.guess[:, ps]), row(self.var[:, ps]), ACT.Ln))
            act.activation(row(self.guess[:, ps]), row(self.guess[:, ps]), ACT.Exp, scale=-0.5).then_inc(
                self.guess_ready, 1)

    def vector(self, dve):
        k = self.k
        for p in range(9):
            if p < 8:
                y, t = self.y[:, p, :], self.mt[p]
                k.wait_acc_full(dve, t)
                dve.tensor_tensor(y, y, k.acc(t), ALU.subtract).then_inc(k.acc_drained[t % NA], 1)
            if p:
                t = self.vt[p - 1]
                k.wait_acc_full(dve, t)
                k.after_dve(dve, dve.tensor_scalar(self.var[:, p - 1, :], k.acc(t), LNX_EPS, None, ALU.add))
                dve.nop().then_inc(self.var_ready, 1)
                dve.nop().then_inc(k.acc_drained[t % NA], 1)
        dve.wait_ge(self.bonus_loaded, 16)
        for half in range(2):
            ps = slice(4 * half, 4 * half + 4)
            g, r, v = row(self.guess[:, ps]), row(self.root[:, ps]), row(self.var[:, ps])
            dve.wait_ge(self.guess_ready, half + 1)
            k.after_dve(dve, dve.tensor_tensor(r, g, g, ALU.mult))
            k.after_dve(dve, dve.scalar_tensor_tensor(r, r, -0.5, v, ALU.mult, ALU.mult))
            k.after_dve(dve, dve.scalar_tensor_tensor(r, r, 1.5, g, ALU.add, ALU.mult))
            for p in range(4 * half, 4 * half + 4):
                y = self.y[:, p, :]
                k.after_dve(dve, dve.scalar_tensor_tensor(y, y, k.vec("lnx_w", p), self.root[:, p, :], ALU.mult, ALU.mult))
                k.after_dve(dve, dve.scalar_tensor_tensor(y, y, k.vec("lnx_b", p), self.bonus[:, p, :], ALU.add, ALU.add))
                t = self.gt[p]
                k.wait_acc_full(dve, t)
                dve.tensor_tensor(y, y, k.acc(t), ALU.mult).then_inc(k.acc_drained[t % NA], 1)

    def wait_out(self, eng, c):
        self.k.wait_acc_drained(eng, self.gt[c])


class CrossAttention(Stage):

    def __init__(self, k, q, keys, values, out, buf, waits):
        super().__init__(k)
        self.q, self.keys, self.values, self.out, self.buf, self.waits = q, keys, values, out, buf, waits
        self.st, self.tt, self.ot = [], [], []
        for _ in range(4):
            self.st.append([k.take_acc(), k.take_acc()])
            self.tt.append([k.take_acc(), k.take_acc()])
            self.ot.append([k.take_acc(), k.take_acc()])
        self.max_ready = k.sem("cross_max_ready")
        self.p_ready = k.sem("cross_probs_ready")
        self.d_ready = k.sem("cross_diag_ready")

    def tensor(self, pe):
        k, b = self.k, self.buf
        for w in self.waits:
            w(pe)
        for h in range(4):
            for i, t in enumerate(self.st[h]):
                k.open_acc(pe, t)
                for j in range(2):
                    for c in range(2):
                        tok = slice((2 * i + j) * P, (2 * i + j + 1) * P)
                        mm = pe.matmul(k.acc(t)[:, j * N_MEM:(j + 1) * N_MEM], self.q[:, 2 * h + c, tok],
                                       self.keys[:, 2 * h + c, :], start=(c == 0), stop=(c == 1))
                mm.then_inc(k.acc_full, 1)
            pe.wait_ge(self.d_ready, h + 1)
            for j, t in enumerate(self.tt[h]):
                k.open_acc(pe, t)
                for i in range(NT):
                    mm = pe.matmul(k.acc(t)[:, i * P:(i + 1) * P], b.p[:, i * N_MEM + j * P:i * N_MEM + (j + 1) * P],
                                   b.diag[:, i, :], start=True, stop=True)
                mm.then_inc(k.acc_full, 1)
            for c, t in enumerate(self.ot[h]):
                k.open_acc(pe, t)
                for j in range(2):
                    if c == 0:
                        k.wait_acc_drained(pe, self.tt[h][j])
                    at = h * 256 + c * P
                    mm = pe.matmul(k.acc(t), self.values[:, j, at:at + P], b.pt[:, j * S:(j + 1) * S],
                                   start=(j == 0), stop=(j == 1))
                mm.then_inc(k.acc_full, 1)

    def vector(self, dve):
        k, b = self.k, self.buf
        for h in range(4):
            for i, t in enumerate(self.st[h]):
                k.wait_acc_full(dve, t)
                m = dve.tensor_reduce(b.max[:, 0, 2 * i:2 * i + 2],
                                      k.acc(t).rearrange("p (j n) -> p j n", n=N_MEM), AX.X, ALU.max)
                k.after_dve(dve, m)
            dve.tensor_scalar(b.negmax[:, 0, :], b.max[:, 0, :], -1.0 / 16, None, ALU.mult).then_inc(self.max_ready, 1)
            dve.wait_ge(self.p_ready, 4 * (h + 1))
            k.after_dve(dve, dve.reciprocal(b.inv[:, 0, :], b.sum[:, 0, :]))
            dve.tensor_tensor(b.diag, k.const("ident").unsqueeze(1).to_broadcast([P, NT, P]),
                              b.inv[:, 0, :].unsqueeze(2).to_broadcast([P, NT, P]), ALU.mult).then_inc(self.d_ready, 1)
            for c, t in enumerate(self.ot[h]):
                k.wait_acc_full(dve, t)
                dve.tensor_copy(self.out[:, 2 * h + c, :], k.acc(t)).then_inc(k.acc_drained[t % NA], 1)

    def scalar(self, act):
        k, b = self.k, self.buf
        for h in range(4):
            act.wait_ge(self.max_ready, h + 1)
            for i in range(NT):
                t = self.st[h][i // 2]
                src = k.acc(t)[:, (i % 2) * N_MEM:(i % 2 + 1) * N_MEM]
                act.activation(b.p[:, i * N_MEM:(i + 1) * N_MEM], src, ACT.Exp, scale=1.0 / 16,
                               bias=b.negmax[:, 0, i:i + 1], accum_out=b.sum[:, 0, i:i + 1]).then_inc(self.p_ready, 1)
                if i % 2:
                    act.wait_ge(self.p_ready, 4 * h + i + 1)
                    act.nop().then_inc(k.acc_drained[t % NA], 1)
            for j, t in enumerate(self.tt[h]):
                k.wait_acc_full(act, t)
                act.activation(b.pt[:, j * S:(j + 1) * S], k.acc(t), ACT.Copy).then_inc(k.acc_drained[t % NA], 1)

    def wait_out(self, eng, c):
        self.k.wait_acc_drained(eng, self.ot[c // 2][c % 2])


class ConvFfn(SplitStage):

    def __init__(self, k, xs, hi, lo, abuf, t0, t1, out, before, after=None):
        super().__init__(k, after)
        self.xs, self.hi, self.lo, self.abuf, self.t0, self.t1, self.out, self.before = (
            xs, hi, lo, abuf, t0, t1, out, before)
        for _ in range(2 * FT2):
            self.take()
        self.at, self.bt = self.ts[0::2], self.ts[1::2]
        self.padded = k.sem("conv_padded")
        self.conv_ready = k.sem("conv_ready")
        self.tanh_ready = k.sem("silu_tanh_ready")
        self.hi_ready = k.sem("ffn_hi_ready")
        self.lo_ready = k.sem("ffn_lo_ready")

    def wait_hi(self, eng, j):
        eng.wait_ge(self.hi_ready, j + 1)

    def wait_lo(self, eng, j):
        eng.wait_ge(self.lo_ready, j + 1)

    def tensor(self, pe):
        k = self.k
        for i, t in enumerate(self.ts):
            k.open_acc(pe, t)
            k.split_product(pe, k.acc(t), self.us[i], self.xs, wait=(i == 0))

    def hidden_hi(self, act, m):
        self.k.wait_acc_drained(act, self.bt[m])
        act.activation(self.hi[:, m, :], self.out[:, m % 2, :], ACT.Copy).then_inc(self.hi_ready, 1)

    def hidden_lo(self, dve, m):
        self.wait_hi(dve, m)
        dve.tensor_tensor(self.lo[:, m, :], self.out[:, m % 2, :], self.hi[:, m, :].bitcast(F32),
                          ALU.subtract).then_inc(self.lo_ready, 1)

    def scalar(self, act):
        k = self.k
        self.convert_first(act, k.convert_hi)
        act.wait_ge(self.padded, 1)
        for m, t in enumerate(self.at):
            self.convert_next(act, k.convert_hi, 2 * m)
            if m:
                self.hidden_hi(act, m - 1)
            k.wait_acc_full(act, t)
            if m >= 2:
                act.wait_ge(self.conv_ready, m - 1)
            act.activation(self.abuf[:, m % 2, 2:2 + S], k.acc(t), ACT.Copy).then_inc(k.acc_drained[t % NA], 1)
            self.convert_next(act, k.convert_hi, 2 * m + 1)
            act.wait_ge(self.conv_ready, m + 1)
            if m >= 2:
                k.wait_acc_drained(act, self.bt[m - 2])
            act.activation(self.t1[:, m % 2, :], self.t0[:, m % 2, :], ACT.Tanh, scale=0.5).then_inc(self.tanh_ready, 1)
        self.hidden_hi(act, FT2 - 1)

    def vector(self, dve):
        k = self.k
        self.before(dve)
        dve.memset(self.abuf[:, :, 0:2], 0.0).then_inc(self.padded, 1)
        self.convert_first(dve, k.convert_lo)
        for m, t in enumerate(self.bt):
            self.convert_next(dve, k.convert_lo, 2 * m)
            if m:
                self.hidden_lo(dve, m - 1)
            k.wait_acc_drained(dve, self.at[m])
            a, c = self.abuf[:, m % 2, :], self.t0[:, m % 2, :]
            k.after_dve(dve, dve.tensor_scalar(c, a[:, 2:2 + S], k.vec("conv", 2 * FT2 + m), k.vec("conv_b", m),
                                               ALU.mult, ALU.add))
            k.after_dve(dve, dve.scalar_tensor_tensor(c, a[:, 1:1 + S], k.vec("conv", FT2 + m), c, ALU.mult, ALU.add))
            dve.scalar_tensor_tensor(c, a[:, 0:S], k.vec("conv", m), c, ALU.mult, ALU.add).then_inc(self.conv_ready, 1)
            self.convert_next(dve, k.convert_lo, 2 * m + 1)
            dve.wait_ge(self.tanh_ready, m + 1)
            k.after_dve(dve, dve.scalar_tensor_tensor(c, self.t1[:, m % 2, :], 1.0, c, ALU.add, ALU.mult))
            k.wait_acc_full(dve, t)
            if m >= 2:
                self.wait_lo(dve, m - 2)
            dve.scalar_tensor_tensor(self.out[:, m % 2, :], c, 0.5, k.acc(t), ALU.mult, ALU.mult).then_inc(
                k.acc_drained[t % NA], 1)
        self.hidden_lo(dve, FT2 - 1)


class Move(Stage):

    def __init__(self, k, name, dst, src, waits):
        super().__init__(k)
        self.dst, self.src, self.waits = dst, src, waits
        self.done = k.sem(name)

    def gpsimd(self, pool):
        for w in self.waits:
            w(pool)
        pool.dma_start(self.dst, self.src).then_inc(self.done, 16)

    def wait_done(self, eng):
        eng.wait_ge(self.done, 16)


class Alibi(Stage):

    def __init__(self, k, table):
        super().__init__(k)
        self.table = table
        self.ready = k.sem("alibi_ready")

    def scalar(self, act):
        k = self.k
        act.wait_ge(k.const_loaded, 16)
        for h in range(H1):
            act.activation(self.table[:, h, :], k.const("neg_dist"), ACT.Copy,
                           scale=float(2.0 ** (-8.0 * (h + 1) / H1))).then_inc(self.ready, 1)


class Store(Stage):

    def __init__(self, k, out, wait_x):
        super().__init__(k)
        self.out, self.wait_x = out, wait_x
        self.stored = k.sem("out_stored")

    def sync(self, sp):
        for j in range(DT_):
            self.wait_x(sp, j)
            sp.dma_start(self.out[:, j, :], self.k.x[:, j, :]).then_inc(self.stored, 16)
        sp.wait_ge(self.stored, 16 * DT_)


class Buffers:

    def __init__(self, view, p, pt, ct, small):
        self.p, self.pt = view(p, [3, TRI_N]), view(pt, [2, TRI_N])
        self.ct = view(ct, [S], parts=NCMP)
        self.max, self.negmax, self.sum = (view(small + 12 * i, [3, NT]) for i in range(3))
        self.inv = view(small + 36, [6, NT])


class CrossBuffers:

    def __init__(self, view, at):
        self.p = view(at, [NT * N_MEM])
        self.pt = view(at + 1024, [2 * S])
        self.diag = view(at + 2048, [NT, P])
        self.max, self.negmax, self.sum, self.inv = (view(at + 2560 + 4 * i, [1, NT]) for i in range(4))


def build(nc, x, consts, vecs, weights, bucket, rel, rel_last, mem, out):
    with ExitStack() as ctx:
        k = Core(nc, ctx)
        k.set_up()
        ARENA = 37884
        k.wring = k.sb("wring", [P, RING, UNIT])
        k.w_hi = ctx.enter_context(nc.sbuf_tensor("w_hi", [P, SPLIT, UNIT], F32R))
        k.w_lo = ctx.enter_context(nc.sbuf_tensor("w_lo", [P, SPLIT, UNIT], F32R))
        hot = ctx.enter_context(nc.sbuf_tensor("one_hot_sb", [BUCKETS + 1, 1024], F32R))
        rows = ctx.enter_context(nc.sbuf_tensor("bias_rows", [BUCKETS + 1, 2 * HQ], F32R))
        k.consts = k.sb("consts_sb", [P, N_CONST])
        k.vecs = k.sb("vecs_sb", [P, N_VEC])
        k.square = k.sb("square", [P, 4, S])
        k.root_in = k.sb("root_in", [P, S])
        k.root_ln = k.root_y = k.sb("root_y", [P, S])
        k.root = k.sb("root", [P, S])
        gain8 = k.sb("q_gain_scaled", [P, 1])
        with nc.sbuf_tensor("arena", [P, ARENA], F32) as arena:
            pass
        k.ps = ctx.enter_context(nc.psum_tensor("ps", [P, 8, S], F32))
        bonus_dram = nc.dram_tensor("bonus_scratch", (P, DT_, S), F32, kind="Internal").ap()
        x_dram = nc.dram_tensor("x_scratch", (P, DT_, S), F32, kind="Internal").ap()

        def view_r(name, at, shape):
            assert at + int(np.prod(shape)) <= ARENA, (at, shape)
            with ExitStack() as place:
                if at:
                    place.enter_context(nc.sbuf_tensor(f"below_{name}", [P, at], F32))
                return place.enter_context(nc.sbuf_tensor(name, [P] + shape, F32R))[:, :, :]

        def view(at, shape, parts=P):
            n = int(np.prod(shape))
            assert at + n <= ARENA, (at, shape)
            a = arena[0:parts, at:at + n]
            if len(shape) == 1:
                return a
            if len(shape) == 2:
                return a.rearrange("p (a b) -> p a b", b=shape[1])
            return a.rearrange("p (a b c) -> p a b c", b=shape[1], c=shape[2])

        k.x = view(0, [DT_, S])
        xn = view(4096, [DT_, S])
        free = 8192

        def drained(stage):
            return lambda eng, j: k.wait_acc_drained(eng, stage.ts[j])

        def tiles(ap):
            return lambda j: ap[:, j, :]

        Load(k, x, consts, vecs, weights)
        cat = view(free, [DT_, S])
        qk = view(12288, [8, S])
        v1 = view(16384, [NT, S])
        u1 = view(18432, [4, 16 + S])
        sums = view(20544, [2, 16 + S])
        mixed = view(21600, [4, S])
        alibi = view(23648, [H1, S])
        buf1 = Buffers(view, 27744, 31584, 34144, 34656)
        begin1 = Begin(k)
        xn32 = view(31840, [DT_, S])
        n1 = Norm(k, k.x, xn32, "norm_mix", lambda eng, j: eng.wait_ge(k.x_loaded, 16))
        xs1 = SplitTiles(k, "first_input", xn32, view_r("first_input_hi", 4096, [DT_, S]),
                         view_r("first_input_lo", 27744, [DT_, S]), n1.wait_dst)
        pq = SplitProject(k, 8, xs1, [copy_out(k, qk[:, i, :], 0.125 if i < 4 else 1.0) for i in range(8)],
                          after=begin1)
        al = Alibi(k, alibi)
        pu = SplitProject(k, 4, xs1, [copy_out(k, u1[:, i, 16:16 + S]) for i in range(4)], wait=False, after=pq)
        pv = Project(k, 4, tiles(xn32), n1.wait_dst,
                     [copy_tokens(k, v1[:, :, i * P:(i + 1) * P], P) for i in range(4)], kind="tokens")
        pool = Pool(k, u1, sums, mixed, cat, pu.ts)
        heads = []
        for h in range(H1):
            lo, p = HD * (h % 2), h // 2
            ready = [lambda pe, p=p: k.wait_acc_drained(pe, pq.ts[p]),
                     lambda pe, p=p: k.wait_acc_drained(pe, pq.ts[4 + p]),
                     lambda pe, p=p: k.wait_acc_drained(pe, pv.ts[p])]
            if h == 0:
                ready.append(lambda pe: pe.wait_ge(al.ready, H1))
            heads.append(Head(qk[lo:lo + HD, p, :], qk[lo:lo + HD, 4 + p, :],
                              lambda j, h=h: v1[:, j, h * HD:(h + 1) * HD], alibi[:, h, :], lo, ready=ready))
        begin_out = Begin(k)
        at1 = Attention(k, "moba", heads, lambda u: cat[:, u // 2, :], buf1)

        def wait_cat(pe, c):
            k.wait_acc_drained(pe, at1.pair[2 * c] if c < 4 else pool.ts[c - 4])

        cats = SplitTiles(k, "mixed", cat, view_r("mixed_hi", 4096, [DT_, S]), view_r("mixed_lo", 18432, [DT_, S]),
                          wait_cat)
        po = SplitProject(k, 8, cats, [add_residual(k, k.x[:, i, :]) for i in range(8)], after=begin_out)
        xn32 = view(28672, [DT_, S])
        n2 = Norm(k, k.x, xn32, "norm_mlp", drained(po))
        xs = SplitTiles(k, "mlp_input", xn32, view_r("mlp_input_hi", 4096, [DT_, S]), view_r("mlp_input_lo", 24576, [DT_, S]), n2.wait_dst)
        hid = Hidden(k, [view_r(f"mlp_hi{i}", 8192 + 8192 * i, [8, S]) for i in range(2)],
                     [view_r(f"mlp_lo{i}", 12288 + 8192 * i, [8, S]) for i in range(2)], view(32768, [4, S]))
        hidden = [hid.group(g) for g in range(4)]
        up, down = [SplitProject(k, 8, xs, hidden[0].drains, after=po)], []
        for g in range(1, 5):
            last = down[-1] if down else up[-1]
            if g < 4:
                last = SplitProject(k, 8, xs, hidden[g].drains, wait=False, after=last)
                up.append(last)
            down.append(SplitProject(k, 8, hidden[g - 1], [add_residual(k, k.x[:, i, :]) for i in range(8)], after=last))
        pd = down[-1]
        n3 = Norm(k, k.x, k.x, "norm_final", drained(pd))

        n4 = Norm(k, k.x, xn, "norm_mix_2", n3.wait_dst)
        save_x = Move(k, "x_saved", x_dram, k.x, [lambda e: n4.wait_dst(e, 7)])
        rr, kk, vv, aa, bb = (view(free + 4096 * i, [DT_, S]) for i in range(5))
        zwa, zg, end = view(28672, [S]), view(29184, [2, S]), view(30208, [DT_, NCH])
        tail = 30272
        shift = view(tail + 6000, [3, 1 + S])
        xs4 = SplitTiles(k, "mixer_input", xn, view_r("mixer_input_hi", 24576, [DT_, S]), view_r("mixer_input_lo", 20480, [DT_, S]), n4.wait_dst)
        inp = RwkvInputs(k, xs4, (rr, kk, vv), zwa, zg, shift, lambda e: n4.wait_dst(e, 7), after=pd)
        tmp = {n: view(tail + S * i, [S]) for i, n in enumerate(("decay", "a", "kk", "sum", "before", "p", "inv", "mix", "rkk"))}
        tmp["bonus"] = view(tail + 9 * S, [2, S])
        tmp["w0h"], tmp["a0h"] = view(tail + 11 * S, [8]), view(tail + 11 * S + 8, [8])
        prep = RwkvPrepare(k, inp, aa, bb, end, tmp, bonus_dram)
        names = ("an", "bn", "kn", "vn", "d", "dt", "x32", "x64", "d2t", "m0", "m1", "akt", "rbt", "rkt",
                 "d2", "d4", "d4t", "d8", "mn", "wt", "sa", "z")
        sbuf = {n: view(tail + S * i if i < 14 else S * (i - 14), [DT_, CH]) for i, n in enumerate(names)}
        sbuf["q"], sbuf["u"], sbuf["g"] = sbuf["d8"], sbuf["d4t"], sbuf["d2t"]
        sbuf["d2t_m0"] = view(tail + S * 8, [2, DT_, CH])
        ra = arena[:, 8192:8192 + 2 * 12288].rearrange("p (s n) -> p s n", s=2)
        scan = RwkvScan(k, prep, sbuf, ra)
        begin_gated = Begin(k)
        xs6 = SplitTiles(k, "gate_input", xn, view_r("gate_input_hi", 0, [DT_, S]),
                         view_r("gate_input_lo", 24576, [DT_, S]),
                         lambda e, j: scan.wait_end(e), alone=True)
        outp = RwkvOutput(k, scan, zg, inp.zg_ready, rr, vv, bonus_dram, prep.bonus_saved, aa, kk,
                          view(30272, [DT_, S]))
        merged = aa
        tanh = view(34944, [2, S])
        tab, hot_in = view(36100, [3, HQ], parts=BUCKETS + 1), view(36200, [1024], parts=BUCKETS + 1)
        table_rows = TableRows(k, rel, rel_last, bucket, tab, hot_in, hot, rows,
                               lambda e: k.wait_aux_drained(e, scan.t[NCH - 1]["z"]))
        ys = SplitTiles(k, "rwkv_y", rr, view_r("rwkv_y_hi", 12288, [DT_, S]), view_r("rwkv_y_lo", 30272, [DT_, S]),
                        outp.wait_out)
        br = Gated(k, ys, xs6, merged, tanh, first=True, after=begin_gated)

        wide = view(8192, [HQ, S])
        q2 = view(16384, [DT_, S])
        kd = [view(24576 + 2048 * i, [NKV, S]) for i in range(2)]
        vs = [view(28672 + 1024 * i, [NT, 256]) for i in range(2)]
        comp = view(30720, [HQ, NT * NCMP])
        gate = view(32704, [NT, 48])
        kraw = [view(32896 + 1024 * i, [2, S]) for i in range(2)]
        kc, vc = view(0, [2, S]), view(1024, [2, S])
        staged = (view(2048, [16, 124]), view(26624, [16, 124]))
        kv_swap = [view(24576 + 1024 * b, [2, S]) for b in range(2)]
        chid, keys_raw = view(34944, [2, 248]), view(35936, [124])
        craw, ctmp = view(32896, [2, 256], parts=124), view(33408, [2, 256], parts=124)
        keys, values = view(37504, [124]), view(37628, [NKV, HD], parts=NCMP)
        buf2 = Buffers(view, 0, 34944, 32896, 3840)

        tb = Tables(k, table_rows, wide, comp)
        gain_ready = k.sem("q_gain_ready")
        nq = SplitProjectNorm(k, 8, xs6, tiles(q2), tiles(q2), lambda i: gain8[:, 0:1], "head_mean", after=br)
        def gate_tanh():
            def scalar(act, t):
                k.wait_acc_full(act, t)
                act.activation(gate, k.acc(t)[:, 0:NT * 48].rearrange("p (b m) -> p b m", m=48), ACT.Tanh,
                               scale=0.5).then_inc(k.acc_drained[t % NA], 1)
            return {"scalar": scalar}

        pg = Project(k, 1, tiles(xn), lambda pe, c: None, [gate_tanh()], kind="tokens", m=48)
        Gates(k, gate, lambda e: k.wait_acc_drained(e, pg.ts[0]))
        pkv = Project(k, 4, tiles(xn), lambda pe, c: None,
                      [copy_out(k, (kc, vc)[i // 2][:, i % 2, :]) for i in range(4)])
        cmp_ = Compress(k, (kc, vc), kv_swap, lambda e, b: k.wait_acc_drained(e, pkv.ts[2 * b + 1]), staged, craw,
                        ctmp, chid, keys_raw, keys, values)
        cmx = view(35936 + 124, [2, HQ * NT])
        cs = CompressedSoftmax(k, q2, keys, comp, gate, cmx, nq.wait_dst,
                               lambda pe: [cmp_.wait_done(pe)] + [k.wait_acc_drained(pe, t) for t in tb.ts])
        nk = [ProjectNorm(k, 2, tiles(xn), lambda pe, c: None, tiles(kraw[b]), tiles(kraw[b]),
                          lambda i, b=b: k.vec("k_gain", 1 + b), "head_mean") for b in range(2)]
        spread = Spread(k, kraw, kd, [nk[0].wait_dst, nk[1].wait_dst])
        pvs = [Project(k, 2, tiles(xn), lambda pe, c: None,
                       [copy_tokens(k, vs[b][:, :, i * P:(i + 1) * P], P) for i in range(2)], kind="tokens")
               for b in range(2)]
        heads = []
        for pair in range(DT_):
            g = pair // 2
            slot = (g % 2) * 2 + g // 2
            for e in range(2):
                h, lo = 2 * pair + e, HD * e
                hf = slice(lo, lo + HD)
                ready = []
                if h == 0:
                    ready = [lambda pe: nq.wait_dst(pe, 7), spread.wait_done, lambda pe: pe.wait_ge(cs.done, 1),
                             lambda pe: [k.wait_acc_drained(pe, t) for p_ in pvs for t in p_.ts]]
                for b in range(2):
                    gt = gate[:, :, 3 * h + 1 + b:3 * h + 2 + b].rearrange("p a b -> p (a b)")
                    heads.append(Head(q2[hf, pair, :], kd[b][hf, g, :],
                                      lambda j, b=b, g=g: vs[b][:, j, g * HD:(g + 1) * HD], wide[:, h, :], lo,
                                      gate=gt, compressed=(comp[:, h, :], values[:, slot, :]) if b == 0 else None,
                                      last=(b == 1), ready=ready if b == 0 else ()))
        begin_gated2 = Begin(k)
        at2 = Attention(k, "nsa", heads, lambda u: q2[:, u // 4, :], buf2)
        xs7 = SplitTiles(k, "gate2_input", xn, view_r("gate2_input_hi", 8192, [DT_, S]),
                         view_r("gate2_input_lo", 12288, [DT_, S]), lambda e, j: k.wait_acc_drained(e, at2.pair[-1]))
        ys2 = SplitTiles(k, "nsa_y", q2, view_r("nsa_y_hi", 24576, [DT_, S]), view_r("nsa_y_lo", 28672, [DT_, S]),
                         lambda e, j: k.wait_acc_drained(e, at2.pair[-1]))
        bn = Gated(k, ys2, xs7, merged, tanh, first=False,
                   wait_merged=lambda e: [k.wait_acc_drained(e, t) for t in br.bt], after=begin_gated2)
        ms = SplitTiles(k, "merged", merged, view_r("merged_hi", 16384, [DT_, S]), view_r("merged_lo", 4096, [DT_, S]),
                        lambda e, c: e.wait_ge(k.merged_ready, c + 1))
        load_x = Move(k, "x_back", k.x, x_dram, [save_x.wait_done, lambda e: k.wait_acc_drained(e, at2.pair[-1])])

        def add_half(i):
            def vector(dve, t):
                if i == 0:
                    load_x.wait_done(dve)
                k.wait_acc_full(dve, t)
                dve.scalar_tensor_tensor(k.x[:, i, :], k.acc(t), 0.5, k.x[:, i, :], ALU.mult, ALU.add).then_inc(
                    k.acc_drained[t % NA], 1)
            return {"vector": vector}

        pm = SplitProject(k, 8, ms, [add_half(i) for i in range(8)], after=bn)

        mem_t = view(32768, [DT_, N_MEM])
        load_mem = Move(k, "mem_loaded", mem_t, mem, [lambda e: k.wait_acc_drained(e, at2.pair[-1])])
        nm = Norm(k, mem_t, mem_t, "norm_mem", lambda e, j: load_mem.wait_done(e), n=N_MEM)
        q3, k3 = view(12288, [DT_, S]), view(16384, [DT_, N_MEM])
        v3, o3 = view(18432, [2, D]), view(24576, [DT_, S])
        pk = ProjectNorm(k, 8, tiles(mem_t), nm.wait_dst, tiles(k3), tiles(k3),
                         lambda i: k.vec("ca_k_gain", i % 2), "ones256", span=2, n=N_MEM)
        pv3 = Project(k, 8, tiles(mem_t), nm.wait_dst,
                      [copy_tokens(k, v3[:, :, i * P:(i + 1) * P], P, blocks=2) for i in range(8)], kind="tokens",
                      n=N_MEM)
        xn32 = view(8192, [DT_, S])
        begin_cross = Begin(k)
        nx = Norm(k, k.x, xn32, "norm_cross", drained(pm))
        xs8 = SplitTiles(k, "cross_input", xn32, view_r("cross_input_hi", 28672, [DT_, S]),
                         view_r("cross_input_lo", 20480, [DT_, S]), nx.wait_dst)
        pq3 = SplitProjectNorm(k, 8, xs8, tiles(q3), tiles(q3), lambda i: k.vec("ca_q_gain", i % 2), "ones256", span=2,
                               after=begin_cross)
        buf3 = CrossBuffers(view, 28672)
        ca = CrossAttention(k, q3, k3, v3, o3, buf3,
                            [lambda pe: pk.wait_dst(pe, 7), lambda pe: pq3.wait_dst(pe, 7),
                             lambda pe: [k.wait_acc_drained(pe, t) for t in pv3.ts]])
        os3 = SplitTiles(k, "cross_out", o3, view_r("cross_out_hi", 8192, [DT_, S]),
                         view_r("cross_out_lo", 4096, [DT_, S]), ca.wait_out)
        pco = SplitProject(k, 8, os3, [add_residual(k, k.x[:, i, :]) for i in range(8)], after=pq3)

        xn32 = view(30720, [DT_, S])
        nf = Norm(k, k.x, xn32, "norm_ffn", drained(pco))
        xs5 = SplitTiles(k, "ffn_input", xn32, view_r("ffn_input_hi", 4096, [DT_, S]), view_r("ffn_input_lo", 8192, [DT_, S]), nf.wait_dst)
        ff = ConvFfn(k, xs5, view_r("ffn_hi", 12288, [FT2, S]), view_r("ffn_lo", 23552, [FT2, S]), view(34816, [2, 2 + S]),
                     k.square[:, 0:2], view(35844, [2, S]), k.square[:, 2:4], lambda e: nf.wait_dst(e, 7), after=pco)
        pf = SplitProject(k, 8, ff, [add_residual(k, k.x[:, i, :]) for i in range(8)], groups=(8, 8, 6), after=ff)
        Store(k, out, drained(pf))

        def scaled_gain(dve):
            dve.tensor_scalar(gain8[:, :], k.vec("q_gain"), 0.125, None, ALU.mult).then_inc(gain_ready, 1)
            dve.wait_ge(gain_ready, 1)

        stages = k.stages
        block = ctx.enter_context(nc.Block())

        @block.sync
        def _(sp):
            for s in stages:
                s.sync(sp)

        @block.tensor
        def _(pe):
            for s in stages:
                s.tensor(pe)

        @block.vector
        def _(dve):
            dve.wait_ge(k.vec_loaded, 16)
            scaled_gain(dve)
            for s in stages:
                s.vector(dve)

        @block.scalar
        def _(act):
            for s in stages:
                s.scalar(act)

        @block.gpsimd
        def _(pool_engine):
            for s in stages:
                s.gpsimd(pool_engine)
        return [u[1] for u in k.units]


def tiled(w, m=P):
    kt = w.shape[0] // P
    return [w[:, i:i + m].reshape(kt, P, -1).transpose(1, 0, 2).reshape(P, -1) for i in range(0, w.shape[1], m)]


def cut_units(tile, sizes):
    out, at = [], 0
    for n in sizes:
        out.append(tile[:, at * P:(at + n) * P])
        at += n
    return out


def stream(a):
    units = []
    w = a["w_in"][0]
    units += tiled(w[:, 0:1024]) + tiled(w[:, 1536:2048]) + tiled(w[:, 1024:1536])
    units.append(a["w_pool"][0].transpose(1, 0, 2).reshape(P, 4 * P))
    units += tiled(a["w_out"][0])
    up, down = tiled(a["w_up"][0]), [cut_units(t, (8, 8, 8, 8)) for t in tiled(a["w_down"][0])]
    units += up[0:8]
    for g in range(1, 5):
        units += up[8 * g:8 * g + 8] + [t[g - 1] for t in down]
    w2 = a["w_in_2"][0]
    units += tiled(w2[:, 0:RWKV_COLS])
    units.append(np.concatenate([a["rwkv_w2_2"][0], a["rwkv_a2_2"][0]], axis=0))
    g2 = a["rwkv_g2_2"][0]
    units += [g2[0:P], np.concatenate([g2[P:], np.zeros((P - 32, D), g2.dtype)], axis=0)]
    at = RWKV_COLS
    part = {}
    for name, n in (("q", 1024), ("kc", 256), ("vc", 256), ("ks", 256), ("vs", 256), ("kw", 256), ("vw", 256),
                    ("g", 48), ("m0", 1024), ("m1", 1024)):
        part[name] = w2[:, at:at + n]
        at += n
    for gw, bw in zip(tiled(part["m0"]), tiled(a["w_branch_rwkv_2"][0])):
        units += [gw, bw]
    units += tiled(part["q"]) + tiled(part["g"], 48) + tiled(part["kc"]) + tiled(part["vc"])
    for s in "kv":
        units += list(a[f"cmp_w1_{s}_2"][0].reshape(4, 4, P, 256).transpose(0, 2, 1, 3).reshape(4, P, 1024))
    ck = a["cmp_w2_k_2"][0].reshape(2, P, HD)
    ck = np.concatenate([ck, ck], axis=2).transpose(1, 0, 2).reshape(P, 256)
    cv = a["cmp_w2_v_2"][0].reshape(2, P, HD).transpose(1, 0, 2).reshape(P, 128)
    units.append(np.concatenate([ck, cv], axis=1))
    units += tiled(part["ks"]) + tiled(part["kw"]) + tiled(part["vs"]) + tiled(part["vw"])
    for gw, bw in zip(tiled(part["m1"]), tiled(a["w_branch_nsa_2"][0])):
        units += [gw, bw]
    units += tiled(a["w_mix_out_2"][0])
    wkv = a["ca_wkv_2"][0]
    units += tiled(wkv[:, 0:1024]) + tiled(wkv[:, 1024:2048]) + tiled(a["ca_wq_2"][0]) + tiled(a["ca_wo_2"][0])
    up = a["ffn_up_2"][0]
    for gw, bw in zip(tiled(up[:, 0:D_FF2]), tiled(up[:, D_FF2:])):
        units += [gw, bw]
    for t in tiled(a["ffn_down_2"][0]):
        units += cut_units(t, (8, 8, 6))
    return units


def vectors(a):
    def cols(v):
        v = np.asarray(v).reshape(-1)
        pad = (-len(v)) % P
        return np.concatenate([v, np.zeros(pad, v.dtype)]).reshape(-1, P).T

    def twice(v):
        return np.concatenate([v, v], axis=-1)

    parts = {
        "norm_mix": a["norm_mix"], "norm_mlp": a["norm_mlp"], "norm_final": a["norm_final"],
        "pool_scale": a["pool_scale"], "norm_mix_2": a["norm_mix_2"], "mu": a["rwkv_mu_2"], "w0": a["rwkv_w0_2"],
        "a0": a["rwkv_a0_2"], "k_k": a["rwkv_kk_2"], "k_a": a["rwkv_ka_2"], "r_k": a["rwkv_rk_2"],
        "lnx_w": a["rwkv_lnx_w_2"], "lnx_b": a["rwkv_lnx_b_2"], "norm_cross": a["norm_cross_2"],
        "norm_mem": a["norm_mem_2"], "norm_ffn": a["norm_ffn_2"], "conv": a["ffn_conv_2"], "conv_b": a["ffn_conv_b_2"],
        "ca_q_gain": a["ca_q_gain_2"], "ca_k_gain": a["ca_k_gain_2"], "q_gain": twice(a["nsa_q_gain_2"][0]),
        "k_gain": twice(a["nsa_k_gain_2"][0]), "pe_k": twice(a["cmp_pe_k_2"][0]), "pe_v": twice(a["cmp_pe_v_2"][0]),
    }
    return np.concatenate([cols(parts[n]) for n in VECS], axis=1)


def feature_tiles(x):
    return x.T.reshape(-1, P, x.shape[0]).transpose(1, 0, 2)


def kernel(**inputs):
    import concourse.bacc as bacc
    from concourse.bass_utils import run_bass_kernel_spmd

    a = {name: np.asarray(v) for name, v in inputs.items()}
    units = stream(a)
    w = np.zeros((len(units), P, UNIT), a["w_in"].dtype)
    for g, u in enumerate(units):
        w[g, :, 0:u.shape[1]] = u
    rel = a["rel_bias_2"]
    arrays = {
        "x_t": feature_tiles(a["x"][0]), "consts": constants(), "vectors": vectors(a), "weights": w,
        "one_hot": one_hot(),
        "rel_bias": rel, "rel_last": np.repeat(rel[BUCKETS - 1:], BUCKETS, axis=0), "mem_t": feature_tiles(a["mem_2"][0]),
    }
    arrays = {n: np.ascontiguousarray(v) for n, v in arrays.items()}
    nc = bacc.Bacc("TRN2", target_bir_lowering=False, num_devices=1)
    args = [nc.dram_tensor(n, v.shape, F32, kind="ExternalInput").ap() for n, v in arrays.items()]
    out = nc.dram_tensor("out_t", (P, DT_, S), F32, kind="ExternalOutput").ap()
    sizes = build(nc, *args, out)
    assert sizes == [u.shape[1] for u in units]
    r = run_bass_kernel_spmd(nc, [arrays], core_ids=[0])
    return r.results[0]["out_t"].transpose(1, 0, 2).reshape(D, S).T.reshape(1, S, D)
```

```python
from contextlib import ExitStack

import concourse.bass as bass
import numpy as np
from concourse import mybir

F32 = mybir.dt.float32
F32R = mybir.dt.float32r
ACT = mybir.ActivationFunctionType
ALU = mybir.AluOpType
AX = mybir.AxisListType

P = 128
S = 512
D = 1024
DT_ = D // P
NT = S // P
HD = 64
H1 = 8
D_FF = 4096
N_MEM = 256
RH = 16
CH = 64
NCH = S // CH
NKV = 4
HQ = 16
NCMP = (S - 32) // 16 + 1
D_FF2 = 2816
FT2 = D_FF2 // P
RWKV_COLS = 3360
EPS = 1e-6
LNX_EPS = 64e-5
NEG = -1e30
DECAY = float(np.exp(np.float32(-0.5)))
RING = 4
SPLIT = 2
NA, NX = 3, 5
UNIT = 1024
BUCKETS = 32
OH_OFF = 511


def bucket_of(dist):
    n = np.maximum(dist, 0)
    nf = np.maximum(n, 1).astype(np.float32)
    large = 16 + (np.log(nf / 16) / np.log(128 / 16) * 16).astype(np.int32)
    return np.where(n < 16, n, np.minimum(large, 31))


CONST = {}


def constants():
    p = np.arange(P)[:, None]
    c = np.arange(P)[None, :]
    t = np.arange(CH)[None, :]
    q = p % CH
    parts = {
        "ident": (p == c),
        "ones": np.full((P, P), 1.0 / D),
        "ones256": np.full((P, P), 1.0 / 256),
        "head_mean": (p // HD == c // HD) / HD,
        "head_sum": (p // HD == c // HD),
        "ident64": (q == t),
        "diag16": (q // 16 == t // 16) & (q > t),
        "off16": (q // 32 == t // 32) & (q // 16 > t // 16),
        "off32": (q // 32 > t // 32),
        "diag16T": (q // 16 == t // 16) & (q < t),
        "after": (q < t),
        "from": (q <= t),
        "restart": np.broadcast_to((np.arange(S) % CH != 0)[None], (P, S)),
    }
    w = np.arange(S)[None, :]
    neg_dist = (w - p - (S - P)).astype(np.float64)
    parts["neg_dist"] = np.where(neg_dist > 0, NEG, neg_dist)
    cnt = np.stack([1.0 / np.minimum(np.arange(16) + 1, 2 << g) for g in range(4)]).reshape(1, -1)
    parts["inv_count"] = np.broadcast_to(cnt, (P, 64))
    at = 0
    for name, a in parts.items():
        CONST[name] = (at, a.shape[1])
        at += a.shape[1]
    return np.concatenate([np.asarray(a, np.float32) for a in parts.values()], axis=1)


N_CONST = constants().shape[1]


def one_hot():
    dist = np.arange(1024) - OH_OFF
    hot = np.zeros((BUCKETS + 1, 1024), np.float32)
    hot[:BUCKETS] = (bucket_of(dist)[None] == np.arange(BUCKETS)[:, None]) & (dist >= 0)[None]
    hot[BUCKETS] = dist < 0
    return hot


VECS = {}


def vec_columns():
    at = 0
    for name, n in (("norm_mix", 8), ("norm_mlp", 8), ("norm_final", 8), ("pool_scale", 4), ("norm_mix_2", 8),
                    ("mu", 27), ("w0", 8), ("a0", 8), ("k_k", 8), ("k_a", 8), ("r_k", 8), ("lnx_w", 8), ("lnx_b", 8),
                    ("norm_cross", 8), ("norm_mem", 8), ("norm_ffn", 8), ("conv", 3 * FT2), ("conv_b", FT2),
                    ("ca_q_gain", 2), ("ca_k_gain", 2), ("q_gain", 1), ("k_gain", 3), ("pe_k", 32), ("pe_v", 32)):
        VECS[name] = at
        at += n
    return at


N_VEC = vec_columns()


class Core:

    def __init__(self, nc, ctx):
        self.nc, self.ctx = nc, ctx
        self.units = []
        self.split = []
        self.n_used = 0
        self.n_acc = 0
        self.n_aux = 0
        self.count = {}
        self.stages = []

    def sb(self, name, shape):
        return self.ctx.enter_context(self.nc.sbuf_tensor(name, shape, F32))

    def sem(self, name):
        return self.ctx.enter_context(self.nc.semaphore(name))

    def take_acc(self, n=1):
        a = self.n_acc
        self.n_acc += n
        return a

    def take_aux(self, n=1):
        a = self.n_aux
        self.n_aux += n
        return a

    def take_unit(self, acc, n=UNIT):
        self.units.append((len(self.units), n, acc, None))
        return len(self.units) - 1

    def take_split(self, acc, n=UNIT, last=True):
        self.units.append((len(self.units), n, acc, len(self.split)))
        self.n_used += 0 if last else 1
        self.split.append((len(self.units) - 1, acc, last, self.n_used))
        return len(self.split) - 1

    def reserve(self, name, n):
        a = self.count.get(name, 0)
        self.count[name] = a + n
        return a

    def set_up(self):
        sem = self.sem
        self.acc_full = sem("acc_full")
        self.acc_drained = [sem(f"acc_drained{b}") for b in range(NA)]
        self.aux_full = sem("aux_full")
        self.aux_drained = [sem(f"aux_drained{b}") for b in range(NX)]
        self.w_loaded = [sem(f"w_loaded{i}") for i in range(RING)]
        self.w_hi_ready = sem("w_hi_ready")
        self.w_lo_ready = sem("w_lo_ready")
        self.split_used = sem("split_used")
        self.const_loaded = sem("const_loaded")
        self.vec_loaded = sem("vec_loaded")
        self.x_loaded = sem("x_loaded")
        self.x_updated = sem("x_updated")
        self.square_ready = sem("square_ready")
        self.square_used = sem("square_used")
        self.root_ready = sem("root_ready")
        self.xn_ready = sem("xn_ready")
        self.merged_ready = sem("merged_ready")
        self.act_step = sem("act_step")
        self.dve_step = sem("dve_step")
        self.pool_step = sem("pool_step")
        self.steps = {"act": 0, "dve": 0, "pool": 0}

    def after_act(self, act, ins):
        self.steps["act"] += 1
        ins.then_inc(self.act_step, 1)
        act.wait_ge(self.act_step, self.steps["act"])

    def after_dve(self, dve, ins):
        self.steps["dve"] += 1
        ins.then_inc(self.dve_step, 1)
        dve.wait_ge(self.dve_step, self.steps["dve"])

    def after_pool(self, pool, ins):
        self.steps["pool"] += 1
        ins.then_inc(self.pool_step, 1)
        pool.wait_ge(self.pool_step, self.steps["pool"])

    def acc(self, t):
        return self.ps[:, t % NA, :]

    def aux(self, t):
        return self.ps[:, NA + t % NX, :]

    def wait_acc_full(self, eng, t):
        eng.wait_ge(self.acc_full, t + 1)

    def wait_acc_drained(self, eng, t):
        eng.wait_ge(self.acc_drained[t % NA], t // NA + 1)

    def open_acc(self, pe, t):
        if t >= NA:
            self.wait_acc_drained(pe, t - NA)

    def wait_aux_full(self, eng, t):
        eng.wait_ge(self.aux_full, t + 1)

    def wait_aux_drained(self, eng, t):
        eng.wait_ge(self.aux_drained[t % NX], t // NX + 1)

    def open_aux(self, pe, t):
        if t >= NX:
            self.wait_aux_drained(pe, t - NX)

    def weights(self, pe, g):
        pe.wait_ge(self.w_loaded[g % RING], 16 * (g // RING + 1))
        return self.wring[:, g % RING, :]

    def wait_split_used(self, eng, m):
        _, acc, last, used = self.split[m]
        if last:
            self.wait_acc_full(eng, acc)
        else:
            eng.wait_ge(self.split_used, used)

    def convert_hi(self, act, m):
        g = self.split[m][0]
        n = self.units[g][1]
        act.wait_ge(self.w_loaded[g % RING], 16 * (g // RING + 1))
        if m >= SPLIT:
            self.wait_split_used(act, m - SPLIT)
        act.activation(self.w_hi[:, m % SPLIT, 0:n], self.wring[:, g % RING, 0:n], ACT.Copy).then_inc(self.w_hi_ready, 1)

    def convert_lo(self, dve, m):
        g = self.split[m][0]
        n = self.units[g][1]
        dve.wait_ge(self.w_hi_ready, m + 1)
        dve.tensor_tensor(self.w_lo[:, m % SPLIT, 0:n], self.wring[:, g % RING, 0:n],
                          self.w_hi[:, m % SPLIT, 0:n].bitcast(F32), ALU.subtract).then_inc(self.w_lo_ready, 1)

    def split_product(self, pe, out, units, src, wait=False, m=P):
        at = 0
        for u in units:
            g, _, last, _ = self.split[u]
            kc = self.units[g][1] // m
            hi, lo = (w[:, u % SPLIT, 0:kc * m].rearrange("p (c m) -> p c m", m=m) for w in (self.w_hi, self.w_lo))
            pe.wait_ge(self.w_lo_ready, u + 1)
            for c in range(kc):
                if wait:
                    src.wait_hi(pe, at + c)
                pe.matmul(out, hi[:, c, :], src.hi[:, at + c, :], start=(at + c == 0), stop=False)
                pe.matmul(out, lo[:, c, :], src.hi[:, at + c, :], start=False, stop=False)
            for c in range(kc):
                if wait:
                    src.wait_lo(pe, at + c)
                mm = pe.matmul(out, hi[:, c, :], src.lo[:, at + c, :], start=False, stop=(last and c == kc - 1))
            mm.then_inc(self.acc_full if last else self.split_used, 1)
            at += kc

    def vec(self, name, i=0, lo=0, hi=P):
        c = VECS[name] + i
        return self.vecs[lo:hi, c:c + 1]

    def const(self, name, lo=0, hi=P):
        at, n = CONST[name]
        return self.consts[lo:hi, at:at + n]


def row(ap):
    return ap.rearrange("p a b -> p (a b)")


class Stage:
    def __init__(self, k):
        self.k = k
        k.stages.append(self)

    def sync(self, sp):
        pass

    def tensor(self, pe):
        pass

    def vector(self, dve):
        pass

    def scalar(self, act):
        pass

    def gpsimd(self, pool):
        pass


class InverseRoot:

    def __init__(self, k, t, n, eps, floor=False):
        self.k, self.t, self.n, self.eps, self.floor = k, t, n, eps, floor
        self.at = k.reserve("root", 1)

    def take_mean(self, dve):
        k = self.k
        k.wait_acc_full(dve, self.t)
        op = ALU.max if self.floor else ALU.add
        dve.tensor_scalar(k.root_in[:, 0:self.n], k.acc(self.t)[:, 0:self.n], self.eps, None, op).then_inc(
            k.acc_drained[self.t % NA], 1)

    def guess(self, act):
        k, n = self.k, self.n
        k.wait_acc_drained(act, self.t)
        k.after_act(act, act.activation(k.root_ln[:, 0:n], k.root_in[:, 0:n], ACT.Ln))
        act.activation(k.root_y[:, 0:n], k.root_ln[:, 0:n], ACT.Exp, scale=-0.5).then_inc(k.root_ready, 1)

    def refine(self, dve):
        k, n = self.k, self.n
        y, r, m = k.root_y[:, 0:n], k.root[:, 0:n], k.root_in[:, 0:n]
        dve.wait_ge(k.root_ready, self.at + 1)
        k.after_dve(dve, dve.tensor_tensor(r, y, y, ALU.mult))
        k.after_dve(dve, dve.scalar_tensor_tensor(r, r, -0.5, m, ALU.mult, ALU.mult))
        k.after_dve(dve, dve.scalar_tensor_tensor(r, r, 1.5, y, ALU.add, ALU.mult))
        return r


class Norm(Stage):

    def __init__(self, k, src, dst, gain, wait_src, n=S, source=None):
        super().__init__(k)
        self.gradual = source is not None
        if self.gradual:
            source.norm = self
        self.src, self.dst, self.gain, self.wait_src, self.n = src, dst, gain, wait_src, n
        self.t = k.take_acc()
        self.root = InverseRoot(k, self.t, n, EPS)
        self.sq0 = k.reserve("square", DT_)
        self.used0 = k.reserve("used", DT_ - 1)
        self.ready0 = k.reserve("xn", DT_)

    def wait_dst(self, pe, j):
        pe.wait_ge(self.k.xn_ready, self.ready0 + j + 1)

    def square_tile(self, act, j):
        k = self.k
        self.wait_src(act, j)
        if j >= 2:
            act.wait_ge(k.square_used, self.used0 + (max(1, j - 2) if self.gradual else j - 1))
        act.activation(k.square[:, j % 2, 0:self.n], self.src[:, j, :], ACT.Square).then_inc(k.square_ready, 1)

    def scalar(self, act):
        for j in range(DT_ - 1 if self.gradual else 0, DT_):
            self.square_tile(act, j)
        self.root.guess(act)

    def tensor(self, pe):
        k = self.k
        pe.wait_ge(k.const_loaded, 16)
        k.open_acc(pe, self.t)
        if self.gradual:
            pe.wait_ge(k.square_used, self.used0 + DT_ - 1)
            pe.matmul(k.acc(self.t)[:, 0:self.n], k.const("ones"), k.square[:, 3, 0:self.n], start=True,
                      stop=True).then_inc(k.acc_full, 1)
            return
        for j in range(DT_):
            pe.wait_ge(k.square_ready, self.sq0 + j + 1)
            mm = pe.matmul(k.acc(self.t)[:, 0:self.n], k.const("ones"), k.square[:, j % 2, 0:self.n],
                           start=(j == 0), stop=(j == DT_ - 1))
            mm.then_inc(k.square_used if j < DT_ - 1 else k.acc_full, 1)

    def gpsimd(self, pool):
        k, total = self.k, self.k.square[:, 3, 0:self.n]
        for j in range(1, DT_ if self.gradual else 1):
            pool.wait_ge(k.square_ready, self.sq0 + j + 1)
            if j > 1:
                pool.wait_ge(k.square_used, self.used0 + j - 1)
            pool.tensor_tensor(total, k.square[:, 0, 0:self.n] if j == 1 else total, k.square[:, j % 2, 0:self.n],
                               ALU.add).then_inc(k.square_used, 1)

    def vector(self, dve):
        k = self.k
        self.root.take_mean(dve)
        dve.wait_ge(k.vec_loaded, 16)
        r = self.root.refine(dve)
        for j in range(DT_):
            dve.scalar_tensor_tensor(self.dst[:, j, :], self.src[:, j, :], k.vec(self.gain, j), r,
                                     ALU.mult, ALU.mult).then_inc(k.xn_ready, 1)


class Project(Stage):

    def __init__(self, k, outs, src, wait_src, drains, groups=(8,), kind="features", m=P, n=S):
        super().__init__(k)
        self.src, self.wait_src, self.drains, self.groups, self.kind, self.m, self.n = (
            src, wait_src, drains, groups, kind, m, n)
        self.outs = outs
        self.ts, self.us = [], []
        for _ in range(outs):
            t = k.take_acc()
            self.ts.append(t)
            self.us.append([k.take_unit(t, kc * m) for kc in groups])

    def tensor(self, pe):
        k = self.k
        total = sum(self.groups)
        for i, (t, units) in enumerate(zip(self.ts, self.us)):
            k.open_acc(pe, t)
            at = 0
            views = []
            for g, kc in zip(units, self.groups):
                w = k.weights(pe, g)[:, 0:kc * self.m].rearrange("p (c m) -> p c m", m=self.m)
                if self.kind == "features":
                    for c in range(kc):
                        if i == 0:
                            self.wait_src(pe, at + c)
                        mm = pe.matmul(k.acc(t)[0:self.m, 0:self.n], w[:, c, :], self.src(at + c),
                                       start=(at + c == 0), stop=(at + c == total - 1))
                else:
                    views.append(w)
                at += kc
            if self.kind == "tokens":
                w = views[0]
                if i == 0:
                    self.wait_src(pe, total - 1)
                for b in range(self.n // P):
                    for c in range(total):
                        mm = pe.matmul(k.acc(t)[:, b * self.m:(b + 1) * self.m], self.src(c)[:, b * P:(b + 1) * P],
                                       w[:, c, :], start=(c == 0), stop=(c == total - 1))
            mm.then_inc(k.acc_full, 1)

    def run(self, eng, name):
        for t, drain in zip(self.ts, self.drains):
            if name in drain:
                drain[name](eng, t)

    def vector(self, dve):
        self.run(dve, "vector")

    def scalar(self, act):
        self.run(act, "scalar")

    def gpsimd(self, pool):
        self.run(pool, "gpsimd")


class SplitTiles(Stage):

    def __init__(self, k, name, src, hi, lo, wait_src, alone=False):
        super().__init__(k)
        self.alone = alone
        self.src, self.hi, self.lo, self.wait_src = src, hi, lo, wait_src
        self.tiles = src.shape[1]
        self.hi_ready = k.sem(f"{name}_hi_ready")
        self.lo_ready = [k.sem(f"{name}_lo_even_ready"), k.sem(f"{name}_lo_odd_ready")]

    def wait_hi(self, eng, j):
        eng.wait_ge(self.hi_ready, j + 1)

    def wait_lo(self, eng, j):
        eng.wait_ge(self.lo_ready[j % 2], j // 2 + 1)

    def scalar(self, act):
        for j in range(self.tiles):
            self.wait_src(act, j)
            act.activation(self.hi[:, j, :], self.src[:, j, :], ACT.Copy).then_inc(self.hi_ready, 1)

    def rest(self, eng, j):
        self.wait_hi(eng, j)
        eng.tensor_tensor(self.lo[:, j, :], self.src[:, j, :], self.hi[:, j, :].bitcast(F32), ALU.subtract).then_inc(
            self.lo_ready[j % 2], 1)

    def gpsimd(self, pool):
        for j in range(0, self.tiles, 1 if self.alone else 2):
            self.rest(pool, j)

    def vector(self, dve):
        for j in range(1, self.tiles, 2):
            if not self.alone:
                self.rest(dve, j)


class SplitStage(Stage):

    def __init__(self, k, after):
        super().__init__(k)
        self.ts, self.us = [], []
        self.begun, self.then = after is not None, None
        if after is not None:
            after.then = self

    def take(self, n=UNIT, groups=1):
        t = self.k.take_acc()
        self.ts.append(t)
        sizes = [n] if groups == 1 else [kc * P for kc in groups]
        self.us.append([self.k.take_split(t, size, last=(i == len(sizes) - 1)) for i, size in enumerate(sizes)])
        return t

    def tensor(self, pe):
        pass

    def convert_first(self, eng, convert):
        if not self.begun:
            for u in self.us[0]:
                convert(eng, u)

    def convert_next(self, eng, convert, i):
        for u in self.us[i + 1] if i + 1 < len(self.us) else self.then.us[0] if self.then else []:
            convert(eng, u)


class Begin(SplitStage):

    def __init__(self, k):
        super().__init__(k, None)

    def vector(self, dve):
        self.convert_next(dve, self.k.convert_lo, -1)

    def scalar(self, act):
        self.convert_next(act, self.k.convert_hi, -1)


class SplitProject(SplitStage):

    def __init__(self, k, outs, src, drains, groups=1, wait=True, after=None):
        super().__init__(k, after)
        self.src, self.drains, self.wait, self.norm = src, drains, wait, None
        for _ in range(outs):
            self.take(groups=groups)

    def tensor(self, pe):
        k = self.k
        for i, t in enumerate(self.ts):
            k.open_acc(pe, t)
            k.split_product(pe, k.acc(t), self.us[i], self.src, self.wait and i == 0)

    def run(self, eng, name, convert):
        self.convert_first(eng, convert)
        for i, t in enumerate(self.ts):
            self.convert_next(eng, convert, i)
            if name in self.drains[i]:
                self.drains[i][name](eng, t)
            if name == "scalar" and self.norm is not None and i:
                self.norm.square_tile(eng, i - 1)

    def vector(self, dve):
        self.run(dve, "vector", self.k.convert_lo)

    def scalar(self, act):
        self.run(act, "scalar", self.k.convert_hi)


def copy_out(k, dst, scale=1.0, m=P, n=S):
    def scalar(act, t):
        k.wait_acc_full(act, t)
        act.activation(dst, k.acc(t)[0:m, 0:n], ACT.Copy, scale=scale).then_inc(k.acc_drained[t % NA], 1)
    return {"scalar": scalar}


def copy_tokens(k, dst, m, blocks=NT):
    def scalar(act, t):
        k.wait_acc_full(act, t)
        src = k.acc(t)[:, 0:blocks * m].rearrange("p (b m) -> p b m", m=m)
        act.activation(dst, src, ACT.Copy).then_inc(k.acc_drained[t % NA], 1)
    return {"scalar": scalar}


def add_residual(k, x):
    def vector(dve, t):
        k.wait_acc_full(dve, t)
        dve.tensor_tensor(x, x, k.acc(t), ALU.add).then_inc(k.acc_drained[t % NA], 1)
    return {"vector": vector}


class Hidden:

    def __init__(self, k, hi, lo, tmp):
        self.k, self.hi, self.lo, self.tmp = k, hi, lo, tmp
        self.relu_ready = k.sem("mlp_relu_ready")
        self.hi_ready = k.sem("mlp_hi_ready")
        self.squared = k.sem("mlp_squared")
        self.lo_ready = k.sem("mlp_lo_ready")

    def drain(self, n):
        k = self.k
        relu, square = self.tmp[:, n % 2, :], self.tmp[:, 2 + n % 2, :]
        hi, lo = self.hi[n // 8 % 2][:, n % 8, :], self.lo[n // 8 % 2][:, n % 8, :]

        def scalar(act, t):
            k.wait_acc_full(act, t)
            if n >= 2:
                act.wait_ge(self.lo_ready, n - 1)
            act.activation(relu, k.acc(t), ACT.Relu).then_inc(k.acc_drained[t % NA], 1)
            k.wait_acc_drained(act, t)
            act.activation(hi, relu, ACT.Square).then_inc(self.hi_ready, 1)

        def vector(dve, t):
            k.wait_acc_drained(dve, t)
            dve.tensor_tensor(square, relu, relu, ALU.mult).then_inc(self.squared, 1)
            dve.wait_ge(self.squared, n + 1)
            dve.wait_ge(self.hi_ready, n + 1)
            dve.tensor_tensor(lo, square, hi.bitcast(F32), ALU.subtract).then_inc(self.lo_ready, 1)
        return {"scalar": scalar, "vector": vector}

    def group(self, g):
        return HiddenGroup(self, g)


class HiddenGroup:

    def __init__(self, hidden, g):
        self.hidden, self.first = hidden, 8 * g
        self.hi, self.lo = hidden.hi[g % 2], hidden.lo[g % 2]
        self.drains = [hidden.drain(8 * g + i) for i in range(8)]

    def wait_hi(self, eng, j):
        eng.wait_ge(self.hidden.hi_ready, self.first + j + 1)

    def wait_lo(self, eng, j):
        eng.wait_ge(self.hidden.lo_ready, self.first + j + 1)


class Load(Stage):

    def __init__(self, k, x, consts, vecs, weights):
        super().__init__(k)
        self.x, self.consts, self.vecs, self.w = x, consts, vecs, weights

    def sync(self, sp):
        k = self.k
        sp.dma_start(k.x[:, :, :], self.x).then_inc(k.x_loaded, 16)
        sp.dma_start(k.consts[:, :], self.consts).then_inc(k.const_loaded, 16)
        sp.dma_start(k.vecs[:, :], self.vecs).then_inc(k.vec_loaded, 16)
        for g, n, _, _ in k.units:
            if g >= RING:
                _, _, acc, split = k.units[g - RING]
                if split is None:
                    k.wait_acc_full(sp, acc)
                else:
                    sp.wait_ge(k.w_lo_ready, split + 1)
            sp.dma_start(k.wring[:, g % RING, 0:n], self.w[g, :, 0:n]).then_inc(k.w_loaded[g % RING], 16)


class Pool(Stage):

    def __init__(self, k, u, sums, mixed, cat, u_ts):
        super().__init__(k)
        self.u, self.sums, self.mixed, self.cat, self.u_ts = u, sums, mixed, cat, u_ts
        self.ts = [k.take_acc() for _ in range(4)]
        self.g = k.take_unit(self.ts[-1], 4 * P)
        self.mixed_ready = k.sem("pool_mixed_ready")

    def gpsimd(self, pool):
        k, u, s = self.k, self.u, self.sums
        pool.memset(s[:, :, 0:16], 0.0)
        k.after_pool(pool, pool.memset(u[:, :, 0:16], 0.0))
        for g in range(4):
            k.wait_acc_drained(pool, self.u_ts[g])
            src = u[:, g, :]
            for r in range(g + 1):
                sh = 1 << r
                dst = s[:, r % 2, :]
                k.after_pool(pool, pool.tensor_tensor(dst[:, 16:], src[:, 16:], src[:, 16 - sh:16 + S - sh], ALU.add))
                src = dst
            w = 2 << g
            mean = s[:, (g + 1) % 2, :]
            k.after_pool(pool, pool.tensor_scalar(mean[:, 16:], src[:, 16:], 1.0 / w, None, ALU.mult))
            if g == 0:
                pool.wait_ge(k.const_loaded, 16)
            inv = k.const("inv_count")[:, 16 * g:16 * g + 16]
            k.after_pool(pool, pool.tensor_tensor(mean[:, 16:32], src[:, 16:32], inv, ALU.mult))
            pool.tensor_tensor(self.mixed[:, g, :], mean[:, 16:], u[:, g, 16:], ALU.subtract).then_inc(
                self.mixed_ready, 1)
            pool.wait_ge(self.mixed_ready, g + 1)

    def tensor(self, pe):
        k = self.k
        w = k.weights(pe, self.g)
        for g, t in enumerate(self.ts):
            pe.wait_ge(self.mixed_ready, g + 1)
            k.open_acc(pe, t)
            pe.matmul(k.acc(t), w[:, g * P:(g + 1) * P], self.mixed[:, g, :], start=True, stop=True).then_inc(
                k.acc_full, 1)

    def scalar(self, act):
        k = self.k
        act.wait_ge(k.vec_loaded, 16)
        for g, t in enumerate(self.ts):
            k.wait_acc_full(act, t)
            act.activation(self.cat[:, 4 + g, :], k.acc(t), ACT.Copy, scale=k.vec("pool_scale", g)).then_inc(
                k.acc_drained[t % NA], 1)


class Head:

    def __init__(self, q, keys, values, table, lo, gate=None, compressed=None, last=True, ready=()):
        self.q, self.keys, self.values, self.table, self.lo = q, keys, values, table, lo
        self.gate, self.compressed, self.last, self.ready = gate, compressed, last, ready


TRI = [0, 128, 384, 768]
TRI_N = 1280
COL = [0, 512, 896, 1152]


class Attention(Stage):

    def __init__(self, k, name, heads, dst, buf):
        super().__init__(k)
        self.heads, self.dst, self.b = heads, dst, buf
        self.aux0 = k.n_aux
        sem = lambda s: k.sem(f"{name}_{s}")
        self.s_full = sem("scores_full")
        self.s_drained = sem("scores_drained")
        self.max_ready = sem("max_ready")
        self.p_ready = sem("probs_ready")
        self.scaled = sem("probs_scaled")
        self.t_full = sem("probs_t_full")
        self.t_drained = sem("probs_t_drained")
        self.pv_done = sem("values_done")
        self.t_at, self.pair, self.pv_at = [], [], []
        t = v = 0
        fresh = True
        for h in heads:
            self.t_at.append(t)
            t += 3 if h.compressed is None else 4
            if fresh and h.lo == 0:
                acc = k.take_acc()
            h.first = fresh
            fresh = h.last
            self.pair.append(acc)
            h.closes = h.last and h.lo == HD
            self.pv_at.append(v)
            v += 0 if h.closes else 1

    def wait_values_done(self, eng, u):
        if self.heads[u].closes:
            self.k.wait_acc_full(eng, self.pair[u])
        else:
            eng.wait_ge(self.pv_done, self.pv_at[u] + 1)

    def scores(self, pe, u):
        k, h = self.k, self.heads[u]
        for wait in h.ready:
            wait(pe)
        for i in range(NT):
            s = NT * u + i
            n = P * (i + 1)
            if s >= 3:
                pe.wait_ge(self.s_drained, s - 2)
            pe.matmul(k.ps[:, 3 + s % 3, 0:n], h.q[:, i * P:(i + 1) * P], h.keys[:, 0:n],
                      start=True, stop=True).then_inc(self.s_full, 1)

    def open_t(self, pe, t):
        if t >= 2:
            pe.wait_ge(self.t_drained, t - 1)
        return self.k.ps[:, 6 + t % 2, :]

    def compressed_t(self, pe, u):
        k, h = self.k, self.heads[u]
        out = self.open_t(pe, self.t_at[u])
        for i in range(NT):
            mm = pe.transpose(out[0:NCMP, i * P:(i + 1) * P], h.compressed[0][:, i * NCMP:(i + 1) * NCMP],
                              k.const("ident"))
        mm.then_inc(self.t_full, 1)

    def probs_t(self, pe, u):
        h = self.heads[u]
        pe.wait_ge(self.scaled, u + 1)
        p, ident = self.b.p[:, u % 3, :], self.k.const("ident")
        for part, blocks in enumerate(((0,), (1,), (2, 3))):
            out = self.open_t(pe, self.t_at[u] + (h.compressed is not None) + part)
            for j in blocks:
                for i in range(j, NT):
                    at = COL[j] - COL[blocks[0]] + (i - j) * P
                    mm = pe.transpose(out[:, at:at + P], p[:, TRI[i] + j * P:TRI[i] + (j + 1) * P], ident)
            mm.then_inc(self.t_full, 1)

    def values(self, pe, u):
        k, h = self.k, self.heads[u]
        acc = self.pair[u]
        if h.first and h.lo == 0:
            k.open_acc(pe, acc)
        out = k.acc(acc)[h.lo:h.lo + HD, :]
        pt = self.b.pt[:, u % 2, :]
        t = self.t_at[u]
        if h.compressed is not None:
            pe.wait_ge(self.t_drained, t + 1)
            pe.matmul(out, h.compressed[1], self.b.ct[:, 0:S], start=True, stop=False)
            t += 1
        for j in range(NT):
            if j < 3:
                pe.wait_ge(self.t_drained, t + j + 1)
            mm = pe.matmul(out[:, j * P:S], h.values(j), pt[:, COL[j]:COL[j] + S - j * P],
                           start=(h.first and h.compressed is None and j == 0), stop=(h.last and j == NT - 1))
        mm.then_inc(k.acc_full if h.closes else self.pv_done, 1)

    def tensor(self, pe):
        n = len(self.heads)
        for t in range(max(0, self.aux0 - NX), self.aux0):
            self.k.wait_aux_drained(pe, t)
        self.scores(pe, 0)
        self.scores(pe, 1)
        for u in range(n):
            if u + 2 < n:
                self.scores(pe, u + 2)
            if u >= 1:
                self.values(pe, u - 1)
            if self.heads[u].compressed is not None:
                self.compressed_t(pe, u)
            self.probs_t(pe, u)
        self.values(pe, n - 1)

    def add_bias(self, dve, u):
        k, h = self.k, self.heads[u]
        p, mx = self.b.p[:, u % 3, :], self.b.max[:, u % 3, :]
        if u >= 3:
            dve.wait_ge(self.t_full, self.t_at[u - 2])
        for i in range(NT):
            s = NT * u + i
            n = P * (i + 1)
            dve.wait_ge(self.s_full, s + 1)
            dve.tensor_tensor_reduce(p[:, TRI[i]:TRI[i] + n], k.ps[:, 3 + s % 3, 0:n], h.table[:, S - n:S],
                                     1.0, -3e38, ALU.add, ALU.max, mx[:, i:i + 1]).then_inc(self.s_drained, 1)
        dve.wait_ge(self.s_drained, NT * (u + 1))
        dve.tensor_scalar(self.b.negmax[:, u % 3, :], mx, -1.0, None, ALU.mult).then_inc(self.max_ready, 1)

    def scale(self, dve, u):
        k, h = self.k, self.heads[u]
        dve.wait_ge(self.p_ready, u + 1)
        inv = self.b.inv[:, u % 3, :]
        k.after_dve(dve, dve.reciprocal(inv, self.b.sum[:, u % 3, :]))
        if h.gate is not None:
            gated = self.b.inv[:, 3 + u % 3, :]
            k.after_dve(dve, dve.tensor_tensor(gated, inv, h.gate, ALU.mult))
            inv = gated
        p = self.b.p[:, u % 3, :]
        for i in range(NT):
            seg = p[:, TRI[i]:TRI[i] + P * (i + 1)]
            last = dve.tensor_scalar(seg, seg, inv[:, i:i + 1], None, ALU.mult)
        last.then_inc(self.scaled, 1)

    def drain(self, dve, u):
        k = self.k
        t = self.pair[u]
        k.wait_acc_full(dve, t)
        dve.tensor_copy(self.dst(u), k.acc(t)).then_inc(k.acc_drained[t % NA], 1)

    def vector(self, dve):
        n = len(self.heads)
        self.add_bias(dve, 0)
        self.add_bias(dve, 1)
        self.scale(dve, 0)
        for u in range(n):
            if u + 2 < n:
                self.add_bias(dve, u + 2)
            if u + 1 < n:
                self.scale(dve, u + 1)
            if u >= 2 and self.heads[u - 2].closes:
                self.drain(dve, u - 2)
        for u in (n - 2, n - 1):
            if self.heads[u].closes:
                self.drain(dve, u)

    def exps(self, act, u):
        p, nm, rs = self.b.p[:, u % 3, :], self.b.negmax[:, u % 3, :], self.b.sum[:, u % 3, :]
        act.wait_ge(self.max_ready, u + 1)
        if u >= 3:
            act.wait_ge(self.scaled, u - 2)
        for i in range(NT):
            at, n = TRI[i], P * (i + 1)
            e = act.activation(p[:, at:at + n], p[:, at:at + n], ACT.Exp, bias=nm[:, i:i + 1], accum_out=rs[:, i:i + 1])
        e.then_inc(self.p_ready, 1)

    def move_t(self, act, u, part):
        k = self.k
        c = self.heads[u].compressed is not None
        t = self.t_at[u] + c + part
        if part == 0 and u >= 2:
            self.wait_values_done(act, u - 2)
        if part == -1 and u >= 1:
            self.wait_values_done(act, u - 1)
        act.wait_ge(self.t_full, t + 1)
        if part == -1:
            src, dst = k.ps[0:NCMP, 6 + t % 2, :], self.b.ct
        else:
            at, n = ((0, 512), (512, 384), (896, 384))[part]
            src, dst = k.ps[:, 6 + t % 2, 0:n], self.b.pt[:, u % 2, at:at + n]
        act.activation(dst, src, ACT.Copy).then_inc(self.t_drained, 1)

    def scalar(self, act):
        n = len(self.heads)
        self.exps(act, 0)
        for u in range(n):
            if u + 1 < n:
                self.exps(act, u + 1)
            if self.heads[u].compressed is not None:
                self.move_t(act, u, -1)
            for part in range(3):
                self.move_t(act, u, part)


class CompressedSoftmax(Stage):

    def __init__(self, k, q, keys, table, gates, mx, wait_q, waits):
        super().__init__(k)
        self.q, self.keys, self.table, self.gates, self.mx, self.wait_q, self.waits = (
            q, keys, table, gates, mx, wait_q, waits)
        self.ts = [k.take_acc() for _ in range(4)]
        self.shifted = k.sem("compressed_shifted")
        self.p_ready = k.sem("compressed_probs")
        self.done = k.sem("compressed_scaled")

    def tensor(self, pe):
        k = self.k
        self.waits(pe)
        for half in range(2):
            banks = self.ts[2 * half:2 * half + 2]
            for t in banks:
                k.open_acc(pe, t)
            for j in range(4):
                pair = 4 * half + j
                self.wait_q(pe, pair)
                g = pair // 2
                slot = (g % 2) * 2 + g // 2
                for i in range(NT):
                    for e in range(2):
                        at = (j * NT + i) * NCMP
                        mm = pe.matmul(k.acc(banks[e])[:, at:at + NCMP],
                                       self.q[e * HD:(e + 1) * HD, pair, i * P:(i + 1) * P],
                                       self.keys[e * HD:(e + 1) * HD, slot * NCMP:(slot + 1) * NCMP],
                                       start=True, stop=True)
                        if j == 3 and i == NT - 1:
                            mm.then_inc(k.acc_full, 1)

    def vector(self, dve):
        k, n = self.k, HQ * NT
        for b, t in enumerate(self.ts):
            k.wait_acc_full(dve, t)
            x = self.table[:, 8 * (b // 2) + b % 2:8 * (b // 2) + 8:2, :]
            dve.tensor_tensor(x, x, k.acc(t)[:, 0:4 * NT * NCMP].rearrange("p (h n) -> p h n", h=4), ALU.add).then_inc(k.acc_drained[t % NA], 1)
        for t in self.ts:
            k.wait_acc_drained(dve, t)
        x = self.table.rearrange("p h (i n) -> p (h i) n", n=NCMP)
        m = self.mx[:, 0, :]
        k.after_dve(dve, dve.tensor_reduce(m, x, AX.X, ALU.max))
        k.after_dve(dve, dve.tensor_scalar(m, m, NEG * 1e-10, None, ALU.max))
        dve.tensor_tensor(x, x, m.unsqueeze(2).to_broadcast([P, n, NCMP]), ALU.subtract).then_inc(self.shifted, 1)
        dve.wait_ge(self.p_ready, 1)
        k.after_dve(dve, dve.tensor_reduce(m, x, AX.X, ALU.add))
        k.after_dve(dve, dve.tensor_scalar(m, m, 1e-30, None, ALU.max))
        inv = self.mx[:, 1, :]
        k.after_dve(dve, dve.reciprocal(inv, m))
        gate = self.gates.rearrange("p i (h b) -> p h i b", b=3)[:, :, :, 0]
        k.after_dve(dve, dve.tensor_tensor(self.mx[:, 0, :].rearrange("p (h i) -> p h i", i=NT),
                                           inv.rearrange("p (h i) -> p h i", i=NT), gate, ALU.mult))
        dve.tensor_tensor(x, x, m.unsqueeze(2).to_broadcast([P, n, NCMP]), ALU.mult).then_inc(self.done, 1)

    def scalar(self, act):
        act.wait_ge(self.shifted, 1)
        x = row(self.table)
        act.activation(x, x, ACT.Exp).then_inc(self.p_ready, 1)


class ProjectNorm(Stage):

    def __init__(self, k, outs, src, wait_src, raw, dst, gain, mean, span=1, n=S, eps=EPS):
        super().__init__(k)
        self.outs, self.src, self.wait_src, self.raw, self.dst, self.gain, self.mean, self.span, self.n = (
            outs, src, wait_src, raw, dst, gain, mean, span, n)
        self.ts, self.us, self.mt, self.roots = [], [], [], []
        for i in range(outs + 1):
            if i < outs:
                t = k.take_acc()
                self.ts.append(t)
                self.us.append(k.take_unit(t))
            if i >= 1 and i % span == 0:
                self.mt.append(k.take_acc())
                self.roots.append(InverseRoot(k, self.mt[-1], n, eps))
        self.sq0 = k.reserve("square", outs)
        self.ready0 = k.reserve("xn", outs)

    def wait_dst(self, eng, i):
        eng.wait_ge(self.k.xn_ready, self.ready0 + i + 1)

    def tensor(self, pe):
        k = self.k
        for i in range(self.outs + 1):
            if i < self.outs:
                t = self.ts[i]
                k.open_acc(pe, t)
                w = k.weights(pe, self.us[i]).rearrange("p (c m) -> p c m", m=P)
                for c in range(DT_):
                    if i == 0:
                        self.wait_src(pe, c)
                    mm = pe.matmul(k.acc(t)[:, 0:self.n], w[:, c, :], self.src(c), start=(c == 0), stop=(c == DT_ - 1))
                mm.then_inc(k.acc_full, 1)
            if i >= 1 and i % self.span == 0:
                t = self.mt[i // self.span - 1]
                k.open_acc(pe, t)
                for r in range(self.span):
                    j = i - self.span + r
                    pe.wait_ge(k.square_ready, self.sq0 + j + 1)
                    mm = pe.matmul(k.acc(t)[:, 0:self.n], k.const(self.mean), k.square[:, j % 4, 0:self.n],
                                   start=(r == 0), stop=(r == self.span - 1))
                mm.then_inc(k.acc_full, 1)

    def scalar(self, act):
        k = self.k
        for i in range(self.outs + 1):
            if i < self.outs:
                t = self.ts[i]
                k.wait_acc_full(act, t)
                act.activation(self.raw(i), k.acc(t)[:, 0:self.n], ACT.Copy)
                if i >= 4:
                    k.wait_acc_full(act, self.mt[(i - 4) // self.span])
                act.activation(k.square[:, i % 4, 0:self.n], k.acc(t)[:, 0:self.n], ACT.Square).then_inc(
                    k.square_ready, 1)
                act.wait_ge(k.square_ready, self.sq0 + i + 1)
                act.nop().then_inc(k.acc_drained[t % NA], 1)
            if i >= 1 and i % self.span == 0:
                self.roots[i // self.span - 1].guess(act)

    def vector(self, dve):
        k = self.k
        for a, root in enumerate(self.roots):
            root.take_mean(dve)
            r = root.refine(dve)
            for i in range(a * self.span, (a + 1) * self.span):
                dve.scalar_tensor_tensor(self.dst(i), self.raw(i), self.gain(i), r, ALU.mult, ALU.mult).then_inc(
                    k.xn_ready, 1)


class Tables:

    SHARE = 3

    def __init__(self, k, rows, wide, comp):
        self.k = k
        self.rows, self.wide, self.comp = rows, wide, comp
        self.cleared = k.sem("wide_table_cleared")
        self.hi_moved = k.sem("table_hi_moved")
        self.banks = []
        for c0 in range(S // 2, S, 16):
            self.banks.append((wide[:, :, c0:c0 + 16], [OH_OFF + (S - P) - c for c in range(c0, c0 + 16)]))
        for i in range(NT):
            for c0, c1 in ((0, 16), (16, NCMP)):
                self.banks.append((comp[:, :, i * NCMP + c0:i * NCMP + c1],
                                   [OH_OFF - 31 + P * i - 16 * c for c in range(c0, c1)]))
        self.ts = []

    def take(self):
        self.ts += [self.k.take_acc() for _ in range(self.SHARE)]

    def share(self, i):
        return [(n, self.ts[n]) + self.banks[n] for n in range(self.SHARE * i, self.SHARE * (i + 1))]

    def tensor(self, pe, i):
        k = self.k
        if i == 0:
            pe.wait_ge(self.rows.ready, 2)
        for _, t, _, starts in self.share(i):
            k.open_acc(pe, t)
            for c, x0 in enumerate(starts):
                mm = pe.matmul(k.acc(t)[:, 2 * c * HQ:2 * (c + 1) * HQ], self.rows.hot[:, x0:x0 + P],
                               self.rows.rows[:, :], start=True, stop=True)
            mm.then_inc(k.acc_full, 1)

    def vector(self, dve, i):
        k = self.k
        if i == 0:
            dve.memset(self.wide[:, :, 0:S // 2], 0.0).then_inc(self.cleared, 1)
        for n, t, dst, starts in self.share(i):
            dve.wait_ge(self.hi_moved, n + 1)
            dve.tensor_tensor(dst, dst, self.part(t, starts, 1), ALU.add).then_inc(k.acc_drained[t % NA], 1)

    def scalar(self, act, i):
        k = self.k
        for _, t, dst, starts in self.share(i):
            k.wait_acc_full(act, t)
            act.activation(dst, self.part(t, starts, 0), ACT.Copy).then_inc(self.hi_moved, 1)

    def part(self, t, starts, half):
        return self.k.acc(t)[:, 0:2 * len(starts) * HQ].rearrange("p (c s h) -> p s h c", s=2, h=HQ)[:, half]


class SplitProjectNorm(SplitStage):

    def __init__(self, k, outs, src, raw, dst, gain, mean, span=1, after=None, tables=None):
        super().__init__(k, after)
        self.tables = tables
        self.outs, self.src, self.raw, self.dst, self.gain, self.mean, self.span = outs, src, raw, dst, gain, mean, span
        self.mt, self.roots = [], []
        for i in range(outs + 1):
            if i < outs:
                self.take()
                if tables:
                    tables.take()
            if i >= 1 and i % span == 0:
                self.mt.append(k.take_acc())
                self.roots.append(InverseRoot(k, self.mt[-1], S, EPS))
        self.sq0 = k.reserve("square", outs)
        self.ready0 = k.reserve("xn", outs)

    def wait_dst(self, eng, i):
        eng.wait_ge(self.k.xn_ready, self.ready0 + i + 1)

    def tensor(self, pe):
        k = self.k
        for i in range(self.outs + 1):
            if i < self.outs:
                k.open_acc(pe, self.ts[i])
                k.split_product(pe, k.acc(self.ts[i]), self.us[i], self.src, wait=(i == 0))
                if self.tables:
                    self.tables.tensor(pe, i)
            if i >= 1 and i % self.span == 0:
                t = self.mt[i // self.span - 1]
                k.open_acc(pe, t)
                for r in range(self.span):
                    j = i - self.span + r
                    pe.wait_ge(k.square_ready, self.sq0 + j + 1)
                    mm = pe.matmul(k.acc(t), k.const(self.mean), k.square[:, j % 4, :], start=(r == 0),
                                   stop=(r == self.span - 1))
                mm.then_inc(k.acc_full, 1)

    def scalar(self, act):
        k = self.k
        self.convert_first(act, k.convert_hi)
        for i in range(self.outs + 1):
            if i < self.outs:
                self.convert_next(act, k.convert_hi, i)
                t = self.ts[i]
                k.wait_acc_full(act, t)
                act.activation(self.raw(i), k.acc(t), ACT.Copy)
                if i >= 4:
                    k.wait_acc_full(act, self.mt[(i - 4) // self.span])
                act.activation(k.square[:, i % 4, :], k.acc(t), ACT.Square).then_inc(k.square_ready, 1)
                act.wait_ge(k.square_ready, self.sq0 + i + 1)
                act.nop().then_inc(k.acc_drained[t % NA], 1)
                if self.tables:
                    self.tables.scalar(act, i)
            if i >= 1 and i % self.span == 0:
                self.roots[i // self.span - 1].guess(act)

    def vector(self, dve):
        k = self.k
        self.convert_first(dve, k.convert_lo)
        for i in range(self.outs + 1):
            if i < self.outs:
                self.convert_next(dve, k.convert_lo, i)
                if self.tables:
                    self.tables.vector(dve, i)
            if i >= 1 and i % self.span == 0:
                root = self.roots[i // self.span - 1]
                root.take_mean(dve)
                r = root.refine(dve)
                for j in range(i - self.span, i):
                    dve.scalar_tensor_tensor(self.dst(j), self.raw(j), self.gain(j), r, ALU.mult, ALU.mult).then_inc(
                        k.xn_ready, 1)


class TableRows(Stage):

    def __init__(self, k, rel, rel_last, bucket, tab, hot_in, hot, rows, wait_free):
        super().__init__(k)
        self.rel, self.rel_last, self.bucket, self.tab, self.hot_in, self.hot, self.rows, self.wait_free = (
            rel, rel_last, bucket, tab, hot_in, hot, rows, wait_free)
        self.loaded = k.sem("rel_bias_loaded")
        self.loaded2 = k.sem("rel_last_loaded")
        self.hot_loaded = k.sem("one_hot_loaded")
        self.tab_ready = k.sem("bias_rows_ready")
        self.hi_ready = k.sem("bias_rows_hi_ready")
        self.ready = k.sem("table_operands_ready")

    def gpsimd(self, pool):
        self.wait_free(pool)
        pool.dma_start(self.tab[0:BUCKETS, 0, :], self.rel).then_inc(self.loaded, 16)
        pool.dma_start(self.tab[0:BUCKETS, 1, :], self.rel_last).then_inc(self.loaded2, 16)
        pool.dma_start(self.hot_in, self.bucket).then_inc(self.hot_loaded, 16)

    def vector(self, dve):
        t = self.tab
        dve.wait_ge(self.loaded, 16)
        dve.wait_ge(self.loaded2, 16)
        dve.tensor_tensor(t[0:BUCKETS, 2, :], t[0:BUCKETS, 0, :], t[0:BUCKETS, 1, :], ALU.subtract).then_inc(
            self.tab_ready, 1)
        dve.memset(t[BUCKETS:BUCKETS + 1, 2, :], NEG).then_inc(self.tab_ready, 1)
        dve.wait_ge(self.hi_ready, 1)
        dve.tensor_tensor(self.rows[:, HQ:2 * HQ], t[:, 2, :], self.rows[:, 0:HQ].bitcast(F32), ALU.subtract).then_inc(
            self.ready, 1)

    def scalar(self, act):
        act.wait_ge(self.tab_ready, 2)
        act.activation(self.rows[:, 0:HQ], self.tab[:, 2, :], ACT.Copy).then_inc(self.hi_ready, 1)
        act.wait_ge(self.hot_loaded, 16)
        act.activation(self.hot[:, :], self.hot_in, ACT.Copy).then_inc(self.ready, 1)


class Compress(Stage):

    def __init__(self, k, src, swapped, raw_ready, staged, raw, tmp, hid, keys_raw, keys, values):
        super().__init__(k)
        self.src, self.swapped, self.raw_ready, self.staged = src, swapped, raw_ready, staged
        self.raw, self.tmp, self.hid = raw, tmp, hid
        self.keys_raw, self.keys, self.values = keys_raw, keys, values
        self.swap_done = [k.sem(f"halves_swapped_{n}") for n in "kv"]
        self.staged_ready = k.sem("blocks_ready")
        self.tanh_in = k.sem("gelu_inner_ready")
        self.tanh_out = k.sem("gelu_tanh_ready")
        self.hid_ready = k.sem("hidden_ready")
        self.ht, self.hu = [], []
        for _ in range(2):
            self.ht.append(k.take_acc())
            self.hu.append([k.take_unit(self.ht[-1]) for _ in range(4)])
        self.tt = [k.take_acc() for _ in range(2)]
        self.kt, self.mt, self.vt = k.take_acc(), k.take_acc(), k.take_acc()
        self.u2 = k.take_unit(self.vt, 384)
        self.root = InverseRoot(k, self.mt, 124, EPS)
        self.sq0 = k.reserve("square", 1)
        self.ready0 = k.reserve("xn", 1)

    def gpsimd(self, pool):
        for b in range(2):
            self.raw_ready(pool, b)
            for e in range(2):
                pool.dma_start(self.swapped[b][(1 - e) * HD:(2 - e) * HD], self.src[b][e * HD:(e + 1) * HD]).then_inc(
                    self.swap_done[b], 16)

    def vector(self, dve):
        k = self.k
        for b in range(2):
            self.raw_ready(dve, b)
            first = VECS[("pe_k", "pe_v")[b]]
            for swap in range(2):
                if swap:
                    dve.wait_ge(self.swap_done[b], 32)
                for parity in range(2):
                    e = parity ^ swap
                    at = slice(parity * HD, (parity + 1) * HD)
                    src = (self.src, self.swapped)[swap][b][at]
                    for tl in range(2):
                        for late in range(2):
                            i0 = src[:, tl, 16 * late:16 * late + 16 * NCMP].rearrange("p (n l) -> p l n", l=16)
                            c = first + 16 * late + parity
                            i1 = k.vecs[at, c:c + 15:2].unsqueeze(2).to_broadcast([HD, 8, NCMP])
                            slot = (2 * e + tl) * NCMP
                            dve.tensor_tensor(self.staged[b][at, 8 * late:8 * late + 8, slot:slot + NCMP],
                                              i0[:, parity::2, :], i1, ALU.add).then_inc(self.staged_ready, 1)
        for b in range(2):
            x, t = self.raw[:, b, :], self.tmp[:, b, :]
            k.wait_acc_drained(dve, self.ht[b])
            k.after_dve(dve, dve.tensor_tensor(t, x, x, ALU.mult))
            k.after_dve(dve, dve.tensor_scalar(t, t, 0.044715, 1.0, ALU.mult, ALU.add))
            dve.tensor_tensor(t, t, x, ALU.mult).then_inc(self.tanh_in, 1)
        for b in range(2):
            x, t = self.raw[:, b, :], self.tmp[:, b, :]
            dve.wait_ge(self.tanh_out, b + 1)
            k.after_dve(dve, dve.scalar_tensor_tensor(t, t, 1.0, x, ALU.add, ALU.mult))
            dve.tensor_scalar(x, t, 0.5, None, ALU.mult).then_inc(self.hid_ready, 1)
        self.root.take_mean(dve)
        r = self.root.refine(dve)
        dve.scalar_tensor_tensor(self.keys, self.keys_raw, k.vec("k_gain", 0), r, ALU.mult, ALU.mult).then_inc(
            k.xn_ready, 1)

    def scalar(self, act):
        k = self.k
        for b in range(2):
            t = self.ht[b]
            k.wait_acc_full(act, t)
            act.activation(self.raw[:, b, :], k.acc(t)[0:124, 0:256], ACT.Copy).then_inc(k.acc_drained[t % NA], 1)
        for b in range(2):
            act.wait_ge(self.tanh_in, b + 1)
            t = self.tmp[:, b, :]
            act.activation(t, t, ACT.Tanh, scale=float(np.sqrt(2 / np.pi))).then_inc(self.tanh_out, 1)
        for b, t in enumerate(self.tt):
            k.wait_acc_full(act, t)
            act.activation(self.hid[:, b, :], k.acc(t)[:, 0:248], ACT.Copy).then_inc(k.acc_drained[t % NA], 1)
        k.wait_acc_full(act, self.kt)
        act.activation(self.keys_raw, k.acc(self.kt)[:, 0:124], ACT.Copy)
        act.activation(k.square[:, 0, 0:124], k.acc(self.kt)[:, 0:124], ACT.Square).then_inc(k.square_ready, 1)
        act.wait_ge(k.square_ready, self.sq0 + 1)
        act.nop().then_inc(k.acc_drained[self.kt % NA], 1)
        self.root.guess(act)
        k.wait_acc_full(act, self.vt)
        act.activation(self.values, k.acc(self.vt)[0:NCMP, 0:256].rearrange("p (g d) -> p g d", d=HD),
                       ACT.Copy).then_inc(k.acc_drained[self.vt % NA], 1)

    def wait_done(self, eng):
        eng.wait_ge(self.k.xn_ready, self.ready0 + 1)
        self.k.wait_acc_drained(eng, self.vt)

    def tensor(self, pe):
        k = self.k
        for b, t in enumerate(self.ht):
            k.open_acc(pe, t)
            pe.wait_ge(self.staged_ready, 16 * (b + 1))
            for u in range(4):
                w = k.weights(pe, self.hu[b][u]).rearrange("p (l c) -> p l c", c=256)
                for l in range(4):
                    mm = pe.matmul(k.acc(t)[0:124, 0:256], self.staged[b][:, 4 * u + l, :], w[:, l, :],
                                   start=(u == 0 and l == 0), stop=(u == 3 and l == 3))
            mm.then_inc(k.acc_full, 1)
        for b, t in enumerate(self.tt):
            k.open_acc(pe, t)
            pe.wait_ge(self.hid_ready, b + 1)
            for ch in range(2):
                mm = pe.transpose(k.acc(t)[:, ch * 124:(ch + 1) * 124], self.raw[:, b, ch * P:(ch + 1) * P],
                                  k.const("ident")[0:124, 0:124])
            mm.then_inc(k.acc_full, 1)
        w = k.weights(pe, self.u2)
        wk = w[:, 0:256].rearrange("p (c m) -> p c m", c=2)
        wv = w[:, 256:384].rearrange("p (c m) -> p c m", c=2)
        k.wait_acc_drained(pe, self.tt[0])
        k.open_acc(pe, self.kt)
        for ch in range(2):
            mm = pe.matmul(k.acc(self.kt)[:, 0:124], wk[:, ch, :], self.hid[:, 0, ch * 124:(ch + 1) * 124],
                           start=(ch == 0), stop=(ch == 1))
        mm.then_inc(k.acc_full, 1)
        k.open_acc(pe, self.mt)
        pe.wait_ge(k.square_ready, self.sq0 + 1)
        pe.matmul(k.acc(self.mt)[:, 0:124], k.const("head_mean"), k.square[:, 0, 0:124], start=True,
                  stop=True).then_inc(k.acc_full, 1)
        k.open_acc(pe, self.vt)
        k.wait_acc_drained(pe, self.tt[1])
        for g in range(4):
            for ch in range(2):
                at = ch * 124 + g * NCMP
                mm = pe.matmul(k.acc(self.vt)[0:NCMP, g * HD:(g + 1) * HD], self.hid[:, 1, at:at + NCMP], wv[:, ch, :],
                               start=(ch == 0), stop=(ch == 1))
        mm.then_inc(k.acc_full, 1)


class Spread(Stage):

    def __init__(self, k, src, dst, waits):
        super().__init__(k)
        self.src, self.dst, self.waits = src, dst, waits
        self.done = k.sem("keys_spread")

    def gpsimd(self, pool):
        for b in range(2):
            for g in range(NKV):
                self.waits[b](pool, g // 2)
                e = g % 2
                for half in range(2):
                    pool.dma_start(self.dst[b][half * HD:(half + 1) * HD, g, :],
                                   self.src[b][e * HD:(e + 1) * HD, g // 2, :]).then_inc(self.done, 16)

    def wait_done(self, eng):
        eng.wait_ge(self.done, 16 * 16)


class Gates(Stage):

    def __init__(self, k, g, wait):
        super().__init__(k)
        self.g, self.wait = g, wait
        self.ready = k.sem("gates_ready")

    def vector(self, dve):
        self.wait(dve)
        dve.tensor_scalar(row(self.g), row(self.g), 0.5, 0.5, ALU.mult, ALU.add).then_inc(self.ready, 1)
        dve.wait_ge(self.ready, 1)


class Gated(SplitStage):

    def __init__(self, k, y, xn, merged, tanh, first, wait_merged=None, after=None):
        super().__init__(k, after)
        self.y, self.xn, self.merged, self.tanh, self.first, self.wait_merged = y, xn, merged, tanh, first, wait_merged
        for _ in range(2 * DT_):
            self.take()
        self.gt, self.bt = self.ts[0::2], self.ts[1::2]

    def tensor(self, pe):
        k = self.k
        for i, t in enumerate(self.ts):
            k.open_acc(pe, t)
            k.split_product(pe, k.acc(t), self.us[i], (self.xn, self.y)[i % 2], wait=(i < 2))

    def scalar(self, act):
        k = self.k
        self.convert_first(act, k.convert_hi)
        for m, t in enumerate(self.gt):
            self.convert_next(act, k.convert_hi, 2 * m)
            k.wait_acc_full(act, t)
            if m >= 2:
                if self.first:
                    k.wait_acc_drained(act, self.bt[m - 2])
                else:
                    act.wait_ge(k.merged_ready, m - 1)
            act.activation(self.tanh[:, m % 2, :], k.acc(t), ACT.Tanh, scale=0.5).then_inc(k.acc_drained[t % NA], 1)
            self.convert_next(act, k.convert_hi, 2 * m + 1)

    def vector(self, dve):
        k = self.k
        self.convert_first(dve, k.convert_lo)
        if self.wait_merged:
            self.wait_merged(dve)
        for m, t in enumerate(self.bt):
            self.convert_next(dve, k.convert_lo, 2 * m)
            self.convert_next(dve, k.convert_lo, 2 * m + 1)
            k.wait_acc_full(dve, t)
            k.wait_acc_drained(dve, self.gt[m])
            g = self.tanh[:, m % 2, :]
            dst = self.merged[:, m, :] if self.first else g
            ins = dve.scalar_tensor_tensor(dst, g, 1.0, k.acc(t), ALU.add, ALU.mult).then_inc(k.acc_drained[t % NA], 1)
            if not self.first:
                k.wait_acc_drained(dve, t)
                dve.tensor_tensor(self.merged[:, m, :], self.merged[:, m, :], g, ALU.add).then_inc(k.merged_ready, 1)


class RwkvInputs(SplitStage):

    ORDER = 27

    def __init__(self, k, xn, rkv, zwa, zg, shift, before, after=None):
        super().__init__(k, after)
        self.xn, self.rkv, self.zwa, self.zg, self.shift, self.before = xn, rkv, zwa, zg, shift, before
        self.m = [P] * 26 + [32]
        for m in self.m:
            self.take(DT_ * m)
        self.padded = k.sem("shift_padded")
        self.done = k.sem("shifted")
        self.zg_ready = k.sem("zg_ready")
        self.zwa_ready = k.sem("zwa_ready")

    def dst(self, i):
        if i < 24:
            return self.rkv[i // 8][:, i % 8, :]
        if i == 24:
            return self.zwa
        return self.zg[0:self.m[i], i - 25, :]

    def tensor(self, pe):
        k = self.k
        for i, m in enumerate(self.m):
            t = self.ts[i]
            k.open_acc(pe, t)
            k.split_product(pe, k.acc(t)[0:m, :], self.us[i], self.xn, wait=(i == 0), m=m)

    def scalar(self, act):
        k = self.k
        self.convert_first(act, k.convert_hi)
        act.wait_ge(self.padded, 1)
        for i, m in enumerate(self.m):
            self.convert_next(act, k.convert_hi, i)
            t = self.ts[i]
            k.wait_acc_full(act, t)
            if i >= 3:
                act.wait_ge(self.done, i - 2)
            act.activation(self.shift[0:m, i % 3, 1:1 + S], k.acc(t)[0:m, :], ACT.Copy).then_inc(
                k.acc_drained[t % NA], 1)
        act.wait_ge(self.done, 27)
        z = self.zwa[0:64, :]
        act.activation(z, z, ACT.Tanh).then_inc(self.zwa_ready, 1)
        for i in (0, 1):
            z = self.zg[0:self.m[25 + i], i, :]
            k.after_act(act, act.activation(z, z, ACT.Tanh, scale=0.5))
            act.activation(z, z, ACT.Copy, scale=0.5, bias=0.5).then_inc(self.zg_ready, 1)

    def vector(self, dve):
        k = self.k
        self.before(dve)
        dve.memset(self.shift[:, :, 0:1], 0.0).then_inc(self.padded, 1)
        self.convert_first(dve, k.convert_lo)
        for i, m in enumerate(self.m):
            self.convert_next(dve, k.convert_lo, i)
            k.wait_acc_drained(dve, self.ts[i])
            z, prev, dst = self.shift[0:m, i % 3, 1:1 + S], self.shift[0:m, i % 3, 0:S], self.dst(i)
            k.after_dve(dve, dve.tensor_tensor(dst, prev, z, ALU.subtract))
            dve.scalar_tensor_tensor(dst, dst, k.vec("mu", i, 0, m), z, ALU.mult, ALU.add).then_inc(self.done, 1)


class RwkvPrepare(Stage):

    def __init__(self, k, inp, aa, bb, end, tmp, bonus_out, before):
        super().__init__(k)
        self.before = before
        self.inp, self.aa, self.bb, self.end, self.tmp, self.bonus_out = inp, aa, bb, end, tmp, bonus_out
        self.wt, self.at, self.nt, self.bt, self.roots = [], [], [], [], []
        for p in range(9):
            if p < 8:
                self.wt.append(k.take_acc())
                self.at.append(k.take_acc())
                self.nt.append(k.take_acc())
                self.roots.append(InverseRoot(k, self.nt[-1], S, 1e-24, floor=True))
            if p:
                self.bt.append(k.take_acc())
        self.u = k.take_unit(self.at[-1], 1024)
        self.sq0 = k.reserve("square", 8)
        sem = k.sem
        self.halved = sem("decay_biases_halved")
        self.decay_ready = sem("log_decay_sum_ready")
        self.exps_ready = sem("decay_products_ready")
        self.prev_ready = sem("log_decay_before_ready")
        self.kk_ready = sem("kk_ready")
        self.rk_ready = sem("rkk_ready")
        self.kka_ready = sem("kk_a_ready")
        self.bonus_ready = sem("bonus_ready")
        self.bonus_saved = [sem(f"bonus_saved{i}") for i in range(2)]
        self.done = sem("a_scaled_ready")
        self.rest_done = sem("bkr_scaled_ready")

    def wait_scaled(self, eng, p):
        eng.wait_ge(self.done, p + 1)
        eng.wait_ge(self.rest_done, p + 1)

    def tensor(self, pe):
        k = self.k
        w = k.weights(pe, self.u)
        z = self.inp.zwa
        pe.wait_ge(self.inp.zwa_ready, 1)
        for p in range(9):
            if p < 8:
                k.open_acc(pe, self.wt[p])
                pe.matmul(k.acc(self.wt[p]), w[0:64, p * P:(p + 1) * P], z[0:64, :], start=True, stop=True).then_inc(
                    k.acc_full, 1)
                k.open_acc(pe, self.at[p])
                pe.matmul(k.acc(self.at[p]), w[64:128, p * P:(p + 1) * P], z[64:128, :], start=True,
                          stop=True).then_inc(k.acc_full, 1)
                k.open_acc(pe, self.nt[p])
                pe.wait_ge(k.square_ready, self.sq0 + p + 1)
                pe.matmul(k.acc(self.nt[p]), k.const("head_sum"), k.square[:, p % 4, :], start=True,
                          stop=True).then_inc(k.acc_full, 1)
            if p:
                k.open_acc(pe, self.bt[p - 1])
                pe.wait_ge(self.rk_ready, p)
                pe.matmul(k.acc(self.bt[p - 1]), k.const("head_sum"), self.tmp["rkk"][:, (p - 1) % 2, :], start=True,
                          stop=True).then_inc(k.acc_full, 1)

    def scalar(self, act):
        k = self.k
        act.wait_ge(self.halved, 1)
        for p in range(9):
            if p < 8:
                tm = {n: self.tmp[n][:, p % 2, :] for n in ("decay", "a", "kk")}
                if p >= 2:
                    self.wait_scaled(act, p - 2)
                k.wait_acc_full(act, self.wt[p])
                act.activation(tm["decay"], k.acc(self.wt[p]), ACT.Tanh, scale=0.5,
                               bias=self.tmp["w0h"][:, p:p + 1]).then_inc(k.acc_drained[self.wt[p] % NA], 1)
                k.wait_acc_full(act, self.at[p])
                act.activation(tm["a"], k.acc(self.at[p]), ACT.Tanh, scale=0.5,
                               bias=self.tmp["a0h"][:, p:p + 1]).then_inc(k.acc_drained[self.at[p] % NA], 1)
                act.wait_ge(self.kk_ready, p + 1)
                act.activation(k.square[:, p % 4, :], tm["kk"], ACT.Square).then_inc(k.square_ready, 1)
            if p:
                q = p - 1
                tm = {n: self.tmp[n][:, q % 2, :] for n in ("p", "inv", "sum", "before")}
                self.roots[q].guess(act)
                act.wait_ge(self.decay_ready, q + 1)
                act.activation(tm["p"], tm["sum"], ACT.Exp)
                act.activation(tm["inv"], tm["sum"], ACT.Exp, scale=-1.0).then_inc(self.exps_ready, 1)
                act.wait_ge(self.prev_ready, q + 1)
                act.activation(tm["before"], tm["before"], ACT.Exp).then_inc(self.exps_ready, 1)

    def gpsimd(self, pool):
        r, kx, _ = self.inp.rkv
        for p in range(8):
            tm = {n: self.tmp[n][:, p % 2, :] for n in ("p", "inv", "a")}
            pool.wait_ge(self.exps_ready, 2 * p + 1)
            pool.wait_ge(self.rk_ready, p + 1)
            pool.tensor_tensor(r[:, p, :], r[:, p, :], tm["p"], ALU.mult)
            pool.tensor_tensor(kx[:, p, :], kx[:, p, :], tm["inv"], ALU.mult)
            pool.wait_ge(self.kka_ready, p + 1)
            pool.tensor_tensor(self.bb[:, p, :], tm["a"], tm["inv"], ALU.mult).then_inc(self.rest_done, 1)
            pool.wait_ge(self.bonus_ready, p + 1)
            pool.dma_start(self.bonus_out[:, p, :], self.tmp["bonus"][:, p % 2, :]).then_inc(
                self.bonus_saved[p % 2], 16)

    def first_half(self, dve, p):
        k, seq = self.k, self.k.after_dve
        tm = {n: self.tmp[n][:, p % 2, :] for n in ("decay", "a", "kk", "sum", "before", "mix", "rkk")}
        r, kx, _ = self.inp.rkv
        rp, kp = r[:, p, :], kx[:, p, :]
        dve.tensor_scalar(tm["kk"], kp, k.vec("k_k", p), None, ALU.mult).then_inc(self.kk_ready, 1)
        k.wait_acc_drained(dve, self.wt[p])
        seq(dve, dve.tensor_scalar(tm["decay"], tm["decay"], 1.0, -0.5 * DECAY, ALU.add, ALU.mult))
        dve.tensor_tensor_scan(tm["sum"], k.const("restart"), tm["decay"], 0.0, ALU.mult, ALU.add).then_inc(
            self.decay_ready, 1)
        dve.wait_ge(self.decay_ready, p + 1)
        dve.tensor_tensor(tm["before"], tm["sum"], tm["decay"], ALU.subtract).then_inc(self.prev_ready, 1)
        k.wait_acc_drained(dve, self.at[p])
        seq(dve, dve.tensor_scalar(tm["a"], tm["a"], 0.5, 0.5, ALU.mult, ALU.add))
        seq(dve, dve.tensor_scalar(tm["mix"], tm["a"], 1.0, k.vec("k_a", p), ALU.subtract, ALU.mult))
        dve.wait_ge(self.kk_ready, p + 1)
        seq(dve, dve.scalar_tensor_tensor(kp, tm["mix"], 1.0, kp, ALU.add, ALU.mult))
        dve.scalar_tensor_tensor(tm["rkk"], rp, k.vec("r_k", p), kp, ALU.mult, ALU.mult).then_inc(self.rk_ready, 1)

    def vector(self, dve):
        k, seq = self.k, self.k.after_dve
        self.before(dve)
        dve.tensor_scalar(self.tmp["w0h"], k.vecs[:, VECS["w0"]:VECS["w0"] + 8], 0.5, None, ALU.mult)
        dve.tensor_scalar(self.tmp["a0h"], k.vecs[:, VECS["a0"]:VECS["a0"] + 8], 0.5, None, ALU.mult).then_inc(
            self.halved, 1)
        self.first_half(dve, 0)
        for p in range(8):
            tm = {n: self.tmp[n][:, p % 2, :] for n in ("a", "kk", "before", "p", "bonus")}
            self.roots[p].take_mean(dve)
            if p + 1 < 8:
                if p >= 1:
                    self.wait_scaled(dve, p - 1)
                self.first_half(dve, p + 1)
            root = self.roots[p].refine(dve)
            seq(dve, dve.tensor_tensor(tm["kk"], tm["kk"], root, ALU.mult))
            dve.tensor_tensor(tm["a"], tm["a"], tm["kk"], ALU.mult).then_inc(self.kka_ready, 1)
            dve.wait_ge(self.exps_ready, 2 * p + 2)
            dve.tensor_copy(self.end[:, p, :], tm["p"][:, CH - 1:S:CH])
            dve.scalar_tensor_tensor(self.aa[:, p, :], tm["kk"], -1.0, tm["before"], ALU.mult, ALU.mult).then_inc(
                self.done, 1)
            k.wait_acc_full(dve, self.bt[p])
            if p >= 2:
                dve.wait_ge(self.bonus_saved[p % 2], 16 * (p // 2))
            dve.tensor_tensor(tm["bonus"], self.inp.rkv[2][:, p, :], k.acc(self.bt[p]), ALU.mult).then_inc(
                k.acc_drained[self.bt[p] % NA], 1)
            k.wait_acc_drained(dve, self.bt[p])
            dve.nop().then_inc(self.bonus_ready, 1)


class RwkvScan(Stage):

    STEPS = ("x", "b_ra0", "b_ra1", "bn0", "bn1", "d2", "d2t", "kn0", "kn1", "d4", "d2_dm0", "d2_dm1", "d8", "m2",
             "vn", "m3", "k_ra0", "k_ra1", "mn", "g", "m4", "mn2", "g2", "an", "q", "m5", "wt", "u", "sa", "y", "z")

    def __init__(self, k, prep, buf, ra):
        super().__init__(k)
        self.prep, self.buf, self.ra = prep, buf, ra
        self.t = [{s: k.take_aux() for s in self.STEPS} for _ in range(NCH)]
        self.zeroed = k.sem("scan_zeroed")
        self.state_ready = k.sem("scan_state_ready")
        self.b_staged = k.sem("scan_b_staged")
        self.k_staged = k.sem("scan_k_staged")

    def chunk(self, ap, c):
        return ap[:, :, c * CH:(c + 1) * CH]

    def gpsimd(self, pool):
        k, b = self.k, self.buf
        self.prep.wait_scaled(pool, 7)
        pool.wait_ge(self.zeroed, 1)
        for c in range(NCH):
            bc, kc = self.chunk(self.prep.bb, c), self.chunk(self.prep.inp.rkv[1], c)
            if c:
                k.wait_aux_full(pool, self.t[c - 1]["bn1"])
            for e in range(2):
                part, cols = slice(e * HD, (e + 1) * HD), slice(e * CH, (e + 1) * CH)
                pool.tensor_copy(b["b_bd"][part, :, cols], bc[part]).then_inc(self.b_staged, 1)
            if c:
                k.wait_aux_full(pool, self.t[c - 1]["k_ra1"])
            for e in range(2):
                part, cols = slice(e * HD, (e + 1) * HD), slice(e * CH, (e + 1) * CH)
                pool.tensor_copy(b["k_bd"][part, :, cols], kc[part]).then_inc(self.k_staged, 1)

    def tensor(self, pe):
        k, b = self.k, self.buf
        r, _, v = self.prep.inp.rkv
        aa, bb = self.prep.aa, self.prep.bb
        ident = k.const("ident64")
        self.prep.wait_scaled(pe, 7)
        pe.wait_ge(self.zeroed, 1)

        def cut(ap, p, e):
            return ap[e * HD:(e + 1) * HD, p, :]

        def product(t, *terms):
            k.open_aux(pe, t)
            out = k.aux(t).rearrange("p (a b) -> p a b", b=CH)
            for p in range(8):
                for e in range(2):
                    for i, (lhs, rhs) in enumerate(terms):
                        right = ident[e * HD:(e + 1) * HD, :] if rhs is None else cut(rhs, p, e)
                        if rhs is None and e == 0:
                            mm = pe.transpose(cut(out, p, e), cut(lhs, p, e), right)
                        else:
                            mm = pe.matmul(cut(out, p, e), cut(lhs, p, e), right, start=(i == 0),
                                           stop=(i == len(terms) - 1))
            mm.then_inc(k.aux_full, 1)

        def blocks(t, *terms):
            k.open_aux(pe, t)
            out = k.aux(t).rearrange("p (a b) -> p a b", b=CH)
            for p in range(8):
                for e in range(2):
                    part = slice(e * HD, (e + 1) * HD)
                    for i, (lhs, rhs) in enumerate(terms):
                        mm = pe.matmul(out[part, p, :], lhs[part, p, e * CH:(e + 1) * CH], rhs[part, p, :],
                                       start=(i == 0), stop=(i == len(terms) - 1))
            mm.then_inc(k.aux_full, 1)

        def full_twin(t, name, lhs, rhs):
            for half in range(2):
                bank = t[f"{name}{half}"]
                k.open_aux(pe, bank)
                out = k.aux(bank).rearrange("p (a s b) -> p a s b", s=2, b=CH)
                for p in range(4 * half, 4 * half + 4):
                    mm = pe.matmul(out[:, p - 4 * half], lhs[:, p, :], rhs(p), start=True, stop=True)
                mm.then_inc(k.aux_full, 1)

        def twin(t, name, lhs, rhs):
            for half in range(2):
                bank = t[f"{name}{half}"]
                k.open_aux(pe, bank)
                out = k.aux(bank).rearrange("p (a s b) -> p a s b", s=2, b=CH)
                for p in range(4 * half, 4 * half + 4):
                    for e in range(2):
                        part = slice(e * HD, (e + 1) * HD)
                        mm = pe.matmul(out[part, p - 4 * half], lhs[part, p, :], rhs(p)[part], start=True, stop=True)
                mm.then_inc(k.aux_full, 1)

        def transposed(t, name, src):
            for half in range(2):
                bank = t[f"{name}{half}"]
                k.open_aux(pe, bank)
                out = k.aux(bank).rearrange("p (a b) -> p a b", b=P)
                for p in range(4 * half, 4 * half + 4):
                    mm = pe.transpose(out[:, p - 4 * half, :], src[:, p, :], k.const("ident"))
                mm.then_inc(k.aux_full, 1)

        for c in range(NCH):
            ra = lambda p, c=c: self.ra[:, :, p * S + c * CH:p * S + (c + 1) * CH]
            t = self.t[c]
            ac, bc, rc, vc = (self.chunk(x, c) for x in (aa, bb, r, v))

            def drained(*steps, t=t):
                for step in steps:
                    k.wait_aux_drained(pe, t[step])

            product(t["x"], (ac, bc))
            pe.wait_ge(self.b_staged, 2 * (c + 1))
            full_twin(t, "b_ra", b["b_bd"], ra)
            transposed(t, "bn", b["b_bd"])
            drained("x", "b_ra0", "b_ra1")
            product(t["d2"], (b["dt"], b["d"]))
            product(t["d2t"], (b["d"], b["dt"]))
            pe.wait_ge(self.k_staged, 2 * (c + 1))
            transposed(t, "kn", b["k_bd"])
            drained("d2", "d2t")
            product(t["d4"], (b["d2t"], b["d2"]))
            twin(t, "d2_dm", b["d2"], lambda p: b["d2t_m0"][:, :, p, :])
            drained("d4", "d2_dm0", "d2_dm1")
            blocks(t["d8"], (b["d4t"], b["d4"]))
            product(t["m2"], (b["d4"], b["m1"]))
            product(t["vn"], (vc, None))
            drained("d8", "m2")
            blocks(t["m3"], (b["d8"], b["m0"]))
            full_twin(t, "k_ra", b["k_bd"], ra)
            drained("m3")
            product(t["mn"], (b["m1"], None))
            blocks(t["g"], (b["x32"], b["m1"]))
            drained("mn", "g")
            blocks(t["m4"], (b["mn"], b["g"]))
            drained("m4")
            product(t["mn2"], (b["m0"], None))
            blocks(t["g2"], (b["x64"], b["m0"]))
            product(t["an"], (ac, None))
            drained("k_ra0", "k_ra1", "vn")
            blocks(t["q"], (b["akt"], b["vn"]))
            drained("mn2", "g2")
            blocks(t["m5"], (b["mn"], b["g"]))
            drained("an", "m5")
            blocks(t["wt"], (b["an"], b["m1"]))
            drained("q")
            product(t["u"], (b["m1"], b["q"]))
            drained("wt")
            if c:
                pe.wait_ge(self.state_ready, c)
            blocks(t["sa"], (b["wt"], b["z"]))
            drained("sa")
            product(t["y"], (b["z"], rc), (b["sa"], b["rbt"]), (b["vn"], b["rkt"]))
            drained("bn0", "bn1", "kn0", "kn1")
            blocks(t["z"], (b["bn"], b["sa"]), (b["kn"], b["vn"]))

    def scalar(self, act):
        k, b = self.k, self.buf

        def copy(t, dst):
            k.wait_aux_full(act, t)
            act.activation(dst, k.aux(t).rearrange("p (a b) -> p a b", b=CH), ACT.Copy).then_inc(
                k.aux_drained[t % NX], 1)

        def copy_diagonal(t, dst):
            k.wait_aux_full(act, t)
            src = k.aux(t).rearrange("p (a b) -> p a b", b=CH)
            act.activation(dst[0:HD, :, 0:CH], src[0:HD], ACT.Copy)
            act.activation(dst[HD:P, :, CH:P], src[HD:P], ACT.Copy).then_inc(k.aux_drained[t % NX], 1)

        def copy_transposed(t, name, dst):
            for half in range(2):
                bank = t[f"{name}{half}"]
                k.wait_aux_full(act, bank)
                act.activation(dst[:, 4 * half:4 * half + 4, :], k.aux(bank).rearrange("p (a b) -> p a b", b=P),
                               ACT.Copy).then_inc(k.aux_drained[bank % NX], 1)

        for c in range(NCH):
            t = self.t[c]
            copy_transposed(t, "bn", b["bn"])
            copy(t["d2"], b["d2"])
            copy(t["d2t"], b["d2t"])
            copy_transposed(t, "kn", b["kn"])
            copy(t["d4"], b["d4"])
            copy_diagonal(t["d8"], b["d8"])
            copy(t["vn"], b["vn"])
            copy_diagonal(t["mn"], b["mn"])
            copy(t["g"], b["g"])
            copy_diagonal(t["mn2"], b["mn"])
            copy(t["g2"], b["g"])
            copy_diagonal(t["an"], b["an"])
            copy(t["q"], b["q"])
            copy_diagonal(t["wt"], b["wt"])
            copy(t["y"], self.chunk(self.prep.inp.rkv[0], c))

    def vector(self, dve):
        k, b = self.k, self.buf
        for s in self.prep.bonus_saved:
            dve.wait_ge(s, 16 * 4)
        self.prep.wait_scaled(dve, 7)
        for name in ("b_bd", "k_bd", "x32", "x64", "d8", "mn"):
            dve.memset(row(b[name]), 0.0)
        dve.memset(row(b["z"]), 0.0).then_inc(self.zeroed, 1)
        dve.wait_ge(self.zeroed, 1)

        def mask(name):
            return k.const(name).unsqueeze(1).to_broadcast([P, 8, CH])

        def src(t):
            return k.aux(t).rearrange("p (a b) -> p a b", b=CH)

        for c in range(NCH):
            tt = self.t[c]

            def done(ins, step):
                ins.then_inc(k.aux_drained[tt[step] % NX], 1)

            def full(step):
                k.wait_aux_full(dve, tt[step])

            def diagonal(dst, source, name, pairs=slice(0, 8)):
                n = pairs.stop - pairs.start
                for e in range(2):
                    part = slice(e * HD, (e + 1) * HD)
                    m = k.const(name)[part].unsqueeze(1).to_broadcast([HD, n, CH])
                    ins = dve.tensor_tensor(dst[part, pairs, e * CH:(e + 1) * CH], source[part], m, ALU.mult)
                return ins

            full("x")
            dve.tensor_tensor(b["d"], src(tt["x"]), mask("diag16"), ALU.mult)
            diagonal(b["x32"], src(tt["x"]), "off16")
            done(diagonal(b["x64"], src(tt["x"]), "off32"), "x")

            def twin(step):
                full(step)
                return k.aux(tt[step]).rearrange("p (a s b) -> p a s b", s=2, b=CH)

            def half_mask(name):
                return k.const(name).unsqueeze(1).to_broadcast([P, 4, CH])

            for half in range(2):
                step, ps = f"b_ra{half}", slice(4 * half, 4 * half + 4)
                both = twin(step)
                k.after_dve(dve, dve.tensor_tensor(b["dt"][:, ps], both[:, :, 1], half_mask("diag16T"), ALU.mult))
                dve.tensor_tensor(b["m0"][:, ps], b["dt"][:, ps], half_mask("ident64"), ALU.add)
                done(dve.tensor_tensor(b["rbt"][:, ps], both[:, :, 0], half_mask("from"), ALU.mult), step)

            def summed(step, dst, old, before):
                k.wait_aux_drained(dve, tt[before])
                full(step)
                done(dve.tensor_tensor(row(b[dst]), row(b[old]), k.aux(tt[step]), ALU.add), step)

            for half in range(2):
                step, ps = f"d2_dm{half}", slice(4 * half, 4 * half + 4)
                both = twin(step)
                for e in range(2):
                    part = slice(e * HD, (e + 1) * HD)
                    dve.tensor_copy(b["d4t"][part, ps, e * CH:(e + 1) * CH], both[part, :, 0])
                done(dve.tensor_tensor(b["m1"][:, ps], b["m0"][:, ps], both[:, :, 1], ALU.add), step)
            k.wait_aux_drained(dve, tt["d2_dm0"])
            summed("m2", "m0", "m1", "d2_dm1")
            summed("m3", "m1", "m0", "m2")
            for half in range(2):
                step, ps = f"k_ra{half}", slice(4 * half, 4 * half + 4)
                both = twin(step)
                diagonal(b["akt"], both[:, :, 1], "after", ps)
                done(dve.tensor_tensor(b["rkt"][:, ps], both[:, :, 0], half_mask("from"), ALU.mult), step)
            summed("m4", "m0", "m1", "m3")
            summed("m5", "m1", "m0", "m4")
            full("u")
            k.after_dve(dve, dve.tensor_copy(row(b["u"]), k.aux(tt["u"])))
            dve.nop().then_inc(k.aux_drained[tt["u"] % NX], 1)
            full("sa")
            done(dve.tensor_tensor(row(b["sa"]), row(b["u"]), k.aux(tt["sa"]), ALU.add), "sa")
            full("z")
            if c:
                dve.wait_ge(self.state_ready, c)
            done(dve.tensor_tensor(row(b["z"]), row(b["z"]), k.aux(tt["z"]), ALU.add), "z")
            k.wait_aux_drained(dve, tt["z"])
            end = self.prep.end[:, :, c:c + 1].to_broadcast([P, 8, CH])
            dve.tensor_tensor(b["z"], b["z"], end, ALU.mult).then_inc(self.state_ready, 1)

    def wait_y(self, eng):
        self.k.wait_aux_drained(eng, self.t[NCH - 1]["y"])

    def wait_end(self, eng):
        eng.wait_ge(self.state_ready, NCH)


class RwkvOutput(Stage):

    def __init__(self, k, scan, zg, zg_ready, y, bonus, bonus_in, bonus_saved, var, guess, root):
        super().__init__(k)
        self.scan, self.zg, self.zg_ready, self.y, self.bonus, self.bonus_in, self.bonus_saved = (
            scan, zg, zg_ready, y, bonus, bonus_in, bonus_saved)
        self.var, self.guess, self.root = var, guess, root
        self.mt, self.vt = [], []
        for p in range(9):
            if p < 8:
                self.mt.append(k.take_acc())
            if p:
                self.vt.append(k.take_acc())
        self.gt = [k.take_acc() for _ in range(8)]
        self.us = [k.take_unit(self.gt[-1]), k.take_unit(self.gt[-1])]
        self.sq0 = k.reserve("square", 8)
        self.bonus_loaded = k.sem("bonus_loaded")
        self.guess_ready = k.sem("rwkv_guess_ready")
        self.var_ready = k.sem("rwkv_var_ready")

    def gpsimd(self, pool):
        self.scan.wait_y(pool)
        for s in self.bonus_saved:
            pool.wait_ge(s, 16 * 4)
        pool.dma_start(self.bonus, self.bonus_in).then_inc(self.bonus_loaded, 16)

    def tensor(self, pe):
        k = self.k
        self.scan.wait_y(pe)
        for p in range(9):
            if p < 8:
                k.open_acc(pe, self.mt[p])
                pe.matmul(k.acc(self.mt[p]), k.const("head_mean"), self.y[:, p, :], start=True, stop=True).then_inc(
                    k.acc_full, 1)
            if p:
                k.open_acc(pe, self.vt[p - 1])
                pe.wait_ge(k.square_ready, self.sq0 + p)
                pe.matmul(k.acc(self.vt[p - 1]), k.const("head_mean"), k.square[:, (p - 1) % 4, :], start=True,
                          stop=True).then_inc(k.acc_full, 1)
        pe.wait_ge(self.zg_ready, 2)
        w = [k.weights(pe, u) for u in self.us]
        for p in range(8):
            k.open_acc(pe, self.gt[p])
            pe.matmul(k.acc(self.gt[p]), w[0][:, p * P:(p + 1) * P], self.zg[:, 0, :], start=True, stop=False)
            pe.matmul(k.acc(self.gt[p]), w[1][0:32, p * P:(p + 1) * P], self.zg[0:32, 1, :], start=False,
                      stop=True).then_inc(k.acc_full, 1)

    def scalar(self, act):
        k = self.k
        for p in range(8):
            k.wait_acc_drained(act, self.mt[p])
            if p >= 4:
                k.wait_acc_full(act, self.vt[p - 4])
            act.activation(k.square[:, p % 4, :], self.y[:, p, :], ACT.Square).then_inc(k.square_ready, 1)
        for half in range(2):
            ps = slice(4 * half, 4 * half + 4)
            act.wait_ge(self.var_ready, 4 * half + 4)
            k.after_act(act, act.activation(row(self.guess[:, ps]), row(self.var[:, ps]), ACT.Ln))
            act.activation(row(self.guess[:, ps]), row(self.guess[:, ps]), ACT.Exp, scale=-0.5).then_inc(
                self.guess_ready, 1)

    def vector(self, dve):
        k = self.k
        for p in range(9):
            if p < 8:
                y, t = self.y[:, p, :], self.mt[p]
                k.wait_acc_full(dve, t)
                dve.tensor_tensor(y, y, k.acc(t), ALU.subtract).then_inc(k.acc_drained[t % NA], 1)
            if p:
                t = self.vt[p - 1]
                k.wait_acc_full(dve, t)
                k.after_dve(dve, dve.tensor_scalar(self.var[:, p - 1, :], k.acc(t), LNX_EPS, None, ALU.add))
                dve.nop().then_inc(self.var_ready, 1)
                dve.nop().then_inc(k.acc_drained[t % NA], 1)
        dve.wait_ge(self.bonus_loaded, 16)
        for half in range(2):
            ps = slice(4 * half, 4 * half + 4)
            g, r, v = row(self.guess[:, ps]), row(self.root[:, ps]), row(self.var[:, ps])
            dve.wait_ge(self.guess_ready, half + 1)
            k.after_dve(dve, dve.tensor_tensor(r, g, g, ALU.mult))
            k.after_dve(dve, dve.scalar_tensor_tensor(r, r, -0.5, v, ALU.mult, ALU.mult))
            k.after_dve(dve, dve.scalar_tensor_tensor(r, r, 1.5, g, ALU.add, ALU.mult))
            for p in range(4 * half, 4 * half + 4):
                y = self.y[:, p, :]
                k.after_dve(dve, dve.scalar_tensor_tensor(y, y, k.vec("lnx_w", p), self.root[:, p, :], ALU.mult, ALU.mult))
                k.after_dve(dve, dve.scalar_tensor_tensor(y, y, k.vec("lnx_b", p), self.bonus[:, p, :], ALU.add, ALU.add))
                t = self.gt[p]
                k.wait_acc_full(dve, t)
                dve.tensor_tensor(y, y, k.acc(t), ALU.mult).then_inc(k.acc_drained[t % NA], 1)

    def wait_out(self, eng, c):
        self.k.wait_acc_drained(eng, self.gt[c])


class CrossAttention(Stage):

    def __init__(self, k, q, keys, values, out, buf, waits):
        super().__init__(k)
        self.q, self.keys, self.values, self.out, self.buf, self.waits = q, keys, values, out, buf, waits
        self.st, self.tt, self.ot = [], [], []
        for h in range(2):
            self.st.append([k.take_acc(), k.take_acc()])
        for h in range(4):
            self.tt.append([k.take_acc(), k.take_acc()])
            self.ot.append([k.take_acc(), k.take_acc()])
            if h + 2 < 4:
                self.st.append([k.take_acc(), k.take_acc()])
        self.max_ready = k.sem("cross_max_ready")
        self.p_ready = k.sem("cross_probs_ready")
        self.scaled = k.sem("cross_probs_scaled")

    def scores(self, pe, h):
        k = self.k
        for i, t in enumerate(self.st[h]):
            k.open_acc(pe, t)
            for j in range(2):
                for c in range(2):
                    tok = slice((2 * i + j) * P, (2 * i + j + 1) * P)
                    mm = pe.matmul(k.acc(t)[:, j * N_MEM:(j + 1) * N_MEM], self.q[:, 2 * h + c, tok],
                                   self.keys[:, 2 * h + c, :], start=(c == 0), stop=(c == 1))
            mm.then_inc(k.acc_full, 1)

    def tensor(self, pe):
        k, b = self.k, self.buf
        for w in self.waits:
            w(pe)
        self.scores(pe, 0)
        self.scores(pe, 1)
        for h in range(4):
            pe.wait_ge(self.scaled, h + 1)
            p = b.p[:, h % 2, :]
            for j, t in enumerate(self.tt[h]):
                k.open_acc(pe, t)
                for i in range(NT):
                    mm = pe.transpose(k.acc(t)[:, i * P:(i + 1) * P], p[:, i * N_MEM + j * P:i * N_MEM + (j + 1) * P],
                                      k.const("ident"))
                mm.then_inc(k.acc_full, 1)
            for c, t in enumerate(self.ot[h]):
                k.open_acc(pe, t)
                for j in range(2):
                    if c == 0:
                        k.wait_acc_drained(pe, self.tt[h][j])
                    at = h * 256 + c * P
                    mm = pe.matmul(k.acc(t), self.values[:, j, at:at + P], b.pt[:, j * S:(j + 1) * S],
                                   start=(j == 0), stop=(j == 1))
                mm.then_inc(k.acc_full, 1)
            if h + 2 < 4:
                self.scores(pe, h + 2)

    def maxima(self, dve, h):
        k, b = self.k, self.buf
        for i, t in enumerate(self.st[h]):
            k.wait_acc_full(dve, t)
            k.after_dve(dve, dve.tensor_reduce(b.max[:, h % 2, 2 * i:2 * i + 2],
                                               k.acc(t).rearrange("p (j n) -> p j n", n=N_MEM), AX.X, ALU.max))
        dve.tensor_scalar(b.negmax[:, h % 2, :], b.max[:, h % 2, :], -1.0 / 16, None, ALU.mult).then_inc(
            self.max_ready, 1)

    def scale(self, dve, h):
        k, b = self.k, self.buf
        dve.wait_ge(self.p_ready, 4 * (h + 1))
        inv = b.inv[:, h % 2, :]
        k.after_dve(dve, dve.reciprocal(inv, b.sum[:, h % 2, :]))
        for i in range(NT):
            seg = b.p[:, h % 2, i * N_MEM:(i + 1) * N_MEM]
            last = dve.tensor_scalar(seg, seg, inv[:, i:i + 1], None, ALU.mult)
        last.then_inc(self.scaled, 1)

    def vector(self, dve):
        k = self.k
        self.maxima(dve, 0)
        self.maxima(dve, 1)
        self.scale(dve, 0)
        for h in range(4):
            if h + 1 < 4:
                self.scale(dve, h + 1)
            for c, t in enumerate(self.ot[h]):
                k.wait_acc_full(dve, t)
                dve.tensor_copy(self.out[:, 2 * h + c, :], k.acc(t)).then_inc(k.acc_drained[t % NA], 1)
            if h + 2 < 4:
                self.maxima(dve, h + 2)

    def exps(self, act, h):
        k, b = self.k, self.buf
        act.wait_ge(self.max_ready, h + 1)
        for i in range(NT):
            t = self.st[h][i // 2]
            src = k.acc(t)[:, (i % 2) * N_MEM:(i % 2 + 1) * N_MEM]
            act.activation(b.p[:, h % 2, i * N_MEM:(i + 1) * N_MEM], src, ACT.Exp, scale=1.0 / 16,
                           bias=b.negmax[:, h % 2, i:i + 1], accum_out=b.sum[:, h % 2, i:i + 1]).then_inc(
                               self.p_ready, 1)
            if i % 2:
                act.wait_ge(self.p_ready, 4 * h + i + 1)
                act.nop().then_inc(k.acc_drained[t % NA], 1)

    def scalar(self, act):
        k, b = self.k, self.buf
        self.exps(act, 0)
        self.exps(act, 1)
        for h in range(4):
            for j, t in enumerate(self.tt[h]):
                k.wait_acc_full(act, t)
                act.activation(b.pt[:, j * S:(j + 1) * S], k.acc(t), ACT.Copy).then_inc(k.acc_drained[t % NA], 1)
            if h + 2 < 4:
                self.exps(act, h + 2)

    def wait_out(self, eng, c):
        self.k.wait_acc_drained(eng, self.ot[c // 2][c % 2])


class ConvFfn(SplitStage):

    def __init__(self, k, xs, hi, lo, abuf, t0, t1, out, before, after=None):
        super().__init__(k, after)
        self.xs, self.hi, self.lo, self.abuf, self.t0, self.t1, self.out, self.before = (
            xs, hi, lo, abuf, t0, t1, out, before)
        for _ in range(2 * FT2):
            self.take()
        self.at, self.bt = self.ts[0::2], self.ts[1::2]
        self.padded = k.sem("conv_padded")
        self.conv_ready = k.sem("conv_ready")
        self.tanh_ready = k.sem("silu_tanh_ready")
        self.hi_ready = k.sem("ffn_hi_ready")
        self.lo_ready = k.sem("ffn_lo_ready")

    def wait_hi(self, eng, j):
        eng.wait_ge(self.hi_ready, j + 1)

    def wait_lo(self, eng, j):
        eng.wait_ge(self.lo_ready, j + 1)

    def tensor(self, pe):
        k = self.k
        for i, t in enumerate(self.ts):
            k.open_acc(pe, t)
            k.split_product(pe, k.acc(t), self.us[i], self.xs, wait=(i == 0))

    def hidden_hi(self, act, m):
        self.k.wait_acc_drained(act, self.bt[m])
        act.activation(self.hi[:, m, :], self.out[:, m % 2, :], ACT.Copy).then_inc(self.hi_ready, 1)

    def hidden_lo(self, dve, m):
        self.wait_hi(dve, m)
        dve.tensor_tensor(self.lo[:, m, :], self.out[:, m % 2, :], self.hi[:, m, :].bitcast(F32),
                          ALU.subtract).then_inc(self.lo_ready, 1)

    def scalar(self, act):
        k = self.k
        self.convert_first(act, k.convert_hi)
        act.wait_ge(self.padded, 1)
        for m, t in enumerate(self.at):
            self.convert_next(act, k.convert_hi, 2 * m)
            if m:
                self.hidden_hi(act, m - 1)
            k.wait_acc_full(act, t)
            if m >= 2:
                act.wait_ge(self.conv_ready, m - 1)
            act.activation(self.abuf[:, m % 2, 2:2 + S], k.acc(t), ACT.Copy).then_inc(k.acc_drained[t % NA], 1)
            self.convert_next(act, k.convert_hi, 2 * m + 1)
            act.wait_ge(self.conv_ready, m + 1)
            if m >= 2:
                k.wait_acc_drained(act, self.bt[m - 2])
            act.activation(self.t1[:, m % 2, :], self.t0[:, m % 2, :], ACT.Tanh, scale=0.5).then_inc(self.tanh_ready, 1)
        self.hidden_hi(act, FT2 - 1)

    def vector(self, dve):
        k = self.k
        self.before(dve)
        dve.memset(self.abuf[:, :, 0:2], 0.0).then_inc(self.padded, 1)
        self.convert_first(dve, k.convert_lo)
        for m, t in enumerate(self.bt):
            self.convert_next(dve, k.convert_lo, 2 * m)
            if m:
                self.hidden_lo(dve, m - 1)
            k.wait_acc_drained(dve, self.at[m])
            a, c = self.abuf[:, m % 2, :], self.t0[:, m % 2, :]
            k.after_dve(dve, dve.tensor_scalar(c, a[:, 2:2 + S], k.vec("conv", 2 * FT2 + m), k.vec("conv_b", m),
                                               ALU.mult, ALU.add))
            k.after_dve(dve, dve.scalar_tensor_tensor(c, a[:, 1:1 + S], k.vec("conv", FT2 + m), c, ALU.mult, ALU.add))
            dve.scalar_tensor_tensor(c, a[:, 0:S], k.vec("conv", m), c, ALU.mult, ALU.add).then_inc(self.conv_ready, 1)
            self.convert_next(dve, k.convert_lo, 2 * m + 1)
            dve.wait_ge(self.tanh_ready, m + 1)
            k.after_dve(dve, dve.scalar_tensor_tensor(c, self.t1[:, m % 2, :], 1.0, c, ALU.add, ALU.mult))
            k.wait_acc_full(dve, t)
            if m >= 2:
                self.wait_lo(dve, m - 2)
            dve.scalar_tensor_tensor(self.out[:, m % 2, :], c, 0.5, k.acc(t), ALU.mult, ALU.mult).then_inc(
                k.acc_drained[t % NA], 1)
        self.hidden_lo(dve, FT2 - 1)


class Move(Stage):

    def __init__(self, k, name, dst, src, waits):
        super().__init__(k)
        self.dst, self.src, self.waits = dst, src, waits
        self.done = k.sem(name)

    def gpsimd(self, pool):
        for w in self.waits:
            w(pool)
        pool.dma_start(self.dst, self.src).then_inc(self.done, 16)

    def wait_done(self, eng):
        eng.wait_ge(self.done, 16)


class Alibi(Stage):

    def __init__(self, k, table):
        super().__init__(k)
        self.table = table
        self.ready = k.sem("alibi_ready")

    def scalar(self, act):
        k = self.k
        act.wait_ge(k.const_loaded, 16)
        for h in range(H1):
            act.activation(self.table[:, h, :], k.const("neg_dist"), ACT.Copy,
                           scale=float(2.0 ** (-8.0 * (h + 1) / H1))).then_inc(self.ready, 1)


class Store(Stage):

    def __init__(self, k, out, wait_x):
        super().__init__(k)
        self.out, self.wait_x = out, wait_x
        self.stored = k.sem("out_stored")

    def sync(self, sp):
        for j in range(DT_):
            self.wait_x(sp, j)
            sp.dma_start(self.out[:, j, :], self.k.x[:, j, :]).then_inc(self.stored, 16)
        sp.wait_ge(self.stored, 16 * DT_)


class Buffers:

    def __init__(self, view, p, pt, ct, small):
        self.p, self.pt = view(p, [3, TRI_N]), view(pt, [2, TRI_N])
        self.ct = view(ct, [S], parts=NCMP)
        self.max, self.negmax, self.sum = (view(small + 12 * i, [3, NT]) for i in range(3))
        self.inv = view(small + 36, [6, NT])


class CrossBuffers:

    def __init__(self, view, at):
        self.p = view(at, [2, NT * N_MEM])
        self.pt = view(at + 2048, [2 * S])
        self.max, self.negmax, self.sum, self.inv = (view(at + 3072 + 8 * i, [2, NT]) for i in range(4))


def build(nc, x, consts, vecs, weights, bucket, rel, rel_last, mem, out):
    with ExitStack() as ctx:
        k = Core(nc, ctx)
        k.set_up()
        ARENA = 37884
        k.wring = k.sb("wring", [P, RING, UNIT])
        k.w_hi = ctx.enter_context(nc.sbuf_tensor("w_hi", [P, SPLIT, UNIT], F32R))
        k.w_lo = ctx.enter_context(nc.sbuf_tensor("w_lo", [P, SPLIT, UNIT], F32R))
        hot = ctx.enter_context(nc.sbuf_tensor("one_hot_sb", [BUCKETS + 1, 1024], F32R))
        rows = ctx.enter_context(nc.sbuf_tensor("bias_rows", [BUCKETS + 1, 2 * HQ], F32R))
        k.consts = k.sb("consts_sb", [P, N_CONST])
        k.vecs = k.sb("vecs_sb", [P, N_VEC])
        k.square = k.sb("square", [P, 4, S])
        k.root_in = k.sb("root_in", [P, S])
        k.root_ln = k.root_y = k.sb("root_y", [P, S])
        k.root = k.sb("root", [P, S])
        gain8 = k.sb("q_gain_scaled", [P, 1])
        with nc.sbuf_tensor("arena", [P, ARENA], F32) as arena:
            pass
        k.ps = ctx.enter_context(nc.psum_tensor("ps", [P, 8, S], F32))
        bonus_dram = nc.dram_tensor("bonus_scratch", (P, DT_, S), F32, kind="Internal").ap()
        x_dram = nc.dram_tensor("x_scratch", (P, DT_, S), F32, kind="Internal").ap()

        def view_r(name, at, shape):
            assert at + int(np.prod(shape)) <= ARENA, (at, shape)
            with ExitStack() as place:
                if at:
                    place.enter_context(nc.sbuf_tensor(f"below_{name}", [P, at], F32))
                return place.enter_context(nc.sbuf_tensor(name, [P] + shape, F32R))[:, :, :]

        def view(at, shape, parts=P):
            n = int(np.prod(shape))
            assert at + n <= ARENA, (at, shape)
            a = arena[0:parts, at:at + n]
            if len(shape) == 1:
                return a
            if len(shape) == 2:
                return a.rearrange("p (a b) -> p a b", b=shape[1])
            return a.rearrange("p (a b c) -> p a b c", b=shape[1], c=shape[2])

        k.x = view(0, [DT_, S])
        xn = view(4096, [DT_, S])
        free = 8192

        def drained(stage):
            return lambda eng, j: k.wait_acc_drained(eng, stage.ts[j])

        def tiles(ap):
            return lambda j: ap[:, j, :]

        Load(k, x, consts, vecs, weights)
        cat = view(free, [DT_, S])
        qk = view(12288, [8, S])
        v1 = view(16384, [NT, S])
        u1 = view(18432, [4, 16 + S])
        sums = view(20544, [2, 16 + S])
        mixed = view(21600, [4, S])
        alibi = view(23648, [H1, S])
        buf1 = Buffers(view, 27744, 31584, 34144, 34656)
        begin1 = Begin(k)
        xn32 = view(31840, [DT_, S])
        n1 = Norm(k, k.x, xn32, "norm_mix", lambda eng, j: eng.wait_ge(k.x_loaded, 16))
        xs1 = SplitTiles(k, "first_input", xn32, view_r("first_input_hi", 4096, [DT_, S]),
                         view_r("first_input_lo", 27744, [DT_, S]), n1.wait_dst)
        pq = SplitProject(k, 8, xs1, [copy_out(k, qk[:, i, :], 0.125 if i < 4 else 1.0) for i in range(8)],
                          after=begin1)
        al = Alibi(k, alibi)
        pu = SplitProject(k, 4, xs1, [copy_out(k, u1[:, i, 16:16 + S]) for i in range(4)], wait=False, after=pq)
        pv = Project(k, 4, tiles(xn32), n1.wait_dst,
                     [copy_tokens(k, v1[:, :, i * P:(i + 1) * P], P) for i in range(4)], kind="tokens")
        pool = Pool(k, u1, sums, mixed, cat, pu.ts)
        heads = []
        for h in range(H1):
            lo, p = HD * (h % 2), h // 2
            ready = [lambda pe, p=p: k.wait_acc_drained(pe, pq.ts[p]),
                     lambda pe, p=p: k.wait_acc_drained(pe, pq.ts[4 + p]),
                     lambda pe, p=p: k.wait_acc_drained(pe, pv.ts[p])]
            if h == 0:
                ready.append(lambda pe: pe.wait_ge(al.ready, H1))
            heads.append(Head(qk[lo:lo + HD, p, :], qk[lo:lo + HD, 4 + p, :],
                              lambda j, h=h: v1[:, j, h * HD:(h + 1) * HD], alibi[:, h, :], lo, ready=ready))
        begin_out = Begin(k)
        at1 = Attention(k, "moba", heads, lambda u: cat[:, u // 2, :], buf1)

        def wait_cat(pe, c):
            k.wait_acc_drained(pe, at1.pair[2 * c] if c < 4 else pool.ts[c - 4])

        cats = SplitTiles(k, "mixed", cat, view_r("mixed_hi", 4096, [DT_, S]), view_r("mixed_lo", 18432, [DT_, S]),
                          wait_cat)
        po = SplitProject(k, 8, cats, [add_residual(k, k.x[:, i, :]) for i in range(8)], after=begin_out)
        xn32 = view(28672, [DT_, S])
        n2 = Norm(k, k.x, xn32, "norm_mlp", drained(po), source=po)
        xs = SplitTiles(k, "mlp_input", xn32, view_r("mlp_input_hi", 4096, [DT_, S]), view_r("mlp_input_lo", 24576, [DT_, S]), n2.wait_dst)
        hid = Hidden(k, [view_r(f"mlp_hi{i}", 8192 + 8192 * i, [8, S]) for i in range(2)],
                     [view_r(f"mlp_lo{i}", 12288 + 8192 * i, [8, S]) for i in range(2)], view(32768, [4, S]))
        hidden = [hid.group(g) for g in range(4)]
        up, down = [SplitProject(k, 8, xs, hidden[0].drains, after=po)], []
        for g in range(1, 5):
            last = down[-1] if down else up[-1]
            if g < 4:
                last = SplitProject(k, 8, xs, hidden[g].drains, wait=False, after=last)
                up.append(last)
            down.append(SplitProject(k, 8, hidden[g - 1], [add_residual(k, k.x[:, i, :]) for i in range(8)], after=last))
        pd = down[-1]
        n3 = Norm(k, k.x, k.x, "norm_final", drained(pd), source=pd)

        n4 = Norm(k, k.x, xn, "norm_mix_2", n3.wait_dst)
        save_x = Move(k, "x_saved", x_dram, k.x, [lambda e: n4.wait_dst(e, 7)])
        rr, kk, vv, aa, bb = (view(free + 4096 * i, [DT_, S]) for i in range(5))
        zwa, zg, end = view(28672, [S]), view(29184, [2, S]), view(30208, [DT_, NCH])
        tail = 30272
        shift = view(tail + 6000, [3, 1 + S])
        xs4 = SplitTiles(k, "mixer_input", xn, view_r("mixer_input_hi", 24576, [DT_, S]), view_r("mixer_input_lo", 20480, [DT_, S]), n4.wait_dst)
        inp = RwkvInputs(k, xs4, (rr, kk, vv), zwa, zg, shift, lambda e: n4.wait_dst(e, 7), after=pd)
        names = ("decay", "a", "kk", "sum", "before", "p", "inv", "mix", "rkk", "bonus")
        tmp = {n: view(2 * S * i if i < 4 else tail + 2 * S * (i - 4), [2, S]) for i, n in enumerate(names)}
        tmp["w0h"], tmp["a0h"] = view(tail + 12 * S, [8]), view(tail + 12 * S + 8, [8])
        prep = RwkvPrepare(k, inp, aa, bb, end, tmp, bonus_dram, save_x.wait_done)
        diagonals = ("b_bd", "k_bd", "x32", "x64", "d8", "mn", "bn", "kn")
        sbuf = {n: view(1024 * i if i < 4 else tail + 1024 * (i - 4), [DT_, P]) for i, n in enumerate(diagonals)}
        sbuf.update({n: view(tail + 4096 + S * i, [DT_, CH]) for i, n in enumerate(("d2t", "m0", "m1", "d", "dt", "d2"))})
        sbuf["z"] = view(28672, [DT_, CH])
        for i, n in enumerate(("rbt", "rkt", "d4", "vn")):
            sbuf[n] = k.square[:, i, :].rearrange("p (a b) -> p a b", b=CH)
        for n, place in (("wt", "x32"), ("an", "x64"), ("akt", "d8"), ("d4t", "mn"), ("sa", "d"), ("q", "dt"),
                         ("g", "d2t"), ("u", "d4")):
            sbuf[n] = sbuf[place]
        sbuf["d2t_m0"] = view(tail + 4096, [2, DT_, CH])
        ra = arena[:, 8192:8192 + 2 * 12288].rearrange("p (s n) -> p s n", s=2)
        scan = RwkvScan(k, prep, sbuf, ra)
        begin_gated = Begin(k)
        xs6 = SplitTiles(k, "gate_input", xn, view_r("gate_input_hi", 0, [DT_, S]),
                         view_r("gate_input_lo", 24576, [DT_, S]),
                         lambda e, j: scan.wait_end(e), alone=True)
        outp = RwkvOutput(k, scan, zg, inp.zg_ready, rr, vv, bonus_dram, prep.bonus_saved, aa, kk,
                          view(30272, [DT_, S]))
        merged = aa
        tanh = view(34944, [2, S])
        tab, hot_in = view(36100, [3, HQ], parts=BUCKETS + 1), view(36200, [1024], parts=BUCKETS + 1)
        table_rows = TableRows(k, rel, rel_last, bucket, tab, hot_in, hot, rows,
                               lambda e: k.wait_aux_drained(e, scan.t[NCH - 1]["z"]))
        ys = SplitTiles(k, "rwkv_y", rr, view_r("rwkv_y_hi", 12288, [DT_, S]), view_r("rwkv_y_lo", 30272, [DT_, S]),
                        outp.wait_out)
        br = Gated(k, ys, xs6, merged, tanh, first=True, after=begin_gated)

        wide = view(8192, [HQ, S])
        q2 = view(16384, [DT_, S])
        kd = [view(24576 + 2048 * i, [NKV, S]) for i in range(2)]
        vs = [view(28672 + 1024 * i, [NT, 256]) for i in range(2)]
        comp = view(30720, [HQ, NT * NCMP])
        gate = view(32704, [NT, 48])
        kraw = [view(32896 + 1024 * i, [2, S]) for i in range(2)]
        kc, vc = view(0, [2, S]), view(1024, [2, S])
        staged = (view(2048, [16, 124]), view(26624, [16, 124]))
        kv_swap = [view(24576 + 1024 * b, [2, S]) for b in range(2)]
        chid, keys_raw = view(34944, [2, 248]), view(35936, [124])
        craw, ctmp = view(32896, [2, 256], parts=124), view(33408, [2, 256], parts=124)
        keys, values = view(37504, [124]), view(37628, [NKV, HD], parts=NCMP)
        buf2 = Buffers(view, 0, 34944, 32896, 3840)

        tb = Tables(k, table_rows, wide, comp)
        gain_ready = k.sem("q_gain_ready")
        nq = SplitProjectNorm(k, 8, xs6, tiles(q2), tiles(q2), lambda i: gain8[:, 0:1], "head_mean", after=br,
                              tables=tb)
        def gate_tanh():
            def scalar(act, t):
                k.wait_acc_full(act, t)
                act.activation(gate, k.acc(t)[:, 0:NT * 48].rearrange("p (b m) -> p b m", m=48), ACT.Tanh,
                               scale=0.5).then_inc(k.acc_drained[t % NA], 1)
            return {"scalar": scalar}

        pg = Project(k, 1, tiles(xn), lambda pe, c: None, [gate_tanh()], kind="tokens", m=48)
        Gates(k, gate, lambda e: k.wait_acc_drained(e, pg.ts[0]))
        pkv = Project(k, 4, tiles(xn), lambda pe, c: None,
                      [copy_out(k, (kc, vc)[i // 2][:, i % 2, :]) for i in range(4)])
        cmp_ = Compress(k, (kc, vc), kv_swap, lambda e, b: k.wait_acc_drained(e, pkv.ts[2 * b + 1]), staged, craw,
                        ctmp, chid, keys_raw, keys, values)
        cmx = view(35936 + 124, [2, HQ * NT])
        cs = CompressedSoftmax(k, q2, keys, comp, gate, cmx, nq.wait_dst,
                               lambda pe: [cmp_.wait_done(pe)] + [k.wait_acc_drained(pe, t) for t in tb.ts])
        nk = [ProjectNorm(k, 2, tiles(xn), lambda pe, c: None, tiles(kraw[b]), tiles(kraw[b]),
                          lambda i, b=b: k.vec("k_gain", 1 + b), "head_mean") for b in range(2)]
        spread = Spread(k, kraw, kd, [nk[0].wait_dst, nk[1].wait_dst])
        pvs = [Project(k, 2, tiles(xn), lambda pe, c: None,
                       [copy_tokens(k, vs[b][:, :, i * P:(i + 1) * P], P) for i in range(2)], kind="tokens")
               for b in range(2)]
        heads = []
        for pair in range(DT_):
            g = pair // 2
            slot = (g % 2) * 2 + g // 2
            for e in range(2):
                h, lo = 2 * pair + e, HD * e
                hf = slice(lo, lo + HD)
                ready = []
                if h == 0:
                    ready = [lambda pe: nq.wait_dst(pe, 7), spread.wait_done, lambda pe: pe.wait_ge(cs.done, 1),
                             lambda pe: [k.wait_acc_drained(pe, t) for p_ in pvs for t in p_.ts]]
                for b in range(2):
                    gt = gate[:, :, 3 * h + 1 + b:3 * h + 2 + b].rearrange("p a b -> p (a b)")
                    heads.append(Head(q2[hf, pair, :], kd[b][hf, g, :],
                                      lambda j, b=b, g=g: vs[b][:, j, g * HD:(g + 1) * HD], wide[:, h, :], lo,
                                      gate=gt, compressed=(comp[:, h, :], values[:, slot, :]) if b == 0 else None,
                                      last=(b == 1), ready=ready if b == 0 else ()))
        begin_gated2 = Begin(k)
        at2 = Attention(k, "nsa", heads, lambda u: q2[:, u // 4, :], buf2)
        xs7 = SplitTiles(k, "gate2_input", xn, view_r("gate2_input_hi", 8192, [DT_, S]),
                         view_r("gate2_input_lo", 12288, [DT_, S]), lambda e, j: k.wait_acc_drained(e, at2.pair[-1]))
        ys2 = SplitTiles(k, "nsa_y", q2, view_r("nsa_y_hi", 24576, [DT_, S]), view_r("nsa_y_lo", 28672, [DT_, S]),
                         lambda e, j: k.wait_acc_drained(e, at2.pair[-1]))
        bn = Gated(k, ys2, xs7, merged, tanh, first=False,
                   wait_merged=lambda e: [k.wait_acc_drained(e, t) for t in br.bt], after=begin_gated2)
        ms = SplitTiles(k, "merged", merged, view_r("merged_hi", 16384, [DT_, S]), view_r("merged_lo", 4096, [DT_, S]),
                        lambda e, c: e.wait_ge(k.merged_ready, c + 1))
        load_x = Move(k, "x_back", k.x, x_dram, [save_x.wait_done, lambda e: k.wait_acc_drained(e, at2.pair[-1])])

        def add_half(i):
            def vector(dve, t):
                if i == 0:
                    load_x.wait_done(dve)
                k.wait_acc_full(dve, t)
                dve.scalar_tensor_tensor(k.x[:, i, :], k.acc(t), 0.5, k.x[:, i, :], ALU.mult, ALU.add).then_inc(
                    k.acc_drained[t % NA], 1)
            return {"vector": vector}

        pm = SplitProject(k, 8, ms, [add_half(i) for i in range(8)], after=bn)

        mem_t = view(32768, [DT_, N_MEM])
        load_mem = Move(k, "mem_loaded", mem_t, mem, [lambda e: k.wait_acc_drained(e, at2.pair[-1])])
        nm = Norm(k, mem_t, mem_t, "norm_mem", lambda e, j: load_mem.wait_done(e), n=N_MEM)
        q3, k3 = view(12288, [DT_, S]), view(16384, [DT_, N_MEM])
        v3, o3 = view(18432, [2, D]), view(24576, [DT_, S])
        pk = ProjectNorm(k, 8, tiles(mem_t), nm.wait_dst, tiles(k3), tiles(k3),
                         lambda i: k.vec("ca_k_gain", i % 2), "ones256", span=2, n=N_MEM)
        pv3 = Project(k, 8, tiles(mem_t), nm.wait_dst,
                      [copy_tokens(k, v3[:, :, i * P:(i + 1) * P], P, blocks=2) for i in range(8)], kind="tokens",
                      n=N_MEM)
        xn32 = view(8192, [DT_, S])
        begin_cross = Begin(k)
        nx = Norm(k, k.x, xn32, "norm_cross", drained(pm))
        xs8 = SplitTiles(k, "cross_input", xn32, view_r("cross_input_hi", 28672, [DT_, S]),
                         view_r("cross_input_lo", 20480, [DT_, S]), nx.wait_dst)
        pq3 = SplitProjectNorm(k, 8, xs8, tiles(q3), tiles(q3), lambda i: k.vec("ca_q_gain", i % 2), "ones256", span=2,
                               after=begin_cross)
        buf3 = CrossBuffers(view, 28672)
        ca = CrossAttention(k, q3, k3, v3, o3, buf3,
                            [lambda pe: pk.wait_dst(pe, 7), lambda pe: pq3.wait_dst(pe, 7),
                             lambda pe: [k.wait_acc_drained(pe, t) for t in pv3.ts]])
        os3 = SplitTiles(k, "cross_out", o3, view_r("cross_out_hi", 8192, [DT_, S]),
                         view_r("cross_out_lo", 4096, [DT_, S]), ca.wait_out)
        pco = SplitProject(k, 8, os3, [add_residual(k, k.x[:, i, :]) for i in range(8)], after=pq3)

        xn32 = view(30720, [DT_, S])
        nf = Norm(k, k.x, xn32, "norm_ffn", drained(pco), source=pco)
        xs5 = SplitTiles(k, "ffn_input", xn32, view_r("ffn_input_hi", 4096, [DT_, S]), view_r("ffn_input_lo", 8192, [DT_, S]), nf.wait_dst)
        ff = ConvFfn(k, xs5, view_r("ffn_hi", 12288, [FT2, S]), view_r("ffn_lo", 23552, [FT2, S]), view(34816, [2, 2 + S]),
                     k.square[:, 0:2], view(35844, [2, S]), k.square[:, 2:4], lambda e: nf.wait_dst(e, 7), after=pco)
        pf = SplitProject(k, 8, ff, [add_residual(k, k.x[:, i, :]) for i in range(8)], groups=(8, 8, 6), after=ff)
        Store(k, out, drained(pf))

        def scaled_gain(dve):
            dve.tensor_scalar(gain8[:, :], k.vec("q_gain"), 0.125, None, ALU.mult).then_inc(gain_ready, 1)
            dve.wait_ge(gain_ready, 1)

        stages = k.stages
        block = ctx.enter_context(nc.Block())

        @block.sync
        def _(sp):
            for s in stages:
                s.sync(sp)

        @block.tensor
        def _(pe):
            for s in stages:
                s.tensor(pe)

        @block.vector
        def _(dve):
            dve.wait_ge(k.vec_loaded, 16)
            scaled_gain(dve)
            for s in stages:
                s.vector(dve)

        @block.scalar
        def _(act):
            for s in stages:
                s.scalar(act)

        @block.gpsimd
        def _(pool_engine):
            for s in stages:
                s.gpsimd(pool_engine)
        return [u[1] for u in k.units]


def tiled(w, m=P):
    kt = w.shape[0] // P
    return [w[:, i:i + m].reshape(kt, P, -1).transpose(1, 0, 2).reshape(P, -1) for i in range(0, w.shape[1], m)]


def cut_units(tile, sizes):
    out, at = [], 0
    for n in sizes:
        out.append(tile[:, at * P:(at + n) * P])
        at += n
    return out


def stream(a):
    units = []
    w = a["w_in"][0]
    units += tiled(w[:, 0:1024]) + tiled(w[:, 1536:2048]) + tiled(w[:, 1024:1536])
    units.append(a["w_pool"][0].transpose(1, 0, 2).reshape(P, 4 * P))
    units += tiled(a["w_out"][0])
    up, down = tiled(a["w_up"][0]), [cut_units(t, (8, 8, 8, 8)) for t in tiled(a["w_down"][0])]
    units += up[0:8]
    for g in range(1, 5):
        units += up[8 * g:8 * g + 8] + [t[g - 1] for t in down]
    w2 = a["w_in_2"][0]
    units += tiled(w2[:, 0:RWKV_COLS])
    units.append(np.concatenate([a["rwkv_w2_2"][0], a["rwkv_a2_2"][0]], axis=0))
    g2 = a["rwkv_g2_2"][0]
    units += [g2[0:P], np.concatenate([g2[P:], np.zeros((P - 32, D), g2.dtype)], axis=0)]
    at = RWKV_COLS
    part = {}
    for name, n in (("q", 1024), ("kc", 256), ("vc", 256), ("ks", 256), ("vs", 256), ("kw", 256), ("vw", 256),
                    ("g", 48), ("m0", 1024), ("m1", 1024)):
        part[name] = w2[:, at:at + n]
        at += n
    for gw, bw in zip(tiled(part["m0"]), tiled(a["w_branch_rwkv_2"][0])):
        units += [gw, bw]
    units += tiled(part["q"]) + tiled(part["g"], 48) + tiled(part["kc"]) + tiled(part["vc"])
    for s in "kv":
        units += list(a[f"cmp_w1_{s}_2"][0].reshape(4, 4, P, 256).transpose(0, 2, 1, 3).reshape(4, P, 1024))
    ck = a["cmp_w2_k_2"][0].reshape(2, P, HD)
    ck = np.concatenate([ck, ck], axis=2).transpose(1, 0, 2).reshape(P, 256)
    cv = a["cmp_w2_v_2"][0].reshape(2, P, HD).transpose(1, 0, 2).reshape(P, 128)
    units.append(np.concatenate([ck, cv], axis=1))
    units += tiled(part["ks"]) + tiled(part["kw"]) + tiled(part["vs"]) + tiled(part["vw"])
    for gw, bw in zip(tiled(part["m1"]), tiled(a["w_branch_nsa_2"][0])):
        units += [gw, bw]
    units += tiled(a["w_mix_out_2"][0])
    wkv = a["ca_wkv_2"][0]
    units += tiled(wkv[:, 0:1024]) + tiled(wkv[:, 1024:2048]) + tiled(a["ca_wq_2"][0]) + tiled(a["ca_wo_2"][0])
    up = a["ffn_up_2"][0]
    for gw, bw in zip(tiled(up[:, 0:D_FF2]), tiled(up[:, D_FF2:])):
        units += [gw, bw]
    for t in tiled(a["ffn_down_2"][0]):
        units += cut_units(t, (8, 8, 6))
    return units


def vectors(a):
    def cols(v):
        v = np.asarray(v).reshape(-1)
        pad = (-len(v)) % P
        return np.concatenate([v, np.zeros(pad, v.dtype)]).reshape(-1, P).T

    def twice(v):
        return np.concatenate([v, v], axis=-1)

    parts = {
        "norm_mix": a["norm_mix"], "norm_mlp": a["norm_mlp"], "norm_final": a["norm_final"],
        "pool_scale": a["pool_scale"], "norm_mix_2": a["norm_mix_2"], "mu": a["rwkv_mu_2"], "w0": a["rwkv_w0_2"],
        "a0": a["rwkv_a0_2"], "k_k": a["rwkv_kk_2"], "k_a": a["rwkv_ka_2"], "r_k": a["rwkv_rk_2"],
        "lnx_w": a["rwkv_lnx_w_2"], "lnx_b": a["rwkv_lnx_b_2"], "norm_cross": a["norm_cross_2"],
        "norm_mem": a["norm_mem_2"], "norm_ffn": a["norm_ffn_2"], "conv": a["ffn_conv_2"], "conv_b": a["ffn_conv_b_2"],
        "ca_q_gain": a["ca_q_gain_2"], "ca_k_gain": a["ca_k_gain_2"], "q_gain": twice(a["nsa_q_gain_2"][0]),
        "k_gain": twice(a["nsa_k_gain_2"][0]), "pe_k": twice(a["cmp_pe_k_2"][0]), "pe_v": twice(a["cmp_pe_v_2"][0]),
    }
    return np.concatenate([cols(parts[n]) for n in VECS], axis=1)


def feature_tiles(x):
    return x.T.reshape(-1, P, x.shape[0]).transpose(1, 0, 2)


def kernel(**inputs):
    import concourse.bacc as bacc
    from concourse.bass_utils import run_bass_kernel_spmd

    a = {name: np.asarray(v) for name, v in inputs.items()}
    units = stream(a)
    w = np.zeros((len(units), P, UNIT), a["w_in"].dtype)
    for g, u in enumerate(units):
        w[g, :, 0:u.shape[1]] = u
    rel = a["rel_bias_2"]
    arrays = {
        "x_t": feature_tiles(a["x"][0]), "consts": constants(), "vectors": vectors(a), "weights": w,
        "one_hot": one_hot(),
        "rel_bias": rel, "rel_last": np.repeat(rel[BUCKETS - 1:], BUCKETS, axis=0), "mem_t": feature_tiles(a["mem_2"][0]),
    }
    arrays = {n: np.ascontiguousarray(v) for n, v in arrays.items()}
    nc = bacc.Bacc("TRN2", target_bir_lowering=False, num_devices=1)
    args = [nc.dram_tensor(n, v.shape, F32, kind="ExternalInput").ap() for n, v in arrays.items()]
    out = nc.dram_tensor("out_t", (P, DT_, S), F32, kind="ExternalOutput").ap()
    sizes = build(nc, *args, out)
    assert sizes == [u.shape[1] for u in units]
    r = run_bass_kernel_spmd(nc, [arrays], core_ids=[0])
    return r.results[0]["out_t"].transpose(1, 0, 2).reshape(D, S).T.reshape(1, S, D)
```
